# Optimizing a Trainium2 kernel written in Bass

```python
import math
import jax, jax.numpy as jnp
from jax import lax
import numpy as np

D_MODEL = 1024
BATCH = 1
SEQ = 256
DEPTH = 2

GRID_W = 64
CTX_LEN = 256
N_MIXERS = 2
N_MLSTM_LAYERS = (DEPTH + 1) // 2
N_RGLRU_LAYERS = DEPTH // 2
M_HEADS = 8
M_DQK = 64
M_DV = 128
M_CHUNK = 64
M_PROJ = 2 * M_HEADS * M_DQK + 2 * M_HEADS * M_DV + 4 * M_HEADS
R_WIDTH = D_MODEL
R_BLOCKS = 8
R_BW = R_WIDTH // R_BLOCKS
R_CONV = 4
R_C = 8.0
N_EXPERTS = 16
N_GROUPS = 4
EXPERTS_PER_GROUP = N_EXPERTS // N_GROUPS
TOP_K = 2
D_EXPERT = 512
EPS = 1e-6
POS_BASE = 10000.0

kernel_name = "hybrid_mlstm_rglru_moe_prefix_dit"

F32 = jnp.float32

def rmsnorm(x, g):
    x32 = x.astype(F32)
    y = x32 * lax.rsqrt(jnp.mean(x32 * x32, axis=-1, keepdims=True) + EPS) * g.astype(F32)
    return y.astype(x.dtype)

def modulate(x, g, shift, scale):
    return rmsnorm(x, g) * (1 + scale) + shift

def pos_embed_2d(n_tokens, dim, dtype):
    rows = n_tokens // GRID_W
    r, col = jnp.meshgrid(jnp.arange(rows, dtype=F32), jnp.arange(GRID_W, dtype=F32), indexing='ij')
    quarter = dim // 4
    freqs = jnp.exp(-math.log(POS_BASE) * jnp.arange(quarter, dtype=F32) / quarter)
    def enc(p):
        ang = p.reshape(-1, 1) * freqs
        return jnp.concatenate([jnp.sin(ang), jnp.cos(ang)], axis=-1)
    return jnp.concatenate([enc(r), enc(col)], axis=-1).astype(dtype)

def mlstm_chunkwise(q, k, v, ig, lf, state):
    bsz, nh, t, _ = q.shape
    nc = t // M_CHUNK
    def chunks(a):
        a = a.reshape(bsz, nh, nc, M_CHUNK, *a.shape[3:])
        return jnp.moveaxis(a, 2, 0)
    causal = jnp.tril(jnp.ones((M_CHUNK, M_CHUNK), dtype=bool))
    def step(carry, inp):
        C, n, m = carry
        qc, kc, vc, ic, fc = inp
        b = jnp.cumsum(fc, axis=-1)
        logd = jnp.where(causal, b[..., :, None] - b[..., None, :] + ic[..., None, :], -jnp.inf)
        log_inter = b + m[..., None]
        m_pos = jnp.maximum(log_inter, jnp.max(logd, axis=-1))
        w_intra = jnp.exp(logd - m_pos[..., None])
        w_inter = jnp.exp(log_inter - m_pos)
        s = jnp.einsum('bhjd,bhsd->bhjs', qc, kc) * w_intra
        num = jnp.einsum('bhjs,bhsv->bhjv', s, vc) + w_inter[..., None] * jnp.einsum('bhjd,bhdv->bhjv', qc, C)
        den = jnp.sum(s, axis=-1) + w_inter * jnp.einsum('bhjd,bhd->bhj', qc, n)
        h = num / jnp.maximum(jnp.abs(den), jnp.exp(-m_pos))[..., None]
        m_new = m_pos[..., -1]
        w_s = jnp.exp(b[..., -1:] - b + ic - m_new[..., None])
        decay = jnp.exp(b[..., -1] + m - m_new)
        C_new = decay[..., None, None] * C + jnp.einsum('bhs,bhsd,bhsv->bhdv', w_s, kc, vc)
        n_new = decay[..., None] * n + jnp.einsum('bhs,bhsd->bhd', w_s, kc)
        return (C_new, n_new, m_new), h
    state, h = lax.scan(step, state, (chunks(q), chunks(k), chunks(v), chunks(ig), chunks(lf)))
    h = jnp.moveaxis(h, 0, 2).reshape(bsz, nh, t, -1)
    return h, state

def mlstm_mixer(hl, hc, w_in, b_gate, g_head, w_out, ctx_out):
    split_at = [M_HEADS * M_DQK, 2 * M_HEADS * M_DQK, 2 * M_HEADS * M_DQK + M_HEADS * M_DV,
                2 * M_HEADS * M_DQK + 2 * M_HEADS * M_DV]
    def project(h):
        bsz, t, _ = h.shape
        p = jnp.einsum('btd,dp->btp', h, w_in).astype(F32)
        q, k, v, o, g = jnp.split(p, split_at, axis=-1)
        heads = lambda a: a.reshape(bsz, t, M_HEADS, -1).transpose(0, 2, 1, 3)
        g = g.reshape(bsz, t, 4, M_HEADS).transpose(2, 0, 3, 1) + b_gate.astype(F32)[:, None, :, None]
        return (heads(q) * (M_DQK ** -0.5), heads(k), heads(v), jax.nn.sigmoid(o),
                g[0], jax.nn.log_sigmoid(g[1]), g[2], jax.nn.log_sigmoid(g[3]))
    flip = lambda a: jnp.flip(a, axis=2)
    def bidir(q, k, v, i_f, lf_f, i_b, lf_b, st_f, st_b):
        h_f, st_f = mlstm_chunkwise(q, k, v, i_f, lf_f, st_f)
        h_b, st_b = mlstm_chunkwise(flip(q), flip(k), flip(v), flip(i_b), flip(lf_b), st_b)
        return h_f + flip(h_b), st_f, st_b
    def readout(h, o, dtype):
        bsz, _, t, _ = h.shape
        h = h * lax.rsqrt(jnp.mean(h * h, axis=-1, keepdims=True) + EPS)
        h = h.transpose(0, 2, 1, 3).reshape(bsz, t, M_HEADS * M_DV) * g_head.astype(F32) * o
        return jnp.einsum('bte,ed->btd', h.astype(dtype), w_out).astype(dtype)
    qc, kc, vc, oc, icf, lfcf, icb, lfcb = project(hc)
    bsz = hc.shape[0]
    zero = (jnp.zeros((bsz, M_HEADS, M_DQK, M_DV), F32), jnp.zeros((bsz, M_HEADS, M_DQK), F32),
            jnp.zeros((bsz, M_HEADS), F32))
    hc_sum, st_f, st_b = bidir(qc, kc, vc, icf, lfcf, icb, lfcb, zero, zero)
    ql, kl, vl, ol, ilf, lflf, ilb, lflb = project(hl)
    hl_sum, _, _ = bidir(ql, kl, vl, ilf, lflf, ilb, lflb, st_f, st_b)
    out_l = readout(hl_sum, ol, hl.dtype)
    out_c = readout(hc_sum, oc, hc.dtype) if ctx_out else None
    return out_l, out_c

def centred_dwconv(x, w, b):
    t = x.shape[1]
    left = R_CONV // 2
    xp = jnp.pad(x, ((0, 0), (left, R_CONV - 1 - left), (0, 0)))
    y = b + xp[:, 0:t] * w[0]
    for j in range(1, R_CONV):
        y = y + xp[:, j:j + t] * w[j]
    return y

def _lru_combine(left, right):
    a1, b1 = left
    a2, b2 = right
    return a1 * a2, a2 * b1 + b2

def lru_scan(a, bx, h0, reverse):
    edge = -1 if reverse else 0
    bx = bx.at[:, edge].add(a[:, edge] * h0)
    _, h = lax.associative_scan(_lru_combine, (a, bx), reverse=reverse, axis=1)
    return h

def rglru_mixer(hl, hc, w_in, conv_w, conv_b, w_gate, b_gate, lam, w_out, ctx_out):
    def branches(h):
        p = jnp.einsum('btd,de->bte', h, w_in)
        y, xr = jnp.split(p, 2, axis=-1)
        return y, centred_dwconv(xr, conv_w, conv_b).astype(F32)
    def gates(xr, d):
        bsz, t, _ = xr.shape
        xb = xr.reshape(bsz, t, R_BLOCKS, R_BW)
        g = jnp.einsum('btnd,nde->btne', xb, w_gate[d].astype(F32)) + b_gate[d].astype(F32)
        r = jax.nn.sigmoid(g[..., :R_BW]).reshape(bsz, t, R_WIDTH)
        i = jax.nn.sigmoid(g[..., R_BW:]).reshape(bsz, t, R_WIDTH)
        log_a = -R_C * r * jax.nn.softplus(-lam[d].astype(F32))
        a = jnp.exp(log_a)
        return a, jnp.sqrt(-jnp.expm1(2.0 * log_a)) * (i * xr)
    def readout(y, h, dtype):
        return jnp.einsum('bte,ed->btd', (jax.nn.gelu(y.astype(F32)) * h).astype(dtype), w_out).astype(dtype)
    yc, xcr = branches(hc)
    yl, xlr = branches(hl)
    h0 = jnp.zeros((hc.shape[0], R_WIDTH), F32)
    a, bx = gates(xcr, 0)
    hc_f = lru_scan(a, bx, h0, False)
    a, bx = gates(xcr, 1)
    hc_b = lru_scan(a, bx, h0, True)
    a, bx = gates(xlr, 0)
    hl_f = lru_scan(a, bx, hc_f[:, -1], False)
    a, bx = gates(xlr, 1)
    hl_b = lru_scan(a, bx, hc_b[:, 0], True)
    out_l = readout(yl, hl_f + hl_b, hl.dtype)
    out_c = readout(yc, hc_f + hc_b, hc.dtype) if ctx_out else None
    return out_l, out_c

def moe(h, w_router, b_router, w1, w3, w2):
    logits = jnp.einsum('bnd,de->bne', h.astype(F32), w_router.astype(F32))
    scores = jax.nn.softmax(logits, axis=-1)
    sel = scores + b_router.astype(F32)
    bsz, n, _ = sel.shape
    grp = sel.reshape(bsz, n, N_GROUPS, EXPERTS_PER_GROUP)
    grp_score = jnp.sum(lax.top_k(grp, TOP_K)[0], axis=-1)
    g_idx = jnp.argmax(grp_score, axis=-1)
    in_grp = (jnp.arange(N_EXPERTS) // EXPERTS_PER_GROUP) == g_idx[..., None]
    _, top_idx = lax.top_k(jnp.where(in_grp, sel, -jnp.inf), TOP_K)
    top_w = jnp.take_along_axis(scores, top_idx, axis=-1)
    top_w = top_w / jnp.sum(top_w, axis=-1, keepdims=True)
    gate = jnp.einsum('bnk,bnke->bne', top_w, jax.nn.one_hot(top_idx, N_EXPERTS, dtype=F32))
    y = jnp.zeros(h.shape, F32)
    for e in range(N_EXPERTS):
        u = jax.nn.silu(h @ w1[e]) * (h @ w3[e])
        y = y + gate[..., e:e + 1] * (u @ w2[e]).astype(F32)
    return y.astype(h.dtype)

def setup_inputs(seed: int = 0) -> dict:
    key = jax.random.key(seed)
    ks = jax.random.split(key, 25)
    nrm = lambda k, shape, scale: jax.random.normal(k, shape, F32) * scale
    D = D_MODEL
    f_base = 3.0 + 3.0 * jnp.linspace(0.0, 1.0, M_HEADS)
    zh = jnp.zeros((M_HEADS,), F32)
    gate_base = jnp.stack([zh, f_base, zh, f_base])
    u = jax.random.uniform(ks[18], (N_RGLRU_LAYERS, 2, R_WIDTH), F32, minval=0.9, maxval=0.999)
    return {
        "x": nrm(ks[0], (BATCH, SEQ, D), 1.0),
        "c": nrm(ks[1], (BATCH, D), 1.0),
        "ctx": nrm(ks[2], (BATCH, CTX_LEN, D), 1.0),
        "c_ctx": nrm(ks[3], (D,), 1.0),
        "w_ada": nrm(ks[4], (DEPTH, D, 6 * D), 0.5 * D ** -0.5),
        "b_ada": nrm(ks[5], (DEPTH, 6 * D), 0.02),
        "g_mix": 1.0 + nrm(ks[6], (DEPTH, D), 0.02),
        "g_ffn": 1.0 + nrm(ks[7], (DEPTH, D), 0.02),
        "g_final": 1.0 + nrm(ks[8], (D,), 0.02),
        "m_w_in": nrm(ks[9], (N_MLSTM_LAYERS, D, M_PROJ), D ** -0.5),
        "m_b_gate": gate_base[None] + nrm(ks[10], (N_MLSTM_LAYERS, 4, M_HEADS), 0.1),
        "m_g_head": 1.0 + nrm(ks[11], (N_MLSTM_LAYERS, M_HEADS * M_DV), 0.02),
        "m_w_out": nrm(ks[12], (N_MLSTM_LAYERS, M_HEADS * M_DV, D), (M_HEADS * M_DV) ** -0.5),
        "r_w_in": nrm(ks[13], (N_RGLRU_LAYERS, D, 2 * R_WIDTH), D ** -0.5),
        "r_conv_w": nrm(ks[14], (N_RGLRU_LAYERS, R_CONV, R_WIDTH), R_CONV ** -0.5),
        "r_conv_b": nrm(ks[15], (N_RGLRU_LAYERS, R_WIDTH), 0.02),
        "r_w_gate": nrm(ks[16], (N_RGLRU_LAYERS, 2, R_BLOCKS, R_BW, 2 * R_BW), R_BW ** -0.5),
        "r_b_gate": nrm(ks[17], (N_RGLRU_LAYERS, 2, R_BLOCKS, 2 * R_BW), 0.02),
        "r_lam": jnp.log(u) - jnp.log1p(-u),
        "r_w_out": nrm(ks[19], (N_RGLRU_LAYERS, R_WIDTH, D), R_WIDTH ** -0.5),
        "w_router": nrm(ks[20], (D, N_EXPERTS), D ** -0.5),
        "b_router": nrm(ks[21], (N_EXPERTS,), 0.01),
        "e_w1": nrm(ks[22], (DEPTH, N_EXPERTS, D, D_EXPERT), D ** -0.5),
        "e_w3": nrm(ks[23], (DEPTH, N_EXPERTS, D, D_EXPERT), D ** -0.5),
        "e_w2": nrm(ks[24], (DEPTH, N_EXPERTS, D_EXPERT, D), D_EXPERT ** -0.5),
    }

def reference(x, c, ctx, c_ctx, w_ada, b_ada, g_mix, g_ffn, g_final,
              m_w_in, m_b_gate, m_g_head, m_w_out,
              r_w_in, r_conv_w, r_conv_b, r_w_gate, r_b_gate, r_lam, r_w_out,
              w_router, b_router, e_w1, e_w3, e_w2):
    xl = x + pos_embed_2d(x.shape[1], x.shape[2], x.dtype)[None]
    xc = ctx
    silu_l = jax.nn.silu(c)[:, None, :]
    silu_c = jax.nn.silu(c_ctx)[None, None, :]
    for i in range(DEPTH):
        last = i == DEPTH - 1
        mod_l = jnp.split(silu_l @ w_ada[i] + b_ada[i], 6, axis=-1)
        mod_c = jnp.split(silu_c @ w_ada[i] + b_ada[i], 6, axis=-1)
        hl = modulate(xl, g_mix[i], mod_l[0], mod_l[1])
        hc = modulate(xc, g_mix[i], mod_c[0], mod_c[1])
        j = i // N_MIXERS
        if i % N_MIXERS == 0:
            ol, oc = mlstm_mixer(hl, hc, m_w_in[j], m_b_gate[j], m_g_head[j], m_w_out[j], not last)
        else:
            ol, oc = rglru_mixer(hl, hc, r_w_in[j], r_conv_w[j], r_conv_b[j], r_w_gate[j],
                                 r_b_gate[j], r_lam[j], r_w_out[j], not last)
        xl = xl + mod_l[2] * ol
        hl = modulate(xl, g_ffn[i], mod_l[3], mod_l[4])
        xl = xl + mod_l[5] * moe(hl, w_router, b_router, e_w1[i], e_w3[i], e_w2[i])
        if not last:
            xc = xc + mod_c[2] * oc
            hc = modulate(xc, g_ffn[i], mod_c[3], mod_c[4])
            xc = xc + mod_c[5] * moe(hc, w_router, b_router, e_w1[i], e_w3[i], e_w2[i])
    return rmsnorm(xl, g_final)


_drawn_inputs = setup_inputs


def setup_inputs(seed=0):
    import zlib

    import numpy as np

    out = dict(_drawn_inputs(seed))
    spreads = {}
    factors = {'g_final': 9.086,
     'm_g_head': 19.757,
     'r_conv_b': 2.669,
     'r_b_gate': 17.093,
     'g_ffn': 3.455}
    for name, (base, spread) in spreads.items():
        noise = np.random.default_rng([zlib.crc32(name.encode()), seed]).standard_normal(out[name].shape)
        drawn = base * np.exp(spread * noise) if base else spread * noise
        out[name] = __import__('jax').numpy.asarray(drawn.astype(out[name].dtype))
    for name, factor in factors.items():
        out[name] = (out[name] * factor).astype(out[name].dtype)
    return out
```

```python
from contextlib import ExitStack

import numpy as np

import concourse.bass as bass
from concourse import mybir

F32 = mybir.dt.float32
U32 = mybir.dt.uint32
I32 = mybir.dt.int32
ALU = mybir.AluOpType
ACT = mybir.ActivationFunctionType
AX_X = mybir.AxisListType.X

P = 128
D = 1024
KD = D // P
SEQ = 256
TILES = 4
T_ALL = TILES * P
HEADS = 8
DQK = 64
DV = 128
DVX = DV + 1
NE = 16
DE = 512
EPS = 1e-6
NEG = -1e30
RGLRU_C = 8.0
SLOTS = 6
CHUNK = 4096
PASS = 64
CAP = 512
PAD = 1.0e6

ADA_CHUNKS = 12
N_ADA0 = 0
N_MIX0 = N_ADA0 + ADA_CHUNKS
N_OUT0 = N_MIX0 + 6
N_MOE0 = N_OUT0 + 2
N_ADA1 = N_MOE0 + 3 * NE
N_MIX1 = N_ADA1 + ADA_CHUNKS
N_OUT1 = N_MIX1 + 5
N_MOE1 = N_OUT1 + 2
N_CHUNKS = N_MOE1 + 3 * NE


def fwd_keys(j):
    return list(range(j + 1))


def bwd_keys(j):
    return [[0, 1], [1], [0, 1, 2, 3], [0, 1, 3]][j]


PAIRS = [[(s, j) for s in range(TILES) for j in range(TILES) if s in keys(j)] for keys in (fwd_keys, bwd_keys)]


def runs_of(pairs, s):
    js = [j for (a, j) in pairs if a == s]
    out = []
    for j in js:
        if out and out[-1][0] + out[-1][1] == j:
            out[-1][1] += 1
        else:
            out.append([j, 1])
    return [tuple(r) for r in out]


def build(nc, a, out):
    ctx = ExitStack()
    with ctx:
        def sb(name, shape, dt=F32):
            return ctx.enter_context(nc.sbuf_tensor(name, shape, dt))

        def sem(name):
            return ctx.enter_context(nc.semaphore(name))

        ctx.enter_context(nc.allow_non_contiguous_dma("columns of small vectors"))

        ps = ctx.enter_context(nc.psum_tensor("ps", [P, 8, 512], F32))
        ring = sb("ring", [P, SLOTS, CHUNK])
        X = sb("X", [P, TILES, D])
        hT = sb("hT", [P, KD, T_ALL])
        XN = sb("XN", [P, TILES, D])
        QK = sb("QK", [P, 8, T_ALL])
        VR = sb("VR", [P, TILES * HEADS * DVX])
        WR = sb("WR", [P, 2 * 16 * P])
        modr = sb("modr", [P, 3, 512])
        ident = sb("ident", [P, P])
        masks = sb("masks", [P, 2, P])
        triu = sb("triu", [P, P])
        ones = sb("ones", [P, P])
        wrt = sb("wrt", [P, KD, NE])
        gcol = sb("gcol", [P, TILES, P])
        rrow = sb("rrow", [64, T_ALL])
        silu_c = sb("silu_c", [P, KD, 2, 16])
        cvec = sb("cvec", [P, 2, KD])
        acol = sb("acol", [P, 2, KD])
        bcol = sb("bcol", [P, 2, KD])
        gmix = sb("gmix", [P, 2, KD])
        ghead = sb("ghead", [P, KD])
        bgate = sb("bgate", [P, 1])
        brt = sb("brt", [P, NE])
        iota16i = sb("iota16i", [P, NE], I32)
        iota16 = sb("iota16", [P, NE])
        toki = sb("toki", [P, TILES], I32)
        tokf = sb("tokf", [P, TILES])
        half = sb("half", [P, 1])
        mhalf = sb("mhalf", [P, HEADS])
        stat = sb("stat", [P, 8, TILES])
        att = sb("att", [P, 2, TILES])

        V = VR[:, :].rearrange("p (t h c) -> p t h c", t=TILES, h=HEADS)
        bada = VR[:, 0:1536].rearrange("p (g n) -> p g n", g=3)
        wg = VR[:, 1536:2560].rearrange("p (k t d r) -> p k t d r", k=KD, t=2, d=2)
        H = XN[:, :, :].rearrange("p t (h v) -> p t h v", h=HEADS)
        qT, kT = QK[:, 0:4, :], QK[:, 4:8, :]
        O = QK[:, :, :].rearrange("p a b -> p (a b)").rearrange("p (t n) -> p t n", t=TILES)
        W = WR[:, :].rearrange("p (u s j n) -> p u s j n", u=2, s=TILES, j=TILES)
        gtmp = WR[:, 0:3072].rearrange("p (a n) -> p a n", a=6)
        gate2 = WR[:, 0:2048].rearrange("p (s n) -> p s n", s=2)
        gtmp2 = WR[:, 2048:2560]
        sq = WR[:, 2560:3584].rearrange("p (h v) -> p h v", h=HEADS)
        hs = WR[:, 3584:3616].rearrange("p (t h) -> p t h", t=TILES)
        hss_ready, hr_ready = sem("head_squares"), sem("head_roots")

        ld = [sem(f"chunk_loaded{i}") for i in range(SLOTS)]
        x_in, cv_in, pos_in = sem("x_in"), sem("cv_in"), sem("pos_in")
        bada_in, small_in = sem("bada_in"), sem("small_in")
        wg_zero, wg_in = sem("wg_zero"), sem("wg_in")
        bg_zero = sem("bg_zero")
        consts, pool_step = sem("consts"), sem("pool_step")
        dve_step, act_step = sem("dve_step"), sem("act_step")
        silu_ready, ada_done, modr_ready = sem("silu_ready"), sem("ada_done"), sem("modr_ready")
        ada_part = sem("ada_part")
        modcol_done, cols_ready = sem("modcol_done"), sem("cols_ready")
        x_ready, ss_ready, rstd_ready, xn_ready = sem("x_ready"), sem("ss_ready"), sem("rstd_ready"), sem("xn_ready")
        nt_done, nt_act, nt_dve = sem("norm_turned"), sem("norm_kept_act"), sem("norm_kept_dve")
        gate_done, proj_done, proj_kept = sem("gate_done"), sem("proj_done"), sem("proj_kept")
        gates_ready, gturn_done, gcol_ready = sem("gates_ready"), sem("gturn_done"), sem("gcol_ready")
        v_ones, lsig_ready, lsig_kept, em_ready = sem("v_ones"), sem("lsig_ready"), sem("lsig_kept"), sem("em_ready")
        s_done, r_done, d_done, e_done, p_done, o_done = (
            sem("att_scores"), sem("att_rows"), sem("att_diag"), sem("att_exp"), sem("att_prod"), sem("att_out"))
        den_ready, fin_act, fin_dve = sem("att_den"), sem("att_kept_act"), sem("att_kept_dve")
        oproj_done, og_ready = sem("oproj_done"), sem("ogate_ready")
        g2_done, g2_ready = sem("gate2_done"), sem("gate2_ready")
        y_ready, yt_done, yt_kept = sem("mix_ready"), sem("mix_turned"), sem("mix_kept")
        out_done, out_added = sem("out_done"), sem("out_added")
        stored = sem("stored")

        table_ready, pool_held, sp_held, rg_in = sem("table_ready"), sem("pool_held"), sem("sp_held"), sem("rg_in")

        ab = QK[:, :, :].rearrange("p a b -> p (a b)").rearrange("p (v s n) -> p v s n", v=2, s=2)
        g5 = QK[:, 0:4, :].rearrange("p a b -> p (a b)").rearrange("p (s n) -> p s n", s=2)
        gffn = WR[:, 0:D]
        XG = VR[:, 0:1024].rearrange("p (a n) -> p a n", a=2)
        XT = VR[:, 1024:2048].rearrange("p (a j n) -> p a j n", a=2, j=4)
        YS = VR[:, 2048:3072].rearrange("p (a n) -> p a n", a=2)
        SG = VR[:, 3072:3584].rearrange("p (a n) -> p a n", a=2)
        U = VR[:, 3584:4096].rearrange("p (a n) -> p a n", a=2)
        UT = WR[:, 1024:1536].rearrange("p (a c n) -> p a c n", a=2, c=2)
        sm = WR[:, 1536:4096].rearrange("p (a n) -> p a n", n=64)
        GIX = sm[:, 36, 0:32].bitcast(U32)
        SIX = sm[:, 36, 32:64].bitcast(U32)
        gi = sm[:, 37, 0:2].bitcast(U32)
        si = sm[:, 37, 2:4].bitcast(U32)
        LST = sm[:, 38:40, :].rearrange("p a n -> p (a n)")
        pad = WR[:, 3616:3680]
        more = sb("more", [1, 32], I32)
        orow = sm[0:1, 33:35, :].rearrange("p a n -> p (a n)")
        ov = sm[:, 35, 0:8]
        ogi, osi = sm[:, 35, 8:9].bitcast(U32), sm[:, 35, 9:10].bitcast(U32)

        block = ctx.enter_context(nc.Block())

        XC = XN[:, :, :].rearrange("p a b -> p (a b)").rearrange("p (n t) -> p n t", n=8)
        YB = QK[:, 0:4, :].rearrange("p a b -> p (a b)").rearrange("p (n t) -> p n t", n=8)
        YT = QK[:, 4:8, :].rearrange("p a b -> p (a b)").rearrange("p (n t) -> p n t", n=8)
        RB = VR[:, 0:4096].rearrange("p (d a n) -> p d a n", d=2, a=4)
        xpad = WR[:, 2560:3600].rearrange("p (u s n) -> p u s n", u=2, s=2)
        hfb = WR[:, 0:1024].rearrange("p (d n) -> p d n", d=2)
        convw, convb = sb("convw", [P, 4, KD]), sb("convb", [P, KD])
        rbias, lam = sb("rbias", [P, 2, KD, 2]), sb("lam", [P, 2, KD])
        spl, spn, lt = sb("spl", [P, 2, KD]), sb("spn", [P, 2, KD]), sb("lt", [P, 4, 2 * KD])
        xr_done, yb_done, rg_done = sem("xr_done"), sem("yb_done"), sem("rg_done")
        xr_kept, yb_kept, conv_done, pads = sem("xr_kept"), sem("yb_kept"), sem("conv_done"), sem("pads")
        lam_exp, lam_u, lam_ln, lam_ready = sem("lam_exp"), sem("lam_u"), sem("lam_ln"), sem("lam_ready")
        rg_tanh, rg_q, rg_sqrt, rg_scan = sem("rg_tanh"), sem("rg_q"), sem("rg_sqrt"), sem("rg_scan")
        gfin_in, fin_ready = sem("gfin_in"), sem("fin_ready")
        RG_ORDER = ([("x", n) for n in range(4)] + [("y", n) for n in range(4)]
                    + [(w, n) for n in range(4) for w, n in (("x", n + 4), ("g", n))]
                    + [(w, n) for n in range(4, 8) for w in ("y", "g")])

        MOE_SIGNALS = dict(
            gffn_in=lambda m: 16, rows_done=lambda m: 2 * m.nt, scale_kept=lambda m: m.nt, shift_kept=lambda m: m.nt,
            h_ready=lambda m: m.nt, rows_stored=lambda m: 16 * m.nt, turned=lambda m: 2 * m.nt,
            turn_kept_act=lambda m: m.nt, turn_kept_dve=lambda m: m.nt, logits_done=lambda m: 1,
            shifted=lambda m: 1, expd=lambda m: 1, picked=lambda m: 1, pos_done=lambda m: 1, addr_ready=lambda m: 1,
            filled=lambda m: 32 * m.nt, list_in=lambda m: 32 * m.subs, list_turned=lambda m: 1,
            lists_ready=lambda m: 1, gi_ready=lambda m: m.G, si_ready=lambda m: m.G, tx_done=lambda m: m.G,
            xt_ready=lambda m: m.G, half_done=lambda m: NE, h_done=lambda m: m.G, silu_done=lambda m: m.G,
            u_ready=lambda m: m.G, tu_done=lambda m: m.G, ut_ready=lambda m: m.G, y_done=lambda m: m.G,
            ys_ready=lambda m: m.G, g5_done=lambda m: m.nt, g5_kept=lambda m: m.nt, y_in=lambda m: 32 * m.nt,
            y_scaled=lambda m: m.nt, added=lambda m: m.nt, more_ready=lambda m: 1, passes_over=lambda m: 1, gathered=lambda m: 8 * m.G, scattered=lambda m: 8 * m.G)
        moe_sems = {name: [sem(f"{name}{i}") for i in range(2)] if name in ("gathered", "scattered") else sem(name)
                    for name in MOE_SIGNALS}

        class Moe:
            def __init__(self, l, tiles, subs, base):
                self.l, self.tiles, self.subs, self.base = l, tiles, subs, base
                self.nt = len(tiles)
                self.T = P * self.nt
                self.G = NE * subs
                self.hrows = nc.dram_tensor(f"hrows{l}", [self.T, D], F32, kind="Internal").ap()
                self.yrows = nc.dram_tensor(f"yrows{l}", [2 * self.T, D], F32, kind="Internal").ap()
                self.table = nc.dram_tensor(f"table{l}", [NE * CAP, 1], F32, kind="Internal").ap()
                self.hhalf = self.hrows.rearrange("t (h n) -> (t h) n", h=2)
                self.yhalf = self.yrows.rearrange("t (h n) -> (t h) n", h=2)
                self.was = {name: (per(moes[0]) if l else 0) for name, per in MOE_SIGNALS.items()}
                self.gffn_in = moe_sems["gffn_in"]
                self.rows_done = moe_sems["rows_done"]
                self.scale_kept = moe_sems["scale_kept"]
                self.shift_kept = moe_sems["shift_kept"]
                self.h_ready = moe_sems["h_ready"]
                self.rows_stored = moe_sems["rows_stored"]
                self.turned = moe_sems["turned"]
                self.turn_kept_act = moe_sems["turn_kept_act"]
                self.turn_kept_dve = moe_sems["turn_kept_dve"]
                self.logits_done = moe_sems["logits_done"]
                self.shifted = moe_sems["shifted"]
                self.expd = moe_sems["expd"]
                self.picked = moe_sems["picked"]
                self.pos_done = moe_sems["pos_done"]
                self.addr_ready = moe_sems["addr_ready"]
                self.filled = moe_sems["filled"]
                self.list_in = moe_sems["list_in"]
                self.list_turned = moe_sems["list_turned"]
                self.lists_ready = moe_sems["lists_ready"]
                self.gi_ready = moe_sems["gi_ready"]
                self.si_ready = moe_sems["si_ready"]
                self.tx_done = moe_sems["tx_done"]
                self.xt_ready = moe_sems["xt_ready"]
                self.half_done = moe_sems["half_done"]
                self.h_done = moe_sems["h_done"]
                self.silu_done = moe_sems["silu_done"]
                self.u_ready = moe_sems["u_ready"]
                self.tu_done = moe_sems["tu_done"]
                self.ut_ready = moe_sems["ut_ready"]
                self.y_done = moe_sems["y_done"]
                self.ys_ready = moe_sems["ys_ready"]
                self.g5_done = moe_sems["g5_done"]
                self.g5_kept = moe_sems["g5_kept"]
                self.y_in = moe_sems["y_in"]
                self.y_scaled = moe_sems["y_scaled"]
                self.added = moe_sems["added"]
                self.more_ready = moe_sems["more_ready"]
                self.passes_over = moe_sems["passes_over"]
                self.gathered = moe_sems["gathered"]
                self.scattered = moe_sems["scattered"]

                (self.further_pe, self.further_act, self.further_dve, self.further_dma, self.further_loaded) = (
                    [sem(f"{name}{l}") for name in FURTHER_SIGNALS])
                self.further = self.T // PASS - subs
                self.most = max(min(n * self.further, (2 * self.T - n * (PASS * subs - PASS + 1)) // PASS)
                                for n in range(1, NE + 1))
                self.addr = sm[:, 30, 0:2 * self.nt].bitcast(U32)
                self.value = sm[:, 31, 0:2 * self.nt]
                self.weight = sm[:, 32, 0:2 * self.nt]

        FURTHER_SIGNALS = ("further_pe", "further_act", "further_dve", "further_dma", "further_loaded")
        PE_STEPS = ("column", "turned", "up", "u_turned", "down")
        ACT_STEPS = ("silu", "y_kept")
        DVE_STEPS = ("v", "second", "token", "row", "gather_index", "scatter_index", "xt", "u", "ut")

        def after(steps, o, name):
            return len(steps) * o + steps.index(name) + 1

        moes = []
        moes.append(Moe(0, [0, 1, 2, 3], 2, N_MOE0))
        moes.append(Moe(1, [2, 3], 1, N_MOE1))
        def slot(n):
            return ring[:, n % SLOTS, :]

        def cols_of(w, n, cb):
            v = w.rearrange("(k p) n -> p k n", p=P)
            d = slot(n).rearrange("p (k n) -> p k n", k=KD)
            return [(d[:, 4 * h:4 * h + 4, :], v[:, 4 * h:4 * h + 4, 512 * cb:512 * cb + 512]) for h in range(2)]

        def ada_of(l, n, j):
            g, kk = j // 4, j % 4
            v = a["w_ada"][l].rearrange("(k p) n -> p k n", p=P)
            d = slot(n).rearrange("p (k n) -> p k n", k=2)
            return [(d[:, h, :], v[:, 2 * kk + h, 2048 * g:2048 * g + 2048]) for h in range(2)]

        def expert_of(l, e, n, part):
            if part < 2:
                d = slot(n).rearrange("p (k w n) -> p k w n", k=4, w=2)
                return [(d[:, :, w, :], a[name][l, e].rearrange("(k p) n -> p k n", p=P)[:, 4 * part:4 * part + 4, :])
                        for w, name in enumerate(("e_w1", "e_w3"))]
            d = slot(n).rearrange("p (c n) -> p c n", c=4)
            v = a["e_w2"][l, e].rearrange("(c p) n -> p c n", p=P)
            return [(d[:, 2 * h:2 * h + 2, :], v[:, 2 * h:2 * h + 2, :]) for h in range(2)]

        m_in, r_in = a["m_w_in"][0], a["r_w_in"][0]
        r_gate = a["r_w_gate"][0].rearrange("d n p e -> p d n e")

        def used(n):
            for l, base in enumerate((N_ADA0, N_ADA1)):
                j = n - base
                if 0 <= j < ADA_CHUNKS:
                    g, kk = j // 4, j % 4
                    return (ada_done, 3 * l + g + 1) if kk == 3 else (ada_part, 9 * l + 3 * g + kk + 1)
            if N_MIX0 <= n < N_OUT0:
                j = n - N_MIX0
                return (proj_done, 4 * j + 4) if j < 4 else (oproj_done, 4 * (j - 4) + 4)
            if N_OUT0 <= n < N_MOE0:
                return out_done, TILES * (n - N_OUT0 + 1)
            if N_MIX1 <= n < N_OUT1:
                return [(xr_done, 4), (yb_done, 4), (rg_done, 16), (xr_done, 8), (yb_done, 8)][n - N_MIX1]
            if N_OUT1 <= n < N_MOE1:
                return out_done, 2 * TILES + 2 * (n - N_OUT1 + 1)
            for m in moes:
                if m.base <= n < m.base + 3 * NE:
                    e, part = (n - m.base) // 3, (n - m.base) % 3
                    return [(m.half_done, m.was["half_done"] + e + 1), (m.h_done, m.was["h_done"] + m.subs * (e + 1)),
                            (m.y_done, m.was["y_done"] + m.subs * (e + 1))][part]
            raise ValueError(n)

        @block.sync
        def _(sp):
            def load(n, parts):
                if n >= SLOTS:
                    sp.wait_ge(*used(n - SLOTS))
                for dst, src in parts:
                    sp.dma_start(dst, src).then_inc(ld[n % SLOTS], 16)

            for j in range(ADA_CHUNKS):
                load(N_ADA0 + j, ada_of(0, N_ADA0 + j, j))
            for j, cb in enumerate((0, 1, 2, 3, 4, 5)):
                load(N_MIX0 + j, cols_of(m_in, N_MIX0 + j, cb))
            for cb in range(2):
                load(N_OUT0 + cb, cols_of(a["m_w_out"][0], N_OUT0 + cb, cb))
            def experts(m):
                for n in range(m.base, m.base + 6):
                    e, part = (n - m.base) // 3, (n - m.base) % 3
                    load(n, expert_of(m.l, e, n, part))
                with sp.Fori(1, NE // 2) as i:
                    for j in range(6):
                        b, part = j // 3, j % 3
                        k = 2 * (i - 1) + b + 1
                        if part == 0:
                            sp.wait_ge(m.half_done, m.was["half_done"] + k)
                        elif part == 1:
                            sp.wait_ge(m.h_done, m.was["h_done"] + m.subs * k)
                        else:
                            sp.wait_ge(m.y_done, m.was["y_done"] + m.subs * k)
                        for dst, src in expert_of(m.l, 2 * i + b, m.base + j, part):
                            sp.dma_start(dst, src).then_inc(ld[(m.base + j) % SLOTS], 16)

            def experts_again(m):
                sp.wait_ge(m.more_ready, m.was["more_ready"] + 1)
                count = sp.value_load(more[0:1, 0:1], min_val=0, max_val=m.most)
                with sp.Fori(0, m.most) as o:
                    with sp.If(count > o):
                        sp.wait_ge(m.h_done, m.was["h_done"] + m.G)
                        sp.wait_ge(m.y_done, m.was["y_done"] + m.G)
                        e = sp.value_load(more[0:1, bass.ds(o + 1, 1)], min_val=0, max_val=NE - 1)
                        for part in range(3):
                            for dst, src in expert_of(m.l, e, part, part):
                                sp.dma_start(dst, src).then_inc(m.further_loaded, 16)
                        sp.wait_ge(m.further_pe, after(PE_STEPS, o, "down"))
                        sp.sem_inc(sp_held, 1)
            experts(moes[0])
            experts_again(moes[0])
            for j in range(ADA_CHUNKS):
                load(N_ADA1 + j, ada_of(1, N_ADA1 + j, j))
            for j, cb in ((0, 2), (1, 0), (3, 3), (4, 1)):
                if j == 3:
                    d = slot(N_MIX1 + 2).rearrange("p (d n e) -> p d n e", d=2, n=8)
                    load(N_MIX1 + 2, [(d[:, i], r_gate[:, i]) for i in range(2)])
                load(N_MIX1 + j, cols_of(r_in, N_MIX1 + j, cb))
            for cb in range(2):
                load(N_OUT1 + cb, cols_of(a["r_w_out"][0], N_OUT1 + cb, cb))
            experts(moes[1])
            experts_again(moes[1])
            for t in range(2):
                sp.wait_ge(stored, 16 * (t + 1))

        def use(pe, n, i=0):
            pe.wait_ge(ld[n % SLOTS], 32 * (n // SLOTS + 1) + 32 * i)

        @block.gpsimd
        def _(pool):
            steps = [0]

            def step(ins):
                steps[0] += 1
                ins.then_inc(pool_step, 1)
                pool.wait_ge(pool_step, steps[0])

            step(pool.memset(wg, 0.0))
            pool.memset(bgate[:, :], 0.0).then_inc(bg_zero, 1)
            step(pool.memset(ident[:, :], 0.0))
            step(pool.affine_select(out=ident[:, :], in_=ident[:, :], compare_op=ALU.not_equal, fill=1.0,
                                    base=0, pattern=[[-1, P]], channel_multiplier=1))
            step(pool.memset(masks[:, :, :], 0.0))
            step(pool.affine_select(out=masks[:, 0, :], in_=masks[:, 0, :], compare_op=ALU.is_ge, fill=NEG,
                                    base=0, pattern=[[1, P]], channel_multiplier=-1))
            step(pool.affine_select(out=masks[:, 1, :], in_=masks[:, 1, :], compare_op=ALU.is_ge, fill=NEG,
                                    base=0, pattern=[[-1, P]], channel_multiplier=1))
            step(pool.memset(ones[:, :], 1.0))
            step(pool.affine_select(out=triu[:, :], in_=ones[:, :], compare_op=ALU.is_ge, fill=0.0,
                                    base=-1, pattern=[[1, P]], channel_multiplier=-1))
            step(pool.iota(iota16i[:, :], pattern=[[1, NE]], base=0, channel_multiplier=0))
            step(pool.iota(toki[:, :], pattern=[[P, TILES]], base=0, channel_multiplier=1))
            step(pool.memset(pad, PAD))
            for m in moes:
                pool.dma_start(m.table.rearrange("(p n) o -> p (n o)", p=P), pad).then_inc(table_ready, 16)
            pool.wait_ge(table_ready, 32)
            pool.memset(mhalf[:, :], -0.5).then_inc(consts, 1)
            pool.wait_ge(consts, 1)

            def rstd(t0, squares):
                pool.wait_ge(ss_ready, squares)
                step(pool.tensor_scalar(stat[:, 1, t0:TILES], stat[:, 0, t0:TILES], 1.0 / D, EPS, ALU.mult, ALU.add))
                pool.tensor_tensor(stat[:, 2, t0:TILES], stat[:, 1, t0:TILES], mhalf[:, t0:TILES], ALU.pow
                                   ).then_inc(rstd_ready, 1)

            def held():
                pool.sem_inc(pool_held, 1)

            def gather(m, g, par):
                if not isinstance(g, int) or g >= 2:
                    pool.wait_ge(m.tx_done, m.was["tx_done"] + g - 1)
                    held()
                pool.tensor_copy(gi[:, par:par + 1], GIX[:, bass.ds(g, 1)]).then_inc(m.gi_ready, 1)
                pool.wait_ge(m.gi_ready, m.was["gi_ready"] + g + 1)
                held()
                pool.indirect_dma_start(XG[:, par, :], None, m.hhalf,
                                        bass.IndirectOffsetOnAxis(ap=gi[:, par:par + 1], axis=0)
                                        ).then_inc(m.gathered[par], 16)

            def scatter(m, g, par, at):
                if not isinstance(at, int) or at >= 1:
                    pool.wait_ge(m.scattered[par], m.was["scattered"] + 16 * at)
                    held()
                pool.tensor_copy(si[:, par:par + 1], SIX[:, bass.ds(g, 1)]).then_inc(m.si_ready, 1)
                pool.wait_ge(m.si_ready, m.was["si_ready"] + g + 1)
                pool.wait_ge(m.ys_ready, m.was["ys_ready"] + g + 1)
                held()
                pool.indirect_dma_start(m.yhalf, bass.IndirectOffsetOnAxis(ap=si[:, par:par + 1], axis=0),
                                        YS[:, par, :], None, bounds_check=4 * m.T - 1, oob_is_err=False
                                        ).then_inc(m.scattered[par], 16)

            def route_pool(m, squares):
                rstd(m.tiles[0], squares)
                pool.wait_ge(m.addr_ready, m.was["addr_ready"] + 1)
                for r in range(2 * m.nt):
                    pool.indirect_dma_start(m.table, bass.IndirectOffsetOnAxis(ap=m.addr[:, r:r + 1], axis=0),
                                            m.value[:, r:r + 1], None).then_inc(m.filled, 16)
                pool.wait_ge(m.filled, m.was["filled"] + 32 * m.nt)
                rows = m.table.rearrange("(e c s) o -> c e (s o)", e=NE, s=PASS)
                for c in range(m.subs):
                    for h in range(2):
                        pool.dma_start(LST[c:m.G:m.subs, PASS * h:PASS * h + PASS], rows[c]).then_inc(m.list_in, 16)

            LAG = 3

            def passes_pool(m):
                pool.wait_ge(m.lists_ready, m.was["lists_ready"] + 1)
                pool.wait_ge(m.rows_stored, m.was["rows_stored"] + 16 * m.nt)
                n = 2 * m.subs

                def body(i, first):
                    for r in range(n):
                        g = i * n + r
                        gather(m, g, r % 2)
                        if not first or r >= LAG:
                            scatter(m, g - LAG, (r - LAG) % 2, (i * n + r - LAG) // 2 if isinstance(i, int)
                                    else i * (n // 2) + (r - LAG) // 2)
                body(0, True)
                if n < LAG:
                    for r in range(n):
                        g = n + r
                        gather(m, g, r % 2)
                        if g >= LAG:
                            scatter(m, g - LAG, (g - LAG) % 2, (g - LAG) // 2)
                with pool.Fori(1 if n >= LAG else 2, NE // 2) as i:
                    body(i, False)
                for g in range(m.G - LAG, m.G):
                    scatter(m, g, g % 2, g // 2)

            def further_pool(m):
                pool.wait_ge(m.scattered[0], m.was["scattered"] + 8 * m.G)
                pool.wait_ge(m.scattered[1], m.was["scattered"] + 8 * m.G)
                pool.wait_ge(m.more_ready, m.was["more_ready"] + 1)
                count = pool.value_load(more[0:1, 0:1], min_val=0, max_val=m.most)
                rows = m.table.rearrange("(r s) o -> r (o s)", s=PASS)
                with pool.Fori(0, m.most) as o:
                    with pool.If(count > o):
                        r = pool.value_load(more[0:1, bass.ds(o + 16, 1)], min_val=0, max_val=NE * CAP // PASS - 1)
                        for h in range(2):
                            pool.dma_start(orow[:, PASS * h:PASS * h + PASS], rows[bass.ds(r, 1), :]).then_inc(m.further_dma, 16)
                        pool.wait_ge(m.further_dve, after(DVE_STEPS, o, "scatter_index"))
                        held()
                        pool.indirect_dma_start(XG[:, 0, :], None, m.hhalf, bass.IndirectOffsetOnAxis(ap=ogi, axis=0)
                                                ).then_inc(m.further_dma, 16)
                        pool.wait_ge(m.further_act, after(ACT_STEPS, o, "y_kept"))
                        held()
                        pool.indirect_dma_start(m.yhalf, bass.IndirectOffsetOnAxis(ap=osi, axis=0), YS[:, 0, :], None,
                                                bounds_check=4 * m.T - 1, oob_is_err=False).then_inc(m.further_dma, 16)
                        pool.wait_ge(m.further_dma, 64 * o + 64)
                        held()
                pool.sem_inc(m.passes_over, 1)

            rstd(0, 4)
            for t in range(TILES):
                pool.wait_ge(hss_ready, t + 1)
                step(pool.tensor_scalar(hs[:, t], hs[:, t], 1.0 / DV, EPS, ALU.mult, ALU.add))
                pool.tensor_tensor(hs[:, t], hs[:, t], mhalf[:, :], ALU.pow).then_inc(hr_ready, 1)
            route_pool(moes[0], 8)
            passes_pool(moes[0])
            further_pool(moes[0])
            rstd(0, 12)
            route_pool(moes[1], 14)
            passes_pool(moes[1])
            further_pool(moes[1])
            rstd(2, 16)

        def keep_fwd(act, u):
            h = u // 2
            act.wait_ge(den_ready, u + 1)
            for j in range(TILES):
                ins = act.activation(H[:, j, h, :], ps[:, 5 + j // 2, DVX * (j % 2):DVX * (j % 2) + DV], ACT.Copy,
                                     scale=att[:, u % 2, j:j + 1])
            ins.then_inc(fin_act, 1)

        @block.scalar
        def _(act):
            act.dma_start(cvec[:, 0, :], a["c_ctx"].rearrange("(k p) -> p k", p=P)).then_inc(cv_in, 16)
            act.dma_start(cvec[:, 1, :], a["c"][0].rearrange("(k p) -> p k", p=P)).then_inc(cv_in, 16)
            for q in range(4):
                act.dma_start(bada[32 * q:32 * q + 32, :, :],
                              a["b_ada"][0].rearrange("(g q n) -> q g n", g=3, q=4)[q:q + 1].to_broadcast([32, 3, 512])
                              ).then_inc(bada_in, 16)
            for t in range(TILES):
                src = a["ctx"][0] if t < 2 else a["x"][0]
                act.dma_start(X[:, t, :], src[P * (t % 2):P * (t % 2) + P, :]).then_inc(x_in, 16)
            for t in range(2):
                act.dma_start(XN[:, 2 + t, :], a["pos"][P * t:P * t + P, :]).then_inc(pos_in, 16)
            for l in range(2):
                act.dma_start(gmix[:, l, :], a["g_mix"][l].rearrange("(k p) -> p k", p=P)).then_inc(small_in, 16)
            act.dma_start(ghead[:, :], a["m_g_head"][0].rearrange("(k p) -> p k", p=P)).then_inc(small_in, 16)
            act.dma_start(brt[:, :], a["b_router"].rearrange("(o e) -> o e", o=1).to_broadcast([P, NE])).then_inc(small_in, 16)
            act.dma_start(wrt[:, :, :], a["w_router"].rearrange("(k p) e -> p k e", p=P)).then_inc(small_in, 16)
            act.dma_start(convw[:, :, :], a["r_conv_w"][0].rearrange("j (k p) -> p j k", p=P)).then_inc(rg_in, 16)
            act.dma_start(convb[:, :], a["r_conv_b"][0].rearrange("(k p) -> p k", p=P)).then_inc(rg_in, 16)
            act.dma_start(lam[:, :, :], a["r_lam"][0].rearrange("d (k p) -> p d k", p=P)).then_inc(rg_in, 16)
            for d in range(2):
                act.dma_start(rbias[:, d, :, :], a["r_b_gate"][0][d].rearrange("n (e p) -> p n e", p=P)).then_inc(rg_in, 16)
            act.wait_ge(pool_step, 1)
            act.wait_ge(bg_zero, 1)
            wgv = m_in[:, 3072:3104].rearrange("(k p) (g h) -> p k g h", p=P, g=4)
            for t in range(2):
                for d in range(2):
                    act.dma_start(wg[:, :, t, d, 0:HEADS], wgv[:, :, 2 * d + t, :]).then_inc(wg_in, 16)
                    act.dma_start(bgate[64 * t + 32 * d:64 * t + 32 * d + HEADS, :],
                                  a["m_b_gate"][0][2 * d + t].rearrange("(h o) -> h o", o=1)).then_inc(wg_in, 16)

            steps = [0]

            def step(ins):
                steps[0] += 1
                ins.then_inc(act_step, 1)
                act.wait_ge(act_step, steps[0])

            def gate2_act(base, tiles):
                for b in range(tiles):
                    s, cb = 2 - tiles // 2 + b // 2, b % 2
                    act.wait_ge(g2_done, base + b + 1)
                    act.activation(gate2[:, s, 512 * cb:512 * cb + 512], ps[:, 3 + b % 2, :], ACT.Copy).then_inc(g2_ready, 1)

            act.wait_ge(cv_in, 32)
            act.activation(cvec[:, :, :], cvec[:, :, :], ACT.Silu).then_inc(silu_ready, 1)

            def norm_mix(l):
                for t in range(TILES):
                    if l == 0:
                        act.wait_ge(x_ready, t + 1)
                    else:
                        act.wait_ge(moes[0].added, TILES)
                    act.activation(XN[:, t, :], X[:, t, :], ACT.Square, accum_out=stat[:, 0, t:t + 1]
                                   ).then_inc(ss_ready, 1)
                for t in range(TILES):
                    act.wait_ge(rstd_ready, 2 * l + 1)
                    act.activation(XN[:, t, :], X[:, t, :], ACT.Copy, scale=stat[:, 2, t:t + 1]).then_inc(xn_ready, 1)
                act.wait_ge(cols_ready, l + 1)
                for b in range(0, 8, 2):
                    s, kp = b // 4, b % 4
                    act.wait_ge(nt_done, 8 * l + b + 1)
                    for kk in range(2):
                        k = 2 * kp + kk
                        ins = act.activation(hT[:, k, 256 * s:256 * s + 256], ps[:, 4 + b % 4, 256 * kk:256 * kk + 256],
                                             ACT.Identity, bias=bcol[:, s, k:k + 1], scale=acol[:, s, k:k + 1])
                    ins.then_inc(nt_act, 1)

            norm_mix(0)

            tm, em = gtmp[0:64, 4, :], gtmp[64:128, 5, :]
            act.wait_ge(lsig_ready, 1)
            step(act.activation(tm, tm, ACT.Exp))
            act.activation(tm, tm, ACT.Ln, bias=1.0).then_inc(lsig_kept, 1)
            for g in range(16):
                if g == 4:
                    act.wait_ge(em_ready, 2)
                    act.activation(em, em, ACT.Exp).then_inc(gates_ready, 1)
                act.wait_ge(proj_done, g + 1)
                if g < 4:
                    ins = act.activation(qT[:, g, :], ps[:, g % 4, :], ACT.Copy, scale=float(DQK) ** -0.5)
                elif g < 8:
                    ins = act.activation(kT[:, g - 4, :], ps[:, g % 4, :], ACT.Copy)
                else:
                    cb, t = (g - 8) // 4, g % 4
                    if g == 8:
                        act.wait_ge(gate_done, 1)
                    ins = act.activation(V[:, t, 4 * cb:4 * cb + 4, 0:DV],
                                         ps[:, g % 4, :].rearrange("p (h v) -> p h v", h=4), ACT.Copy)
                ins.then_inc(proj_kept, 1)

            for u in range(16):
                h, d = u // 2, u % 2
                act.wait_ge(d_done, u + 1)
                wd = W[:, u % 2].rearrange("p s j n -> p (s j) n")[:, 0:16:5, :]
                act.activation(wd, wd, ACT.Exp)
                todo = [(s, j, c) for s in range(TILES)
                        for j, c in runs_of([q for q in PAIRS[d] if q[0] != q[1]], s)]
                for s, j, c in todo:
                    ins = act.activation(W[:, u % 2, s, j:j + c, :], ps[:, 3 + u % 2, P * j:P * (j + c)].rearrange("p (j n) -> p j n", n=P),
                                         ACT.Exp, bias=gcol[:, s, 32 * d + h:32 * d + h + 1])
                ins.then_inc(e_done, 1)
                if u >= 1 and (u - 1) % 2 == 0:
                    keep_fwd(act, u - 1)
            for g in range(8):
                cb, t = g // 4, g % 4
                act.wait_ge(oproj_done, g + 1)
                act.activation(O[:, t, 512 * cb:512 * cb + 512], ps[:, g % 3, :], ACT.Sigmoid).then_inc(og_ready, 1)
            act.wait_ge(o_done, 16)
            gate2_act(0, TILES)
            act.wait_ge(out_added, 8)

            def route_act(m):
                l, t0 = m.l, m.tiles[0]
                act.dma_start(gffn, a["g_ffn"][l].rearrange("(o n) -> o n", o=1).to_broadcast([P, D])).then_inc(m.gffn_in, 16)
                for t in m.tiles:
                    act.activation(XN[:, t, :], X[:, t, :], ACT.Square, accum_out=stat[:, 0, t:t + 1]).then_inc(ss_ready, 1)
                ns = m.nt // 2
                for b in range(2 * ns):
                    s, cb = 2 - ns + b // 2, b % 2
                    act.wait_ge(m.rows_done, m.was["rows_done"] + 2 * b + 2)
                    act.activation(ab[:, 1, s, 512 * cb:512 * cb + 512], ps[:, 4, :], ACT.Copy).then_inc(m.shift_kept, 1)
                for i in range(m.nt):
                    act.wait_ge(m.h_ready, m.was["h_ready"] + i + 1)
                    act.dma_start(m.hrows[P * i:P * i + P, :], XN[:, t0 + i, :]).then_inc(m.rows_stored, 16)
                for b in range(0, 2 * m.nt, 2):
                    i = b // 2
                    act.wait_ge(m.turned, m.was["turned"] + b + 1)
                    act.activation(hT[:, 0:4, P * (t0 + i):P * (t0 + i) + P], ps[:, 5, :].rearrange("p (k n) -> p k n", k=4),
                                   ACT.Copy).then_inc(m.turn_kept_act, 1)
                act.wait_ge(m.shifted, m.was["shifted"] + 1)
                lg = sm[:, 0, 0:NE * m.nt]
                act.activation(lg, lg, ACT.Exp).then_inc(m.expd, 1)

            def passes_act(m):
                def silu(g, par):
                    act.wait_ge(m.h_done, m.was["h_done"] + g + 1)
                    if not isinstance(g, int) or g >= 2:
                        act.wait_ge(m.u_ready, m.was["u_ready"] + g - 1)
                    act.activation(SG[:, par, :], ps[:, 2 + par, 0:256], ACT.Silu).then_inc(m.silu_done, 1)

                def keep_y(g, par, at):
                    act.wait_ge(m.y_done, m.was["y_done"] + g + 1)
                    if not isinstance(at, int) or at >= 1:
                        act.wait_ge(m.scattered[par], m.was["scattered"] + 16 * at)
                    act.activation(YS[:, par, :], ps[:, 6 + par, :], ACT.Copy).then_inc(m.ys_ready, 1)

                def body(i):
                    n = 2 * m.subs
                    for e in range(2):
                        for r in range(e * m.subs, (e + 1) * m.subs):
                            silu(i * n + r, r % 2)
                        for r in range(e * m.subs, (e + 1) * m.subs):
                            keep_y(i * n + r, r % 2, i * m.subs + r // 2)
                body(0)
                with act.Fori(1, NE // 2) as i:
                    body(i)

            def rglru_act():
                act.wait_ge(lam_u, 1)
                act.activation(lt[:, 0, :], lt[:, 0, :], ACT.Exp).then_inc(lam_exp, 1)
                act.wait_ge(lam_u, 2)
                act.activation(lt[:, 2, :], lt[:, 1, :], ACT.Ln).then_inc(lam_ln, 1)
                for what, n in RG_ORDER:
                    if what == "x":
                        act.wait_ge(xr_done, n + 1)
                        act.wait_ge(pads, 1)
                        if n >= 2:
                            act.wait_ge(conv_done, n - 1)
                        act.activation(xpad[:, n % 2, :, 2:258], ps[:, n % 2, :].rearrange("p (s n) -> p s n", s=2), ACT.Copy
                                       ).then_inc(xr_kept, 1)
                    elif what == "y":
                        act.wait_ge(yb_done, n + 1)
                        act.activation(YB[:, n, :], ps[:, 2 + n % 2, 0:256], ACT.Gelu_apprx_tanh).then_inc(yb_kept, 1)
                    else:
                        act.wait_ge(lam_ready, 1)
                        for d in range(2):
                            act.wait_ge(rg_done, 2 * n + d + 1)
                            if n >= 1:
                                act.wait_ge(rg_scan, 2 * (n - 1) + d + 1)
                            for e in range(2):
                                ins = act.activation(RB[:, d, e, :], ps[:, 4 + 2 * d + e, :], ACT.Tanh,
                                                     bias=rbias[:, d, n, e:e + 1], scale=0.5)
                            step(ins)
                            act.activation(RB[:, d, 3, :], RB[:, d, 0, :], ACT.Exp, bias=spn[:, d, n:n + 1],
                                           scale=spn[:, d, n:n + 1])
                            step(act.activation(RB[:, d, 2, :], RB[:, d, 0, :], ACT.Tanh, bias=spl[:, d, n:n + 1],
                                                scale=spl[:, d, n:n + 1]))
                            act.activation(RB[:, d, 0, :], RB[:, d, 3, :], ACT.Square).then_inc(rg_tanh, 1)
                        for d in range(2):
                            act.wait_ge(rg_q, 2 * n + d + 1)
                            act.activation(RB[:, d, 2, :], RB[:, d, 2, :], ACT.Sqrt, scale=0.25).then_inc(rg_sqrt, 1)

            def further_act(m):
                act.wait_ge(m.more_ready, m.was["more_ready"] + 1)
                count = act.value_load(more[0:1, 0:1], min_val=0, max_val=m.most)
                with act.Fori(0, m.most) as o:
                    with act.If(count > o):
                        act.wait_ge(m.further_pe, after(PE_STEPS, o, "up"))
                        act.activation(SG[:, 0, :], ps[:, 2, 0:256], ACT.Silu).then_inc(m.further_act, 1)
                        act.wait_ge(m.further_pe, after(PE_STEPS, o, "down"))
                        act.activation(YS[:, 0, :], ps[:, 6, :], ACT.Copy).then_inc(m.further_act, 1)

            def combine_act(m):
                ns = m.nt // 2
                for b in range(2 * ns):
                    s, cb = 2 - ns + b // 2, b % 2
                    act.wait_ge(m.g5_done, m.was["g5_done"] + b + 1)
                    act.activation(g5[:, s, 512 * cb:512 * cb + 512], ps[:, 3 + b % 2, :], ACT.Copy).then_inc(m.g5_kept, 1)
                act.wait_ge(m.passes_over, m.was["passes_over"] + 1)
                for i in range(m.nt):
                    if i >= 2:
                        act.wait_ge(m.added, m.was["added"] + i - 1)
                    for k in range(2):
                        act.dma_start(XN[:, 2 * (i % 2) + k, :], m.yrows[m.T * k + P * i:m.T * k + P * i + P, :]
                                      ).then_inc(m.y_in, 16)
                    act.wait_ge(m.y_in, m.was["y_in"] + 32 * (i + 1))
                    y0 = XN[:, 2 * (i % 2), :]
                    act.activation(y0, y0, ACT.Copy, scale=m.weight[:, i:i + 1]).then_inc(m.y_scaled, 1)

            route_act(moes[0])
            passes_act(moes[0])
            further_act(moes[0])
            combine_act(moes[0])
            for q in range(4):
                act.dma_start(bada[32 * q:32 * q + 32, :, :],
                              a["b_ada"][1].rearrange("(g q n) -> q g n", g=3, q=4)[q:q + 1].to_broadcast([32, 3, 512])
                              ).then_inc(bada_in, 16)
            norm_mix(1)
            rglru_act()
            gate2_act(4, 2)
            act.wait_ge(out_added, 12)
            route_act(moes[1])
            passes_act(moes[1])
            further_act(moes[1])
            combine_act(moes[1])
            act.wait_ge(moes[1].added, moes[1].was["added"] + 2)
            act.dma_start(gffn, a["g_final"].rearrange("(o n) -> o n", o=1).to_broadcast([P, D])).then_inc(gfin_in, 16)
            for t in (2, 3):
                act.activation(XN[:, t, :], X[:, t, :], ACT.Square, accum_out=stat[:, 0, t:t + 1]).then_inc(ss_ready, 1)
            for t in range(2):
                act.wait_ge(fin_ready, t + 1)
                act.dma_start(out[0, P * t:P * t + P, :], XN[:, 2 + t, :]).then_inc(stored, 16)

        @block.tensor
        def _(pe):
            def ada(l):
                base = N_ADA0 if l == 0 else N_ADA1
                pe.wait_ge(silu_ready, 2)
                for g in range(3):
                    for kk in range(4):
                        c = base + 4 * g + kk
                        use(pe, c)
                        w = slot(c).rearrange("p (k q n) -> p k q n", k=2, q=4)
                        for k2 in range(2):
                            k = 2 * kk + k2
                            for q in range(4):
                                ins = pe.matmul(ps[32 * q:32 * q + 32, g, :],
                                                silu_c[:, k, :, :].rearrange("p s r -> p (s r)"),
                                                w[:, k2, q, :], start=(k == 0), stop=(k == KD - 1))
                        ins.then_inc(ada_done if kk == 3 else ada_part, 1)

            def modcol(l):
                pe.wait_ge(modr_ready, 3 * l + 1)
                pe.wait_ge(consts, 1)
                for c in range(4):
                    ins = pe.transpose(ps[:, 3, P * c:P * c + P], modr[:, 0, P * c:P * c + P], ident[:, :])
                ins.then_inc(modcol_done, 1)

            def norm_turn(l):
                for b in range(8):
                    s, kp = b // 4, b % 4
                    pe.wait_ge(xn_ready, TILES * l + 2 * s + 2)
                    if b >= 4:
                        pe.wait_ge(nt_act if b % 2 == 0 else nt_dve, 4 * l + (b - 4) // 2 + 1)
                    for kk in range(2):
                        for t in range(2):
                            k = 2 * kp + kk
                            ins = pe.transpose(ps[:, 4 + b % 4, 256 * kk + P * t:256 * kk + P * t + P],
                                               XN[:, 2 * s + t, P * k:P * k + P], ident[:, :])
                    ins.then_inc(nt_done, 1)

            ada(0)
            modcol(0)
            norm_turn(0)

            pe.wait_ge(nt_act, 4)
            pe.wait_ge(nt_dve, 4)
            pe.wait_ge(wg_in, 128)
            for k in range(KD):
                for t in range(2):
                    ins = pe.matmul(ps[64 * t:64 * t + 64, 4, :], wg[:, k, t, :, :].rearrange("p d r -> p (d r)"),
                                    hT[:, k, :], start=(k == 0), stop=(k == KD - 1))
            ins.then_inc(gate_done, 1)
            for g in range(16):
                if g >= 4:
                    pe.wait_ge(proj_kept, g - 3)
                elif g < 3:
                    pe.wait_ge(modr_ready, g + 1)
                else:
                    pe.wait_ge(cols_ready, 1)
                cb = g // 4
                c = N_MIX0 + cb
                if g % 4 == 0:
                    use(pe, c)
                w = slot(c).rearrange("p (k n) -> p k n", k=KD)
                for k in range(KD):
                    if g < 8:
                        l_, r_ = w[:, k, P * (g % 4):P * (g % 4) + P], hT[:, k, :]
                    else:
                        l_, r_ = hT[:, k, P * (g % 4):P * (g % 4) + P], w[:, k, :]
                    ins = pe.matmul(ps[:, g % 4, :], l_, r_, start=(k == 0), stop=(k == KD - 1))
                ins.then_inc(proj_done, 1)
            pe.wait_ge(gates_ready, 1)
            for t in range(TILES):
                ins = pe.transpose(ps[:, 7, P * t:P * t + P], gtmp[:, 5, P * t:P * t + P], ident[:, :])
            ins.then_inc(gturn_done, 1)

            def scores(h):
                p0 = 64 * (h % 2)
                for s in range(TILES):
                    o = ps[:, s, :] if s < 2 else ps[:, 2, 256 * (s - 2):256 * (s - 2) + 256]
                    j0 = 0 if s < 2 else 256
                    ins = pe.matmul(o, kT[p0:p0 + 64, h // 2, P * s:P * s + P], qT[p0:p0 + 64, h // 2, j0:T_ALL],
                                    start=True, stop=True)
                ins.then_inc(s_done, 1)

            def rows(u):
                r = 32 * (u % 2) + u // 2
                if u >= 2:
                    pe.wait_ge(e_done, u - 1)
                pe.matmul(ps[:, 3 + u % 2, :], ident[0:64, r:r + 1].to_broadcast([64, P]), rrow[:, :],
                          start=True, stop=True).then_inc(r_done, 1)

            pe.wait_ge(proj_kept, 16)
            scores(0)
            pe.wait_ge(gcol_ready, 1)
            pe.wait_ge(v_ones, 1)
            rows(0)
            for u in range(16):
                h, d = u // 2, u % 2
                if u < 15:
                    rows(u + 1)
                pe.wait_ge(p_done, u + 1)
                if d == 1 and h + 1 < HEADS:
                    scores(h + 1)
                if u >= 1:
                    pe.wait_ge(fin_act if (u - 1) % 2 == 0 else fin_dve, (u - 1) // 2 + 1)
                for j in range(TILES):
                    keys = (fwd_keys if d == 0 else bwd_keys)(j)
                    for s in keys:
                        ins = pe.matmul(ps[:, 5 + j // 2, DVX * (j % 2):DVX * (j % 2) + DVX], W[:, u % 2, s, j, :],
                                        V[:, s, h, :], start=(s == keys[0]), stop=(s == keys[-1]))
                ins.then_inc(o_done, 1)

            for g in range(8):
                cb, t = g // 4, g % 4
                c = N_MIX0 + 4 + cb
                if t == 0:
                    use(pe, c)
                if g >= 3:
                    pe.wait_ge(og_ready, g - 2)
                w = slot(c).rearrange("p (k n) -> p k n", k=KD)
                for k in range(KD):
                    ins = pe.matmul(ps[:, g % 3, :], hT[:, k, P * t:P * t + P], w[:, k, :],
                                    start=(k == 0), stop=(k == KD - 1))
                ins.then_inc(oproj_done, 1)

            def gate_rows(vec, done, kept, base):
                for b in range(4):
                    s, cb = b // 2, b % 2
                    col = 2 * vec + cb
                    if b >= 2:
                        pe.wait_ge(kept, base + b - 1)
                    r = 32 * (col % 4) + 16 * s
                    pe.matmul(ps[:, 3 + b % 2, :], ident[:, r:r + 1].to_broadcast([P, P]), modr[:, col // 4, :],
                              start=True, stop=True).then_inc(done, 1)

            pe.wait_ge(e_done, 16)
            gate_rows(2, g2_done, g2_ready, 0)

            def out_proj(base, tiles, ybuf, n0):
                for cb in range(2):
                    c = base + cb
                    use(pe, c)
                    w = slot(c).rearrange("p (k n) -> p k n", k=KD)
                    for i in range(tiles):
                        g = cb * tiles + i
                        if g >= 3:
                            pe.wait_ge(out_added, n0 + g - 2)
                        for k in range(KD):
                            ins = pe.matmul(ps[:, g % 3, :], ybuf(k, i), w[:, k, :], start=(k == 0), stop=(k == KD - 1))
                        ins.then_inc(out_done, 1)

            for t in range(TILES):
                pe.wait_ge(y_ready, t + 1)
                for b in range(2):
                    g = 2 * t + b
                    if g >= 3:
                        pe.wait_ge(yt_kept, g - 2)
                    for kk in range(4):
                        k = 4 * b + kk
                        ins = pe.transpose(ps[:, 5 + g % 3, P * kk:P * kk + P], XN[:, t, P * k:P * k + P], ident[:, :])
                    ins.then_inc(yt_done, 1)
            pe.wait_ge(og_ready, 8)
            pe.wait_ge(yt_kept, 8)
            out_proj(N_OUT0, TILES, lambda k, t: hT[:, k, P * t:P * t + P], 0)

            def bcast(col, s, bank):
                r = 32 * (col % 4) + 16 * s
                return pe.matmul(ps[:, bank, :], ident[:, r:r + 1].to_broadcast([P, P]), modr[:, col // 4, :],
                                 start=True, stop=True)

            def route_pe(m, added):
                ns, t0 = m.nt // 2, m.tiles[0]
                for b in range(2 * ns):
                    s, cb = 2 - ns + b // 2, b % 2
                    if b >= 1:
                        pe.wait_ge(m.scale_kept, m.was["scale_kept"] + b)
                    bcast(2 * 4 + cb, s, 3).then_inc(m.rows_done, 1)
                    if b >= 1:
                        pe.wait_ge(m.shift_kept, m.was["shift_kept"] + b)
                    bcast(2 * 3 + cb, s, 4).then_inc(m.rows_done, 1)
                for i in range(m.nt):
                    pe.wait_ge(m.h_ready, m.was["h_ready"] + i + 1)
                    for b in range(2):
                        if i >= 1:
                            pe.wait_ge(m.turn_kept_dve if b else m.turn_kept_act, m.was["turn_kept_act"] + i)
                        for kk in range(4):
                            k = 4 * b + kk
                            ins = pe.transpose(ps[:, 5 + b, P * kk:P * kk + P], XN[:, t0 + i, P * k:P * k + P], ident[:, :])
                        ins.then_inc(m.turned, 1)
                for i in range(m.nt):
                    pe.wait_ge(m.turn_kept_act, m.was["turn_kept_act"] + i + 1)
                    pe.wait_ge(m.turn_kept_dve, m.was["turn_kept_dve"] + i + 1)
                    for k in range(KD):
                        ins = pe.matmul(ps[:, 7, NE * i:NE * i + NE], hT[:, k, P * (t0 + i):P * (t0 + i) + P], wrt[:, k, :],
                                        start=(k == 0), stop=(k == KD - 1))
                ins.then_inc(m.logits_done, 1)
                pe.wait_ge(m.picked, m.was["picked"] + 1)
                both = sm[:, 3, 0:NE * m.nt].rearrange("p (t e) -> p t e", e=NE)
                for i in range(m.nt + 1):
                    o = ps[:, 0, NE * i:NE * i + NE]
                    for j in range(min(i, m.nt - 1) + 1):
                        ins = pe.matmul(o, triu[:, :] if j == i else ones[:, :], both[:, j, :],
                                        start=(j == 0), stop=(j == min(i, m.nt - 1)))
                ins.then_inc(m.pos_done, 1)
                pe.wait_ge(m.list_in, m.was["list_in"] + 32 * m.subs)
                pe.transpose(ps[:, 1, 0:m.G], LST[0:m.G, :], ident[0:m.G, 0:m.G]).then_inc(m.list_turned, 1)

            def up_half(par, h, chunk):
                w = slot(chunk).rearrange("p (k w n) -> p k w n", k=4, w=2)
                for j in range(4):
                    for oh in range(2):
                        ins = pe.matmul(ps[64 * oh:64 * oh + 64, 2 + par, :].rearrange("p (w n) -> p w n", w=2),
                                        XT[:, par, j, 64 * h:64 * h + 64], w[:, j, :, 256 * oh:256 * oh + 256],
                                        start=(h == 0 and j == 0), stop=(h == 1 and j == 3))
                return ins

            def down_all(par, chunk):
                w = slot(chunk).rearrange("p (c n) -> p c n", c=4)
                for kc in range(4):
                    for oh in range(2):
                        ins = pe.matmul(ps[64 * oh:64 * oh + 64, 6 + par, :],
                                        UT[:, par, kc % 2, 64 * (kc // 2):64 * (kc // 2) + 64],
                                        w[:, kc, 512 * oh:512 * oh + 512], start=(kc == 0), stop=(kc == 3))
                return ins

            def passes_pe(m):
                n = 2 * m.subs

                def turn(g, par, at):
                    pe.wait_ge(m.gathered[par], m.was["gathered"] + 16 + 16 * at)
                    if not isinstance(g, int) or g >= 2:
                        pe.wait_ge(m.xt_ready, m.was["xt_ready"] + g - 1)
                    for j in range(4):
                        ins = pe.transpose(ps[:, par, P * j:P * j + P], XG[:, par, P * j:P * j + P], ident[:, :])
                    ins.then_inc(m.tx_done, 1)

                def up(g, par, h, chunk, i, load, sig):
                    if h == 0:
                        pe.wait_ge(m.xt_ready, m.was["xt_ready"] + g + 1)
                        if not isinstance(g, int) or g >= 2:
                            pe.wait_ge(m.u_ready, m.was["u_ready"] + g - 1)
                    if load:
                        use(pe, chunk, i)
                    ins = up_half(par, h, chunk)
                    if sig is not None:
                        ins.then_inc(sig, 1)

                def turn_u(g, par):
                    pe.wait_ge(m.u_ready, m.was["u_ready"] + g + 1)
                    if not isinstance(g, int) or g >= 2:
                        pe.wait_ge(m.ut_ready, m.was["ut_ready"] + g - 1)
                    for c in range(2):
                        ins = pe.transpose(ps[:, 4 + par, P * c:P * c + P], U[:, par, P * c:P * c + P], ident[:, :])
                    ins.then_inc(m.tu_done, 1)

                def down(g, par, chunk, i, load):
                    pe.wait_ge(m.ut_ready, m.was["ut_ready"] + g + 1)
                    if not isinstance(g, int) or g >= 2:
                        pe.wait_ge(m.ys_ready, m.was["ys_ready"] + g - 1)
                    if load:
                        use(pe, chunk, i)
                    down_all(par, chunk).then_inc(m.y_done, 1)

                def body(i, last):
                    for b in range(2):
                        c = m.base + 3 * b
                        r = b * m.subs
                        g = i * n + r
                        at = i * (n // 2)
                        if m.subs == 2:
                            turn(g + 1, 1, at + (r + 1) // 2)
                            up(g, 0, 0, c, i, True, None)
                            up(g, 0, 1, c + 1, i, True, m.h_done)
                            up(g + 1, 1, 0, c, i, False, m.half_done)
                            turn_u(g, 0)
                            up(g + 1, 1, 1, c + 1, i, False, m.h_done)
                            down(g, 0, c + 2, i, True)
                            turn_u(g + 1, 1)
                            if not (last and b == 1):
                                turn(g + 2, 0, at + (r + 2) // 2)
                            down(g + 1, 1, c + 2, i, False)
                        else:
                            up(g, b, 0, c, i, True, m.half_done)
                            up(g, b, 1, c + 1, i, True, m.h_done)
                            if not (last and b == 1):
                                turn(g + 1, 1 - b, at + (r + 1) // 2)
                            turn_u(g, b)
                            down(g, b, c + 2, i, True)

                turn(0, 0, 0)
                body(0, False)
                with pe.Fori(1, NE // 2 - 1) as i:
                    body(i, False)
                body(NE // 2 - 1, True)

            def further_pe(m):
                pe.wait_ge(m.more_ready, m.was["more_ready"] + 1)
                pe.wait_ge(m.ys_ready, m.was["ys_ready"] + m.G)
                count = pe.value_load(more[0:1, 0:1], min_val=0, max_val=m.most)
                with pe.Fori(0, m.most) as o:
                    with pe.If(count > o):
                        pe.wait_ge(m.further_dma, 64 * o + 32)
                        pe.matmul(ps[:, 1, 0:1], orow, ones[0:1, 0:1], start=True, stop=True).then_inc(m.further_pe, 1)
                        pe.wait_ge(m.further_dma, 64 * o + 48)
                        for j in range(4):
                            ins = pe.transpose(ps[:, 0, P * j:P * j + P], XG[:, 0, P * j:P * j + P], ident[:, :])
                        ins.then_inc(m.further_pe, 1)
                        pe.wait_ge(m.further_dve, after(DVE_STEPS, o, "xt"))
                        pe.wait_ge(m.further_loaded, 96 * o + 96)
                        for h in range(2):
                            ins = up_half(0, h, h)
                        ins.then_inc(m.further_pe, 1)
                        pe.wait_ge(m.further_dve, after(DVE_STEPS, o, "u"))
                        for c in range(2):
                            ins = pe.transpose(ps[:, 4, P * c:P * c + P], U[:, 0, P * c:P * c + P], ident[:, :])
                        ins.then_inc(m.further_pe, 1)
                        pe.wait_ge(m.further_dve, after(DVE_STEPS, o, "ut"))
                        down_all(0, 2).then_inc(m.further_pe, 1)

            def combine_pe(m):
                ns = m.nt // 2
                pe.wait_ge(m.u_ready, m.was["u_ready"] + m.G)
                pe.wait_ge(m.ut_ready, m.was["ut_ready"] + m.G)
                for b in range(2 * ns):
                    s, cb = 2 - ns + b // 2, b % 2
                    if b >= 2:
                        pe.wait_ge(m.g5_kept, m.was["g5_kept"] + b - 1)
                    bcast(2 * 5 + cb, s, 3 + b % 2).then_inc(m.g5_done, 1)

            def rglru_pe():
                gates = slot(N_MIX1 + 2).rearrange("p (d n e q) -> p d n e q", d=2, n=8, e=2)
                for what, n in RG_ORDER:
                    hi = n // 4
                    if what == "g":
                        if n == 0:
                            use(pe, N_MIX1 + 2)
                        pe.wait_ge(conv_done, n + 1)
                        for d in range(2):
                            if n >= 1:
                                pe.wait_ge(rg_tanh, 2 * (n - 1) + d + 1)
                            for e in range(2):
                                ins = pe.matmul(ps[:, 4 + 2 * d + e, :], gates[:, d, n, e, :], XC[:, n, :],
                                                start=True, stop=True)
                            ins.then_inc(rg_done, 1)
                        continue
                    c = N_MIX1 + (0, 3)[hi] if what == "x" else N_MIX1 + (1, 4)[hi]
                    if n % 4 == 0:
                        use(pe, c)
                    w = slot(c).rearrange("p (k n) -> p k n", k=KD)[:, :, P * (n % 4):P * (n % 4) + P]
                    kept, done = (xr_kept, xr_done) if what == "x" else (yb_kept, yb_done)
                    if n >= 2:
                        pe.wait_ge(kept, n - 1)
                    o, t0 = (ps[:, n % 2, :], 0) if what == "x" else (ps[:, 2 + n % 2, 0:256], 256)
                    for k in range(KD):
                        ins = pe.matmul(o, w[:, k, :], hT[:, k, t0:T_ALL], start=(k == 0), stop=(k == KD - 1))
                    ins.then_inc(done, 1)

            route_pe(moes[0], 8)
            passes_pe(moes[0])
            further_pe(moes[0])
            combine_pe(moes[0])
            pe.wait_ge(moes[0].xt_ready, moes[0].G)
            pe.wait_ge(moes[0].ys_ready, moes[0].G)
            pe.wait_ge(moes[0].g5_kept, 4)
            ada(1)
            modcol(1)
            norm_turn(1)
            pe.wait_ge(nt_act, 8)
            pe.wait_ge(nt_dve, 8)
            pe.wait_ge(cols_ready, 2)
            pe.wait_ge(modr_ready, 6)
            rglru_pe()
            pe.wait_ge(yb_kept, 8)
            pe.wait_ge(rg_tanh, 16)
            for b in range(2):
                bcast(4 + b, 1, 3 + b).then_inc(g2_done, 1)
            pe.wait_ge(y_ready, TILES + 1)
            out_proj(N_OUT1, 2, lambda k, t: YT[:, k, P * t:P * t + P], 8)
            route_pe(moes[1], 12)
            passes_pe(moes[1])
            further_pe(moes[1])
            combine_pe(moes[1])

        @block.vector
        def _(dve):
            steps = [0]

            def step(ins):
                steps[0] += 1
                ins.then_inc(dve_step, 1)
                dve.wait_ge(dve_step, steps[0])

            dve.wait_ge(silu_ready, 1)
            dve.tensor_copy(silu_c[:, :, :, :].rearrange("p k s r -> p s k r"),
                            cvec[:, :, :].unsqueeze(3).to_broadcast([P, 2, KD, 16])).then_inc(silu_ready, 1)
            dve.wait_ge(x_in, 64)
            for t in range(TILES):
                if t < 2:
                    dve.tensor_copy(X[:, t, 0:1], X[:, t, 0:1]).then_inc(x_ready, 1)
                else:
                    dve.wait_ge(pos_in, 32)
                    dve.tensor_tensor(X[:, t, :], X[:, t, :], XN[:, t, :], ALU.add).then_inc(x_ready, 1)
            dve.wait_ge(consts, 1)
            step(dve.tensor_copy(iota16[:, :], iota16i[:, :]))
            step(dve.tensor_copy(tokf[:, :], toki[:, :]))
            step(dve.tensor_scalar(half[:, :], tokf[:, 0:1], 64.0, None, ALU.is_ge))

            def modulation(l):
                dve.wait_ge(bada_in, 64 * (l + 1))
                for g in range(3):
                    dve.wait_ge(ada_done, 3 * l + g + 1)
                    dve.tensor_tensor(modr[:, g, :], ps[:, g, :], bada[:, g, :], ALU.add).then_inc(modr_ready, 1)
                    if g == 0:
                        dve.wait_ge(small_in, 80)
                        dve.wait_ge(modcol_done, l + 1)
                        m = ps[:, 3, :].rearrange("p (c q r) -> p q c r", c=4, q=4)
                        for s in range(2):
                            dve.tensor_copy(bcol[:, s, :].rearrange("p (q c) -> p q c", q=2), m[:, 0:2, :, 16 * s])
                            ins = dve.scalar_tensor_tensor(
                                out=acol[:, s, :].rearrange("p (q c) -> p q c", q=2), in0=m[:, 2:4, :, 16 * s],
                                scalar=1.0, in1=gmix[:, l, :].rearrange("p (q c) -> p q c", q=2),
                                op0=ALU.add, op1=ALU.mult)
                        ins.then_inc(cols_ready, 1)

            def norm_keep(l):
                dve.wait_ge(cols_ready, l + 1)
                for b in range(1, 8, 2):
                    s, kp = b // 4, b % 4
                    dve.wait_ge(nt_done, 8 * l + b + 1)
                    for kk in range(2):
                        k = 2 * kp + kk
                        ins = dve.tensor_scalar(hT[:, k, 256 * s:256 * s + 256], ps[:, 4 + b % 4, 256 * kk:256 * kk + 256],
                                                acol[:, s, k:k + 1], bcol[:, s, k:k + 1], ALU.mult, ALU.add)
                    ins.then_inc(nt_dve, 1)

            modulation(0)
            norm_keep(0)

            dve.wait_ge(gate_done, 1)
            ig, lf, mm, bb, tm, ce = (gtmp[:, i, :] for i in range(6))
            for t, dst in ((0, ig), (1, lf)):
                for d in range(2):
                    r = 64 * t + 32 * d
                    o = dst[32 * d:32 * d + 32].rearrange("p (s n) -> p s n", s=2)
                    i = ps[r:r + 32, 4, :].rearrange("p (s n) -> p s n", s=2)
                    if d:
                        o = o[:, :, ::-1]
                    step(dve.tensor_scalar(o, i, bgate[r:r + 32, 0:1], None, ALU.add))
            g64 = slice(0, 64)
            step(dve.scalar_tensor_tensor(out=tm[g64], in0=lf[g64], scalar=-1.0, in1=lf[g64], op0=ALU.mult, op1=ALU.min))
            ins = dve.tensor_scalar(lf[g64], lf[g64], 0.0, None, ALU.min)
            ins.then_inc(lsig_ready, 1)
            dve.wait_ge(lsig_kept, 1)
            step(dve.tensor_tensor(lf[g64], lf[g64], tm[g64], ALU.subtract))
            step(dve.memset(tm[g64], 0.0))
            step(dve.tensor_tensor_scan(mm[g64], lf[g64], ig[g64], 0.0, ALU.add, ALU.max))
            step(dve.tensor_tensor_scan(bb[g64], lf[g64], tm[g64], 0.0, ALU.add, ALU.add))
            for d in range(2):
                r = slice(32 * d, 32 * d + 32)
                rev = (lambda v: v.rearrange("p (s n) -> p s n", s=2)[:, :, ::-1]) if d else (lambda v: v.rearrange("p (s n) -> p s n", s=2))
                nat = lambda v: v.rearrange("p (s n) -> p s n", s=2)
                step(dve.tensor_tensor(rev(rrow[r, :]), nat(bb[r]), nat(mm[r]), ALU.subtract))
                step(dve.tensor_tensor(rev(ce[r]), nat(ig[r]), nat(bb[r]), ALU.subtract))
                q = slice(64 + 32 * d, 96 + 32 * d)
                dve.tensor_scalar(rev(ce[q]), nat(mm[r]), -1.0, None, ALU.mult).then_inc(em_ready, 1)
            dve.wait_ge(gturn_done, 1)
            dve.tensor_copy(gcol[:, :, :].rearrange("p t c -> p (t c)"), ps[:, 7, :]).then_inc(gcol_ready, 1)
            dve.wait_ge(proj_kept, 16)
            dve.memset(V[:, :, :, DV:DVX], 1.0).then_inc(v_ones, 1)

            def diag(u):
                h, d = u // 2, u % 2
                dve.wait_ge(r_done, u + 1)
                if u >= 2:
                    dve.wait_ge(o_done, u - 1)
                for s in range(TILES):
                    ins = dve.scalar_tensor_tensor(out=W[:, u % 2, s, s, :], in0=ps[:, 3 + u % 2, P * s:P * s + P],
                                                   scalar=gcol[:, s, 32 * d + h:32 * d + h + 1], in1=masks[:, d, :],
                                                   op0=ALU.add, op1=ALU.add)
                ins.then_inc(d_done, 1)

            def prod(u):
                h, d = u // 2, u % 2
                dve.wait_ge(s_done, h + 1)
                dve.wait_ge(e_done, u + 1)
                for s in range(TILES):
                    for j, c in runs_of(PAIRS[d], s):
                        o = P * j if s < 2 else 256 * (s - 2) + P * (j - 2)
                        w = W[:, u % 2, s, j:j + c, :]
                        ins = dve.tensor_tensor(w, ps[:, min(s, 2), o:o + P * c].rearrange("p (j n) -> p j n", n=P), w,
                                                ALU.mult)
                ins.then_inc(p_done, 1)

            def keep(u):
                h, d = u // 2, u % 2
                dve.wait_ge(o_done, u + 1)
                den = ps[:, 5:7, 0:2 * DVX].rearrange("p b (j c) -> p b j c", j=2)[:, :, :, DV]
                e = gcol[:, :, 64 + 32 * d + h].rearrange("p (b j) -> p b j", b=2)
                r = att[:, d, :].rearrange("p (b j) -> p b j", b=2)
                step(dve.scalar_tensor_tensor(out=r, in0=den, scalar=-1.0, in1=e, op0=ALU.mult, op1=ALU.max))
                step(dve.tensor_tensor(r, den, r, ALU.max))
                dve.reciprocal(att[:, d, :], att[:, d, :]).then_inc(den_ready, 1)
                if d == 1:
                    dve.wait_ge(den_ready, u + 1)
                    dve.wait_ge(fin_act, h + 1)
                    for j in range(TILES):
                        ins = dve.scalar_tensor_tensor(out=H[:, j, h, :], in0=ps[:, 5 + j // 2, DVX * (j % 2):DVX * (j % 2) + DV],
                                                       scalar=att[:, d, j:j + 1], in1=H[:, j, h, :],
                                                       op0=ALU.mult, op1=ALU.add)
                    ins.then_inc(fin_dve, 1)

            dve.wait_ge(gcol_ready, 1)
            diag(0)
            for u in range(16):
                if u < 15:
                    diag(u + 1)
                prod(u)
                if u >= 1:
                    keep(u - 1)
            keep(15)

            dve.wait_ge(fin_dve, 8)
            for t in range(TILES):
                step(dve.tensor_tensor(sq, H[:, t], H[:, t], ALU.mult))
                dve.tensor_reduce(hs[:, t], sq, AX_X, ALU.add).then_inc(hss_ready, 1)
                dve.wait_ge(hss_ready, t + 1)
            for t in range(TILES):
                dve.wait_ge(hr_ready, t + 1)
                step(dve.tensor_tensor(H[:, t], H[:, t], hs[:, t].unsqueeze(2).to_broadcast([P, HEADS, DV]), ALU.mult))
                dve.wait_ge(og_ready, 4 + t + 1)
                dve.tensor_tensor(XN[:, t, :], XN[:, t, :], O[:, t, :], ALU.mult).then_inc(y_ready, 1)
            for g in range(8):
                t, b = g // 2, g % 2
                dve.wait_ge(yt_done, g + 1)
                dve.tensor_tensor(hT[:, 4 * b:4 * b + 4, P * t:P * t + P],
                                  ps[:, 5 + g % 3, :].rearrange("p (k n) -> p k n", k=4),
                                  ghead[:, 4 * b:4 * b + 4].unsqueeze(2).to_broadcast([P, 4, P]), ALU.mult
                                  ).then_inc(yt_kept, 1)

            def add_out(tiles, t0, n0):
                for g in range(2 * tiles):
                    cb, t = g // tiles, t0 + g % tiles
                    c = slice(512 * cb, 512 * cb + 512)
                    dve.wait_ge(out_done, n0 + g + 1)
                    if g:
                        dve.wait_ge(out_added, n0 + g)
                    step(dve.tensor_tensor(gtmp2, ps[:, g % 3, :], gate2[:, t // 2, c], ALU.mult))
                    dve.tensor_tensor(X[:, t, c], X[:, t, c], gtmp2, ALU.add).then_inc(out_added, 1)

            dve.wait_ge(g2_ready, 4)
            add_out(TILES, 0, 0)

            def route_dve(m, root):
                nt, t0, l = m.nt, m.tiles[0], m.l
                ns = nt // 2
                dve.wait_ge(m.gffn_in, m.was["gffn_in"] + 16)
                for b in range(2 * ns):
                    s, c = 2 - ns + b // 2, slice(512 * (b % 2), 512 * (b % 2) + 512)
                    dve.wait_ge(m.rows_done, m.was["rows_done"] + 2 * b + 1)
                    dve.scalar_tensor_tensor(out=ab[:, 0, s, c], in0=ps[:, 3, :], scalar=1.0, in1=gffn[:, c],
                                             op0=ALU.add, op1=ALU.mult).then_inc(m.scale_kept, 1)
                dve.wait_ge(m.scale_kept, m.was["scale_kept"] + 2 * ns)
                dve.wait_ge(m.shift_kept, m.was["shift_kept"] + 2 * ns)
                dve.wait_ge(rstd_ready, root)
                for i in range(nt):
                    t = t0 + i
                    step(dve.scalar_tensor_tensor(out=XN[:, t, :], in0=X[:, t, :], scalar=stat[:, 2, t:t + 1],
                                                  in1=ab[:, 0, t // 2, :], op0=ALU.mult, op1=ALU.mult))
                    dve.tensor_tensor(XN[:, t, :], XN[:, t, :], ab[:, 1, t // 2, :], ALU.add).then_inc(m.h_ready, 1)
                for i in range(nt):
                    dve.wait_ge(m.turned, m.was["turned"] + 2 * i + 2)
                    dve.tensor_copy(hT[:, 4:8, P * (t0 + i):P * (t0 + i) + P], ps[:, 6, :].rearrange("p (k n) -> p k n", k=4)
                                    ).then_inc(m.turn_kept_dve, 1)

                def row(n, w):
                    return sm[:, n, 0:w * nt].rearrange("p (t e) -> p t e", e=w)

                def bc(v, w):
                    return v.to_broadcast([P, nt, w])

                lg, sel, pick0, pick = row(0, NE), row(1, NE), row(2, NE), row(3, NE)
                tmp, r1, r2 = row(4, NE), row(5, 1), row(6, 1)
                dve.wait_ge(m.logits_done, m.was["logits_done"] + 1)
                L = ps[:, 7, 0:NE * nt].rearrange("p (t e) -> p t e", e=NE)
                step(dve.tensor_reduce(r1[:, :, 0], L, AX_X, ALU.max))
                dve.tensor_tensor(lg, L, bc(r1, NE), ALU.subtract).then_inc(m.shifted, 1)
                dve.wait_ge(m.expd, m.was["expd"] + 1)
                step(dve.tensor_reduce(r1[:, :, 0], lg, AX_X, ALU.add))
                step(dve.reciprocal(r2, r1))
                step(dve.tensor_tensor(lg, lg, bc(r2, NE), ALU.mult))
                step(dve.tensor_tensor(sel, lg, brt[:, :].unsqueeze(1).to_broadcast([P, nt, NE]), ALU.add))
                q = sm[:, 1, 0:NE * nt].rearrange("p (g a b) -> p g a b", a=2, b=2)
                hi = sm[:, 7, 0:8 * nt].rearrange("p (g a) -> p g a", a=2)
                lo = sm[:, 8, 0:8 * nt].rearrange("p (g a) -> p g a", a=2)
                t1, t2, t3 = (sm[:, x, 0:4 * nt] for x in (9, 10, 11))
                step(dve.tensor_tensor(hi, q[:, :, :, 0], q[:, :, :, 1], ALU.max))
                step(dve.tensor_tensor(lo, q[:, :, :, 0], q[:, :, :, 1], ALU.min))
                step(dve.tensor_tensor(t1, hi[:, :, 0], hi[:, :, 1], ALU.max))
                step(dve.tensor_tensor(t2, hi[:, :, 0], hi[:, :, 1], ALU.min))
                step(dve.tensor_tensor(t3, lo[:, :, 0], lo[:, :, 1], ALU.max))
                step(dve.tensor_tensor(t2, t2, t3, ALU.max))
                step(dve.tensor_tensor(t1, t1, t2, ALU.add))
                gs, eq, first = row(9, 4), row(10, 4), row(11, 4)
                step(dve.tensor_reduce(r1[:, :, 0], gs, AX_X, ALU.max))
                step(dve.tensor_tensor(eq, gs, bc(r1, 4), ALU.is_equal))
                step(dve.tensor_scalar(first[:, 0, :], iota16[:, 0:4], -1.0, 4.0, ALU.mult, ALU.add))
                step(dve.tensor_tensor(eq, eq, first[:, 0:1, :].to_broadcast([P, nt, 4]), ALU.mult))
                step(dve.tensor_reduce(r1[:, :, 0], eq, AX_X, ALU.max))
                step(dve.tensor_tensor(eq, eq, bc(r1, 4), ALU.is_equal))
                eq4 = sm[:, 10, 0:4 * nt].unsqueeze(2).to_broadcast([P, 4 * nt, 4])
                grp = lambda v: v.rearrange("p t (g f) -> p (t g) f", f=4)
                step(dve.tensor_tensor(grp(sel), grp(sel), eq4, ALU.mult))
                step(dve.tensor_scalar(eq, eq, -NEG, NEG, ALU.mult, ALU.add))
                step(dve.tensor_tensor(grp(sel), grp(sel), eq4, ALU.add))
                m8 = row(12, 8)
                i8 = sm[:, 13, 0:8 * nt].bitcast(U32).rearrange("p (t e) -> p t e", e=8)
                for i in range(nt):
                    step(dve.max(m8[:, i, :], sel[:, i, :]))
                    step(dve.max_index(i8[:, i, :], m8[:, i, :], sel[:, i, :]))
                ex = sm[:, 14, 0:2 * nt].rearrange("p (k t) -> p k t", k=2)
                step(dve.tensor_copy(ex.rearrange("p k t -> p t k"), i8[:, :, 0:2]))
                picks = [pick0, row(15, NE)]
                wt = m.weight.rearrange("p (k t) -> p k t", k=2)
                for k in range(2):
                    step(dve.tensor_tensor(picks[k], iota16[:, :].unsqueeze(1).to_broadcast([P, nt, NE]),
                                           ex[:, k, :].unsqueeze(2).to_broadcast([P, nt, NE]), ALU.is_equal))
                dve.tensor_tensor(pick, picks[0], picks[1], ALU.add).then_inc(m.picked, 1)
                for k in range(2):
                    step(dve.tensor_tensor(tmp, lg, picks[k], ALU.mult))
                    step(dve.tensor_reduce(wt[:, k, :], tmp, AX_X, ALU.add))
                step(dve.tensor_tensor(r1[:, :, 0], wt[:, 0, :], wt[:, 1, :], ALU.add))
                step(dve.reciprocal(r2, r1))
                step(dve.tensor_tensor(wt, wt, r2[:, :, 0].unsqueeze(1).to_broadcast([P, 2, nt]), ALU.mult))
                vt = m.value.rearrange("p (k t) -> p k t", k=2)
                step(dve.tensor_copy(vt[:, 0, :], tokf[:, 0:nt]))
                step(dve.tensor_scalar(vt[:, 1, :], tokf[:, 0:nt], float(m.T), None, ALU.add))
                dve.wait_ge(m.pos_done, m.was["pos_done"] + 1)
                pos = row(16, NE)
                step(dve.tensor_copy(sm[:, 16:18, :].rearrange("p a n -> p (a n)")[:, 0:NE * (nt + 1)], ps[:, 0, 0:NE * (nt + 1)]))
                pl = sm[:, 18, 0:2 * nt].rearrange("p (k t) -> p k t", k=2)
                for k in range(2):
                    step(dve.tensor_tensor(tmp, pos, picks[k], ALU.mult))
                    step(dve.tensor_reduce(pl[:, k, :], tmp, AX_X, ALU.add))
                dve.scalar_tensor_tensor(out=m.addr.rearrange("p (k t) -> p k t", k=2), in0=ex, scalar=float(CAP), in1=pl,
                                         op0=ALU.mult, op1=ALU.add).then_inc(m.addr_ready, 1)
                dve.wait_ge(m.list_turned, m.was["list_turned"] + 1)
                G = m.G
                v, ge = sm[:, 19, 0:G], sm[:, 20, 0:G]
                step(dve.tensor_copy(v, ps[:, 1, 0:G]))
                half_rows(v, ge, G, GIX[:, 0:G], SIX[:, 0:G], m.T, m.lists_ready)
                list_further(m, sm[0:1, 16:18, :].rearrange("p a n -> p (a n)")[:, NE * nt:NE * (nt + 1)])

            def half_rows(v, ge, G, gix, six, T, ready):
                step(dve.tensor_scalar(ge, v, float(T), float(T), ALU.is_ge, ALU.mult))
                step(dve.tensor_tensor(ge, v, ge, ALU.subtract))
                step(dve.tensor_scalar(ge, ge, float(T - 1), 2.0, ALU.min, ALU.mult))
                step(dve.tensor_scalar(gix, ge, half[:, 0:1], None, ALU.add))
                dve.tensor_scalar(six, v, 2.0, half[:, 0:1], ALU.mult, ALU.add).then_inc(ready, 1)

            def list_further(m, total):
                F, M = m.further, m.most
                place = iota16[0:1, 0:M]
                flat = lambda n, w: sm[0:1, n:n + 4, :].rearrange("p a n -> p (a n)")[:, 0:w]
                bounds, x, upto_e = sm[0:1, 4, 0:F], sm[0:1, 5, 0:NE], sm[0:1, 6, 0:NE]
                expert, row, before = sm[0:1, 7, 0:M], sm[0:1, 8, 0:M], sm[0:1, 9, 0:M]
                over = flat(10, NE * F).rearrange("p (e k) -> p e k", k=F)
                past = flat(21, M * NE).rearrange("p (o e) -> p o e", e=NE)
                step(dve.tensor_scalar(bounds, iota16[0:1, 0:F], float(PASS), float(PASS * m.subs), ALU.mult, ALU.add))
                step(dve.tensor_tensor(over, total.unsqueeze(2).to_broadcast([1, NE, F]),
                                       bounds.unsqueeze(1).to_broadcast([1, NE, F]), ALU.is_gt))
                step(dve.tensor_reduce(x, over, AX_X, ALU.add))
                step(dve.tensor_tensor_scan(upto_e, ones[0:1, 0:NE], x, 0.0, ALU.mult, ALU.add))
                step(dve.tensor_tensor(past, upto_e.unsqueeze(1).to_broadcast([1, M, NE]),
                                       place.unsqueeze(2).to_broadcast([1, M, NE]), ALU.is_le))
                step(dve.tensor_reduce(expert, past, AX_X, ALU.add))
                step(dve.tensor_tensor(past, past, x.unsqueeze(1).to_broadcast([1, M, NE]), ALU.mult))
                step(dve.tensor_reduce(before, past, AX_X, ALU.add))
                step(dve.tensor_scalar(expert, expert, float(NE - 1), None, ALU.min))
                step(dve.scalar_tensor_tensor(out=row, in0=expert, scalar=float(CAP // PASS), in1=place,
                                              op0=ALU.mult, op1=ALU.add))
                step(dve.tensor_tensor(row, row, before, ALU.subtract))
                step(dve.tensor_scalar(row, row, float(m.subs), float(NE * CAP // PASS - 1), ALU.add, ALU.min))
                step(dve.tensor_copy(more[0:1, 0:1], upto_e[:, NE - 1:NE]))
                step(dve.tensor_copy(more[0:1, 1:1 + M], expert))
                dve.tensor_copy(more[0:1, 16:16 + M], row).then_inc(m.more_ready, 1)

            def passes_dve(m):
                def keep_xt(g, par):
                    dve.wait_ge(m.tx_done, m.was["tx_done"] + g + 1)
                    if not isinstance(g, int) or g >= 2:
                        dve.wait_ge(m.h_done, m.was["h_done"] + g - 1)
                    dve.tensor_copy(XT[:, par, :, :].rearrange("p j n -> p (j n)"), ps[:, par, :]).then_inc(m.xt_ready, 1)

                def mul(g, par):
                    dve.wait_ge(m.silu_done, m.was["silu_done"] + g + 1)
                    if not isinstance(g, int) or g >= 2:
                        dve.wait_ge(m.tu_done, m.was["tu_done"] + g - 1)
                    dve.tensor_tensor(U[:, par, :], ps[:, 2 + par, 256:512], SG[:, par, :], ALU.mult).then_inc(m.u_ready, 1)

                def keep_ut(g, par):
                    dve.wait_ge(m.tu_done, m.was["tu_done"] + g + 1)
                    if not isinstance(g, int) or g >= 2:
                        dve.wait_ge(m.y_done, m.was["y_done"] + g - 1)
                    dve.tensor_copy(UT[:, par, :, :].rearrange("p c n -> p (c n)"), ps[:, 4 + par, 0:256]).then_inc(m.ut_ready, 1)

                def body(i, last):
                    for b in range(2):
                        g = i * 2 * m.subs + b * m.subs
                        if m.subs == 2:
                            keep_xt(g + 1, 1)
                            mul(g, 0)
                            keep_ut(g, 0)
                            mul(g + 1, 1)
                            keep_ut(g + 1, 1)
                            if not (last and b == 1):
                                keep_xt(g + 2, 0)
                        else:
                            mul(g, b)
                            if not (last and b == 1):
                                keep_xt(g + 1, 1 - b)
                            keep_ut(g, b)

                keep_xt(0, 0)
                body(0, False)
                with dve.Fori(1, NE // 2 - 1) as i:
                    body(i, False)
                body(NE // 2 - 1, True)

            def further_dve(m):
                dve.wait_ge(m.more_ready, m.was["more_ready"] + 1)
                count = dve.value_load(more[0:1, 0:1], min_val=0, max_val=m.most)
                with dve.Fori(0, m.most) as o:
                    with dve.If(count > o):
                        dve.wait_ge(m.further_pe, after(PE_STEPS, o, "column"))
                        v, ge = ov[:, 0:1], ov[:, 1:2]
                        dve.tensor_copy(v, ps[:, 1, 0:1]).then_inc(m.further_dve, 1)
                        dve.wait_ge(m.further_dve, after(DVE_STEPS, o, "v"))
                        dve.tensor_scalar(ge, v, float(m.T), float(m.T), ALU.is_ge, ALU.mult).then_inc(m.further_dve, 1)
                        dve.wait_ge(m.further_dve, after(DVE_STEPS, o, "second"))
                        dve.tensor_tensor(ge, v, ge, ALU.subtract).then_inc(m.further_dve, 1)
                        dve.wait_ge(m.further_dve, after(DVE_STEPS, o, "token"))
                        dve.tensor_scalar(ge, ge, float(m.T - 1), 2.0, ALU.min, ALU.mult).then_inc(m.further_dve, 1)
                        dve.wait_ge(m.further_dve, after(DVE_STEPS, o, "row"))
                        dve.tensor_scalar(ogi, ge, half[:, 0:1], None, ALU.add).then_inc(m.further_dve, 1)
                        dve.tensor_scalar(osi, v, 2.0, half[:, 0:1], ALU.mult, ALU.add).then_inc(m.further_dve, 1)
                        dve.wait_ge(m.further_pe, after(PE_STEPS, o, "turned"))
                        dve.tensor_copy(XT[:, 0, :, :].rearrange("p j n -> p (j n)"), ps[:, 0, :]).then_inc(m.further_dve, 1)
                        dve.wait_ge(m.further_act, after(ACT_STEPS, o, "silu"))
                        dve.tensor_tensor(U[:, 0, :], ps[:, 2, 256:512], SG[:, 0, :], ALU.mult).then_inc(m.further_dve, 1)
                        dve.wait_ge(m.further_pe, after(PE_STEPS, o, "u_turned"))
                        dve.tensor_copy(UT[:, 0, :, :].rearrange("p c n -> p (c n)"), ps[:, 4, 0:256]).then_inc(m.further_dve, 1)

            def combine_dve(m):
                dve.wait_ge(m.g5_kept, m.was["g5_kept"] + m.nt)
                for i in range(m.nt):
                    t = m.tiles[0] + i
                    y0, y1 = XN[:, 2 * (i % 2), :], XN[:, 2 * (i % 2) + 1, :]
                    dve.wait_ge(m.y_scaled, m.was["y_scaled"] + i + 1)
                    step(dve.scalar_tensor_tensor(out=y1, in0=y1, scalar=m.weight[:, m.nt + i:m.nt + i + 1], in1=y0,
                                                  op0=ALU.mult, op1=ALU.add))
                    step(dve.tensor_tensor(y1, y1, g5[:, t // 2, :], ALU.mult))
                    dve.tensor_tensor(X[:, t, :], X[:, t, :], y1, ALU.add).then_inc(m.added, 1)

            def conv(n):
                dve.wait_ge(xr_kept, n + 1)
                x = xpad[:, n % 2]
                y = XC[:, n, :].rearrange("p (s n) -> p s n", s=2)
                step(dve.tensor_scalar(y, x[:, :, 0:256], convw[:, 0, n:n + 1], convb[:, n:n + 1], ALU.mult, ALU.add))
                for j in range(1, 4):
                    ins = dve.scalar_tensor_tensor(out=y, in0=x[:, :, j:j + 256], scalar=convw[:, j, n:n + 1], in1=y,
                                                   op0=ALU.mult, op1=ALU.add)
                    if j < 3:
                        step(ins)
                ins.then_inc(conv_done, 1)

            def scans(n):
                for d in range(2):
                    dve.wait_ge(rg_tanh, 2 * n + d + 1)
                    dve.scalar_tensor_tensor(out=RB[:, d, 2, :], in0=RB[:, d, 0, :], scalar=1.0, in1=RB[:, d, 2, :],
                                             op0=ALU.add, op1=ALU.mult).then_inc(rg_q, 1)
                for d in range(2):
                    ti, sq_, dec = RB[:, d, 1, :], RB[:, d, 2, :], RB[:, d, 3, :]
                    step(dve.scalar_tensor_tensor(out=ti, in0=ti, scalar=1.0, in1=XC[:, n, :], op0=ALU.add, op1=ALU.mult))
                    dve.wait_ge(rg_sqrt, 2 * n + d + 1)
                    step(dve.tensor_tensor(ti, ti, sq_, ALU.mult))
                    h = hfb[:, d, :]
                    dve.wait_ge(rg_q, 2 * n + 2)
                    if d == 0:
                        dve.tensor_tensor_scan(h, dec, ti, 0.0, ALU.mult, ALU.add).then_inc(rg_scan, 1)
                    else:
                        step(dve.tensor_tensor_scan(h[:, 0:256][:, ::-1], dec[:, 0:256][:, ::-1], ti[:, 0:256][:, ::-1],
                                                    0.0, ALU.mult, ALU.add))
                        dve.tensor_tensor_scan(h[:, 256:512][:, ::-1], dec[:, 256:512][:, ::-1], ti[:, 256:512][:, ::-1],
                                               h[:, 0:1], ALU.mult, ALU.add).then_inc(rg_scan, 1)
                dve.wait_ge(rg_scan, 2 * n + 2)
                step(dve.tensor_tensor(YT[:, n, :], hfb[:, 0, 256:512], hfb[:, 1, 256:512], ALU.add))
                dve.wait_ge(yb_kept, n + 1)
                ins = dve.tensor_tensor(YT[:, n, :], YT[:, n, :], YB[:, n, :], ALU.mult)
                if n == 7:
                    ins.then_inc(y_ready, 1)

            def rglru_params():
                dve.wait_ge(rg_in, 80)
                lm = lam[:, :, :].rearrange("p d k -> p (d k)")
                e, u, ln, z = (lt[:, i, :] for i in range(4))
                dve.scalar_tensor_tensor(out=e, in0=lm, scalar=-1.0, in1=lm, op0=ALU.mult, op1=ALU.min).then_inc(lam_u, 1)
                dve.wait_ge(lam_exp, 1)
                dve.tensor_scalar(u, e, 1.0, None, ALU.add).then_inc(lam_u, 1)
                dve.wait_ge(lam_ln, 1)
                step(dve.tensor_scalar(u, u, 1.0, None, ALU.subtract))
                step(dve.tensor_scalar(z, u, 0.0, None, ALU.is_equal))
                step(dve.tensor_tensor(ln, ln, z, ALU.add))
                step(dve.tensor_tensor(u, u, z, ALU.add))
                step(dve.reciprocal(u, u))
                step(dve.tensor_tensor(ln, ln, u, ALU.mult))
                step(dve.tensor_tensor(ln, ln, e, ALU.mult))
                step(dve.tensor_scalar(z, lm, -1.0, 0.0, ALU.mult, ALU.max))
                step(dve.tensor_tensor(ln, ln, z, ALU.add))
                step(dve.tensor_scalar(spl[:, :, :].rearrange("p d k -> p (d k)"), ln, 0.5 * RGLRU_C, None, ALU.mult))
                step(dve.tensor_scalar(spn[:, :, :].rearrange("p d k -> p (d k)"), ln, -0.5 * RGLRU_C, None, ALU.mult))
                rb = rbias[:, :, :, :].rearrange("p d n e -> p (d n e)")
                dve.tensor_scalar(rb, rb, 0.5, None, ALU.mult).then_inc(lam_ready, 1)

            route_dve(moes[0], 2)
            passes_dve(moes[0])
            further_dve(moes[0])
            combine_dve(moes[0])
            modulation(1)
            norm_keep(1)
            rglru_params()
            dve.memset(xpad[:, :, :, :], 0.0).then_inc(pads, 1)
            for what, n in RG_ORDER:
                if what == "x":
                    conv(n)
                elif what == "g":
                    scans(n)
            dve.wait_ge(g2_ready, 6)
            add_out(2, 2, 8)
            route_dve(moes[1], 4)
            passes_dve(moes[1])
            further_dve(moes[1])
            combine_dve(moes[1])
            dve.wait_ge(gfin_in, 16)
            dve.wait_ge(rstd_ready, 5)
            for t in (2, 3):
                dve.scalar_tensor_tensor(out=XN[:, t, :], in0=X[:, t, :], scalar=stat[:, 2, t:t + 1], in1=gffn,
                                         op0=ALU.mult, op1=ALU.mult).then_inc(fin_ready, 1)


def position_table(n_tokens, dim, grid_w=64, base=10000.0):
    rows = n_tokens // grid_w
    r, col = np.meshgrid(np.arange(rows, dtype=np.float32), np.arange(grid_w, dtype=np.float32), indexing="ij")
    quarter = dim // 4
    freqs = np.exp(np.float32(-np.log(base)) * np.arange(quarter, dtype=np.float32) / np.float32(quarter))
    enc = lambda p: np.concatenate([np.sin(p.reshape(-1, 1) * freqs), np.cos(p.reshape(-1, 1) * freqs)], -1)
    return np.concatenate([enc(r), enc(col)], -1).astype(np.float32)


INPUTS = ["x", "c", "ctx", "c_ctx", "w_ada", "b_ada", "g_mix", "g_ffn", "g_final", "m_w_in", "m_b_gate", "m_g_head",
          "m_w_out", "r_w_in", "r_conv_w", "r_conv_b", "r_w_gate", "r_b_gate", "r_lam", "r_w_out", "w_router",
          "b_router", "e_w1", "e_w3", "e_w2"]


def kernel(**inputs):
    import concourse.bacc as bacc
    from concourse.bass_utils import run_bass_kernel_spmd

    nc = bacc.Bacc("TRN2", target_bir_lowering=False, num_devices=1)
    arrays = {name: np.ascontiguousarray(inputs[name]) for name in INPUTS}
    arrays["pos"] = position_table(SEQ, D)
    args = {name: nc.dram_tensor("in_" + name, v.shape, F32, kind="ExternalInput").ap() for name, v in arrays.items()}
    out = nc.dram_tensor("out", (1, SEQ, D), F32, kind="ExternalOutput")
    build(nc, args, out.ap())
    r = run_bass_kernel_spmd(nc, [{"in_" + name: v for name, v in arrays.items()}], core_ids=[0])
    return r.results[0]["out"]
```

```python
from contextlib import ExitStack

import numpy as np

import concourse.bass as bass
from concourse import mybir

F32 = mybir.dt.float32
U32 = mybir.dt.uint32
I32 = mybir.dt.int32
ALU = mybir.AluOpType
ACT = mybir.ActivationFunctionType
AX_X = mybir.AxisListType.X

P = 128
D = 1024
KD = D // P
SEQ = 256
TILES = 4
T_ALL = TILES * P
HEADS = 8
DQK = 64
DV = 128
DVX = DV + 1
NE = 16
DE = 512
EPS = 1e-6
NEG = -1e30
RGLRU_C = 8.0
SLOTS = 6
CHUNK = 4096
PASS = 64
CAP = 512
PAD = 1.0e6

ADA_CHUNKS = 12
MIX0_STREAM = ([("ada0", j) for j in range(4)] + [("in0", 0)] + [("ada0", j) for j in range(4, 8)] + [("in0", 1)]
               + [("ada0", j) for j in range(8, 12)] + [("in0", 2), ("in0", 3)]
               + [("ada1", j) for j in range(12)] + [("in0", 4), ("in0", 5), ("out0", 0), ("out0", 1)])
MIX1_STREAM = [("in1", j) for j in range(5)] + [("out1", 0), ("out1", 1)]
N_MOE0 = len(MIX0_STREAM)
N_MIX1 = N_MOE0 + 3 * NE
N_MOE1 = N_MIX1 + len(MIX1_STREAM)
CHUNK_NO = {name: n for n, name in enumerate(MIX0_STREAM)}
CHUNK_NO.update({name: N_MIX1 + n for n, name in enumerate(MIX1_STREAM)})
CHUNK_NAME = {n: name for name, n in CHUNK_NO.items()}


def fwd_keys(j):
    return list(range(j + 1))


def bwd_keys(j):
    return [[0, 1], [1], [0, 1, 2, 3], [0, 1, 3]][j]


PAIRS = [[(s, j) for s in range(TILES) for j in range(TILES) if s in keys(j)] for keys in (fwd_keys, bwd_keys)]


def runs_of(pairs, s):
    js = [j for (a, j) in pairs if a == s]
    out = []
    for j in js:
        if out and out[-1][0] + out[-1][1] == j:
            out[-1][1] += 1
        else:
            out.append([j, 1])
    return [tuple(r) for r in out]


def build(nc, a, out):
    ctx = ExitStack()
    with ctx:
        def sb(name, shape, dt=F32):
            return ctx.enter_context(nc.sbuf_tensor(name, shape, dt))

        def sem(name):
            return ctx.enter_context(nc.semaphore(name))

        ctx.enter_context(nc.allow_non_contiguous_dma("columns of small vectors"))

        ps = ctx.enter_context(nc.psum_tensor("ps", [P, 8, 512], F32))
        ring = sb("ring", [P, SLOTS, CHUNK])
        X = sb("X", [P, TILES, D])
        hT = sb("hT", [P, KD, T_ALL])
        XN = sb("XN", [P, TILES, D])
        QK = sb("QK", [P, 8, T_ALL])
        VR = sb("VR", [P, TILES * HEADS * DVX])
        WR = sb("WR", [P, 2 * 16 * P])
        modr = sb("modr", [P, 3, 512])
        ident = sb("ident", [P, P])
        masks = sb("masks", [P, 2, P])
        triu = sb("triu", [P, P])
        ones = sb("ones", [P, P])
        wrt = sb("wrt", [P, KD, NE])
        gcol = sb("gcol", [P, TILES, P])
        rrow = sb("rrow", [64, T_ALL])
        silu_c = sb("silu_c", [P, KD, 2, 16])
        cvec = sb("cvec", [P, 2, KD])
        acol = sb("acol", [P, 2, KD])
        bcol = sb("bcol", [P, 2, KD])
        gmix = sb("gmix", [P, 2, KD])
        ghead = sb("ghead", [P, KD])
        bgate = sb("bgate", [P, 1])
        brt = sb("brt", [P, NE])
        iota16i = sb("iota16i", [P, NE], I32)
        iota16 = sb("iota16", [P, NE])
        toki = sb("toki", [P, TILES], I32)
        tokf = sb("tokf", [P, TILES])
        half = sb("half", [P, 1])
        mhalf = sb("mhalf", [P, HEADS])
        stat = sb("stat", [P, 8, TILES])
        att = sb("att", [P, 2, TILES])

        V = VR[:, :].rearrange("p (t h c) -> p t h c", t=TILES, h=HEADS)
        bada = WR[:, 2560:4096].rearrange("p (g n) -> p g n", g=3)
        wg = VR[:, 1536:2560].rearrange("p (k t d r) -> p k t d r", k=KD, t=2, d=2)
        H = XN[:, :, :].rearrange("p t (h v) -> p t h v", h=HEADS)
        qT, kT = QK[:, 0:4, :], QK[:, 4:8, :]
        O = QK[:, :, :].rearrange("p a b -> p (a b)").rearrange("p (t n) -> p t n", t=TILES)
        W = WR[:, :].rearrange("p (u s j n) -> p u s j n", u=2, s=TILES, j=TILES)
        gtmp = WR[:, 0:3072].rearrange("p (a n) -> p a n", a=6)
        gate2 = WR[:, 0:2048].rearrange("p (s n) -> p s n", s=2)
        gtmp2 = WR[:, 2048:2560]
        sq = WR[:, 2560:3584].rearrange("p (h v) -> p h v", h=HEADS)
        hs = WR[:, 3584:3616].rearrange("p (t h) -> p t h", t=TILES)
        hss_ready, hr_ready = sem("head_squares"), sem("head_roots")

        ld = [sem(f"chunk_loaded{i}") for i in range(SLOTS)]
        x_in, cv_in, pos_in = sem("x_in"), sem("cv_in"), sem("pos_in")
        bada_in, small_in = sem("bada_in"), sem("small_in")
        wg_zero, wg_in = sem("wg_zero"), sem("wg_in")
        bg_zero, bada_zero = sem("bg_zero"), sem("bada_zero")
        consts, pool_step = sem("consts"), sem("pool_step")
        dve_step, act_step = sem("dve_step"), sem("act_step")
        silu_ready, ada_done, modr_ready = sem("silu_ready"), sem("ada_done"), sem("modr_ready")
        ada_part = sem("ada_part")
        modcol_done, cols_ready = sem("modcol_done"), sem("cols_ready")
        x_ready, ss_ready, rstd_ready, xn_ready = sem("x_ready"), sem("ss_ready"), sem("rstd_ready"), sem("xn_ready")
        nt_done, nt_act, nt_dve = sem("norm_turned"), sem("norm_kept_act"), sem("norm_kept_dve")
        gate_done, proj_done, proj_kept = sem("gate_done"), sem("proj_done"), sem("proj_kept")
        gates_ready, gturn_done, gcol_ready = sem("gates_ready"), sem("gturn_done"), sem("gcol_ready")
        v_ones, lsig_ready, lsig_kept, em_ready = sem("v_ones"), sem("lsig_ready"), sem("lsig_kept"), sem("em_ready")
        s_done, r_done, d_done, e_done, p_done, o_done = (
            sem("att_scores"), sem("att_rows"), sem("att_diag"), sem("att_exp"), sem("att_prod"), sem("att_out"))
        den_ready, fin_act, fin_dve = sem("att_den"), sem("att_kept_act"), sem("att_kept_dve")
        oproj_done, og_ready = sem("oproj_done"), sem("ogate_ready")
        g2_done, g2_ready = sem("gate2_done"), sem("gate2_ready")
        y_ready, yt_done, yt_kept = sem("mix_ready"), sem("mix_turned"), sem("mix_kept")
        out_done, out_added = sem("out_done"), sem("out_added")
        stored = sem("stored")

        table_ready, pool_held, sp_held, rg_in = sem("table_ready"), sem("pool_held"), sem("sp_held"), sem("rg_in")

        g5 = QK[:, 0:4, :].rearrange("p a b -> p (a b)").rearrange("p (s n) -> p s n", s=2)
        gffn = WR[:, 2560:2560 + D]
        XG = VR[:, 0:1024].rearrange("p (a n) -> p a n", a=2)
        XT = VR[:, 1024:2048].rearrange("p (a j n) -> p a j n", a=2, j=4)
        YS = VR[:, 2048:3072].rearrange("p (a n) -> p a n", a=2)
        SG = VR[:, 3072:3584].rearrange("p (a n) -> p a n", a=2)
        U = VR[:, 3584:4096].rearrange("p (a n) -> p a n", a=2)
        UT = WR[:, 1024:1536].rearrange("p (a c n) -> p a c n", a=2, c=2)
        sm = WR[:, 1536:4096].rearrange("p (a n) -> p a n", n=64)
        GIX = sm[:, 36, 0:32].bitcast(U32)
        SIX = sm[:, 36, 32:64].bitcast(U32)
        gi = sm[:, 37, 0:2].bitcast(U32)
        si = sm[:, 37, 2:4].bitcast(U32)
        LST = sm[:, 38:40, :].rearrange("p a n -> p (a n)")
        pad = VR[:, 2560:2624]
        more = sb("more", [1, 32], I32)
        orow = sm[0:1, 33:35, :].rearrange("p a n -> p (a n)")
        ov = sm[:, 35, 0:8]
        ogi, osi = sm[:, 35, 8:9].bitcast(U32), sm[:, 35, 9:10].bitcast(U32)

        block = ctx.enter_context(nc.Block())

        XC = XN[:, :, :].rearrange("p a b -> p (a b)").rearrange("p (n t) -> p n t", n=8)
        YB = QK[:, 0:4, :].rearrange("p a b -> p (a b)").rearrange("p (n t) -> p n t", n=8)
        YT = QK[:, 4:8, :].rearrange("p a b -> p (a b)").rearrange("p (n t) -> p n t", n=8)
        RB = VR[:, 0:4096].rearrange("p (d a n) -> p d a n", d=2, a=4)
        xpad = WR[:, 2560:3600].rearrange("p (u s n) -> p u s n", u=2, s=2)
        hfb = WR[:, 0:1024].rearrange("p (d n) -> p d n", d=2)
        convw, convb = sb("convw", [P, 4, KD]), sb("convb", [P, KD])
        rbias, lam = sb("rbias", [P, 2, KD, 2]), sb("lam", [P, 2, KD])
        spl, spn, lt = sb("spl", [P, 2, KD]), sb("spn", [P, 2, KD]), sb("lt", [P, 4, 2 * KD])
        xr_done, yb_done, rg_done = sem("xr_done"), sem("yb_done"), sem("rg_done")
        xr_kept, yb_kept, conv_done, pads = sem("xr_kept"), sem("yb_kept"), sem("conv_done"), sem("pads")
        lam_exp, lam_u, lam_ln, lam_ready = sem("lam_exp"), sem("lam_u"), sem("lam_ln"), sem("lam_ready")
        rg_tanh, rg_q, rg_sqrt, rg_scan = sem("rg_tanh"), sem("rg_q"), sem("rg_sqrt"), sem("rg_scan")
        gfin_in, fin_ready = sem("gfin_in"), sem("fin_ready")
        RG_ORDER = [("x", 0)] + [(w, n) for m in range(8) for w, n in (("x", m + 1), ("g", m), ("y", m)) if n < 8]

        MOE_SIGNALS = dict(
            gffn_in=lambda m: 16, rows_done=lambda m: 2 * m.nt, scale_kept=lambda m: m.nt, shift_kept=lambda m: m.nt,
            h_ready=lambda m: m.nt, rows_stored=lambda m: 16 * m.nt, turned=lambda m: 2 * m.nt,
            turn_kept_act=lambda m: m.nt, turn_kept_dve=lambda m: m.nt, logits_done=lambda m: 1,
            shifted=lambda m: 1, expd=lambda m: 1, picked=lambda m: 1, pos_done=lambda m: 1, addr_ready=lambda m: 1,
            filled=lambda m: 32 * m.nt, list_in=lambda m: 32 * m.subs, list_turned=lambda m: 1,
            lists_ready=lambda m: 1, gi_ready=lambda m: m.G, si_ready=lambda m: m.G, tx_done=lambda m: m.G,
            xt_ready=lambda m: m.G, half_done=lambda m: NE, h_done=lambda m: m.G, silu_done=lambda m: m.G,
            u_ready=lambda m: m.G, tu_done=lambda m: m.G, ut_ready=lambda m: m.G, y_done=lambda m: m.G,
            ys_ready=lambda m: m.G, g5_done=lambda m: m.nt, g5_kept=lambda m: m.nt, y_in=lambda m: 32,
            y_scaled=lambda m: m.nt, added=lambda m: m.nt, more_ready=lambda m: 1, passes_over=lambda m: 1, gathered=lambda m: 8 * m.G, scattered=lambda m: 8 * m.G)
        SEVERAL = dict(gathered=2, scattered=2, y_in=TILES)
        moe_sems = {name: [sem(f"{name}{i}") for i in range(SEVERAL[name])] if name in SEVERAL else sem(name)
                    for name in MOE_SIGNALS}

        class Moe:
            def __init__(self, l, tiles, subs, base):
                self.l, self.tiles, self.subs, self.base = l, tiles, subs, base
                self.nt = len(tiles)
                self.T = P * self.nt
                self.norms = (4, 12)[l]
                self.outs = (0, 8)[l]
                self.G = NE * subs
                self.hrows = nc.dram_tensor(f"hrows{l}", [self.T, D], F32, kind="Internal").ap()
                self.yrows = nc.dram_tensor(f"yrows{l}", [2 * self.T, D], F32, kind="Internal").ap()
                self.table = nc.dram_tensor(f"table{l}", [NE * CAP, 1], F32, kind="Internal").ap()
                self.hhalf = self.hrows.rearrange("t (h n) -> (t h) n", h=2)
                self.yhalf = self.yrows.rearrange("t (h n) -> (t h) n", h=2)
                self.was = {name: (per(moes[0]) if l else 0) for name, per in MOE_SIGNALS.items()}
                self.gffn_in = moe_sems["gffn_in"]
                self.rows_done = moe_sems["rows_done"]
                self.scale_kept = moe_sems["scale_kept"]
                self.shift_kept = moe_sems["shift_kept"]
                self.h_ready = moe_sems["h_ready"]
                self.rows_stored = moe_sems["rows_stored"]
                self.turned = moe_sems["turned"]
                self.turn_kept_act = moe_sems["turn_kept_act"]
                self.turn_kept_dve = moe_sems["turn_kept_dve"]
                self.logits_done = moe_sems["logits_done"]
                self.shifted = moe_sems["shifted"]
                self.expd = moe_sems["expd"]
                self.picked = moe_sems["picked"]
                self.pos_done = moe_sems["pos_done"]
                self.addr_ready = moe_sems["addr_ready"]
                self.filled = moe_sems["filled"]
                self.list_in = moe_sems["list_in"]
                self.list_turned = moe_sems["list_turned"]
                self.lists_ready = moe_sems["lists_ready"]
                self.gi_ready = moe_sems["gi_ready"]
                self.si_ready = moe_sems["si_ready"]
                self.tx_done = moe_sems["tx_done"]
                self.xt_ready = moe_sems["xt_ready"]
                self.half_done = moe_sems["half_done"]
                self.h_done = moe_sems["h_done"]
                self.silu_done = moe_sems["silu_done"]
                self.u_ready = moe_sems["u_ready"]
                self.tu_done = moe_sems["tu_done"]
                self.ut_ready = moe_sems["ut_ready"]
                self.y_done = moe_sems["y_done"]
                self.ys_ready = moe_sems["ys_ready"]
                self.g5_done = moe_sems["g5_done"]
                self.g5_kept = moe_sems["g5_kept"]
                self.y_in = moe_sems["y_in"]
                self.y_scaled = moe_sems["y_scaled"]
                self.added = moe_sems["added"]
                self.more_ready = moe_sems["more_ready"]
                self.passes_over = moe_sems["passes_over"]
                self.gathered = moe_sems["gathered"]
                self.scattered = moe_sems["scattered"]

                (self.further_pe, self.further_act, self.further_dve, self.further_dma, self.further_loaded) = (
                    [sem(f"{name}{l}") for name in FURTHER_SIGNALS])
                self.further = self.T // PASS - subs
                self.most = max(min(n * self.further, (2 * self.T - n * (PASS * subs - PASS + 1)) // PASS)
                                for n in range(1, NE + 1))
                self.ab = QK[:, 0:4 * self.nt // 2, :].rearrange("p a b -> p (a b)").rearrange(
                    "p (v s n) -> p v s n", v=2, s=self.nt // 2)
                self.yin = [(XN[:, 2 * i, :], XN[:, 2 * i + 1, :]) if i < 2 else
                            (VR[:, 2048 * (i - 2):2048 * (i - 2) + D], VR[:, 2048 * (i - 2) + D:2048 * (i - 2) + 2 * D])
                            for i in range(self.nt)]
                self.addr = sm[:, 30, 0:2 * self.nt].bitcast(U32)
                self.value = sm[:, 31, 0:2 * self.nt]
                self.weight = sm[:, 32, 0:2 * self.nt]

        FURTHER_SIGNALS = ("further_pe", "further_act", "further_dve", "further_dma", "further_loaded")
        PE_STEPS = ("column", "turned", "up", "u_turned", "down")
        ACT_STEPS = ("silu", "y_kept")
        DVE_STEPS = ("v", "second", "token", "row", "gather_index", "scatter_index", "xt", "u", "ut")

        def after(steps, o, name):
            return len(steps) * o + steps.index(name) + 1

        moes = []
        moes.append(Moe(0, [0, 1, 2, 3], 2, N_MOE0))
        moes.append(Moe(1, [2, 3], 1, N_MOE1))
        def slot(n):
            return ring[:, n % SLOTS, :]

        def cols_of(w, n, cb):
            v = w.rearrange("(k p) n -> p k n", p=P)
            d = slot(n).rearrange("p (k n) -> p k n", k=KD)
            return [(d[:, 4 * h:4 * h + 4, :], v[:, 4 * h:4 * h + 4, 512 * cb:512 * cb + 512]) for h in range(2)]

        def ada_of(l, n, j):
            g, kk = j // 4, j % 4
            v = a["w_ada"][l].rearrange("(k p) n -> p k n", p=P)
            d = slot(n).rearrange("p (k n) -> p k n", k=2)
            return [(d[:, h, :], v[:, 2 * kk + h, 2048 * g:2048 * g + 2048]) for h in range(2)]

        def expert_of(l, e, n, part):
            if part < 2:
                d = slot(n).rearrange("p (k w n) -> p k w n", k=4, w=2)
                return [(d[:, :, w, :], a[name][l, e].rearrange("(k p) n -> p k n", p=P)[:, 4 * part:4 * part + 4, :])
                        for w, name in enumerate(("e_w1", "e_w3"))]
            d = slot(n).rearrange("p (c n) -> p c n", c=4)
            v = a["e_w2"][l, e].rearrange("(c p) n -> p c n", p=P)
            return [(d[:, 2 * h:2 * h + 2, :], v[:, 2 * h:2 * h + 2, :]) for h in range(2)]

        m_in, r_in = a["m_w_in"][0], a["r_w_in"][0]
        r_gate = a["r_w_gate"][0].rearrange("d n p e -> p d n e")

        def used(n):
            if n in CHUNK_NAME:
                kind, j = CHUNK_NAME[n]
                if kind in ("ada0", "ada1"):
                    l, g, kk = int(kind[3]), j // 4, j % 4
                    return (ada_done, 3 * l + g + 1) if kk == 3 else (ada_part, 9 * l + 3 * g + kk + 1)
                if kind == "in0":
                    return (proj_done, 4 * j + 4) if j < 4 else (oproj_done, 4 * (j - 4) + 4)
                if kind == "out0":
                    return out_done, 2 * TILES - 1 + j
                if kind == "in1":
                    return [(xr_done, 4), (yb_done, 4), (rg_done, 16), (xr_done, 8), (yb_done, 8)][j]
                return out_done, 3 * TILES - 1 + j
            for m in moes:
                if m.base <= n < m.base + 3 * NE:
                    e, part = (n - m.base) // 3, (n - m.base) % 3
                    return [(m.half_done, m.was["half_done"] + e + 1), (m.h_done, m.was["h_done"] + m.subs * (e + 1)),
                            (m.y_done, m.was["y_done"] + m.subs * (e + 1))][part]
            raise ValueError(n)

        @block.sync
        def _(sp):
            def load(n, parts):
                if n >= SLOTS:
                    sp.wait_ge(*used(n - SLOTS))
                for dst, src in parts:
                    sp.dma_start(dst, src).then_inc(ld[n % SLOTS], 16)

            def load_named(names):
                for kind, j in names:
                    n = CHUNK_NO[kind, j]
                    if kind in ("ada0", "ada1"):
                        load(n, ada_of(int(kind[3]), n, j))
                    elif kind == "in0":
                        load(n, cols_of(m_in, n, j))
                    elif kind == "in1" and j == 2:
                        d = slot(n).rearrange("p (d n e) -> p d n e", d=2, n=8)
                        load(n, [(d[:, i], r_gate[:, i]) for i in range(2)])
                    elif kind == "in1":
                        load(n, cols_of(r_in, n, {0: 2, 1: 0, 3: 3, 4: 1}[j]))
                    else:
                        load(n, cols_of(a["m_w_out" if kind == "out0" else "r_w_out"][0], n, j))

            for t in range(TILES):
                src = a["ctx"][0] if t < 2 else a["x"][0]
                sp.dma_start(X[:, t, :], src[P * (t % 2):P * (t % 2) + P, :]).then_inc(x_in, 16)
            for t in range(2):
                sp.dma_start(XN[:, 2 + t, :], a["pos"][P * t:P * t + P, :]).then_inc(pos_in, 16)
            load_named(MIX0_STREAM)

            def experts(m):
                for n in range(m.base, m.base + 6):
                    e, part = (n - m.base) // 3, (n - m.base) % 3
                    load(n, expert_of(m.l, e, n, part))
                with sp.Fori(1, NE // 2) as i:
                    for j in range(6):
                        b, part = j // 3, j % 3
                        k = 2 * (i - 1) + b + 1
                        if part == 0:
                            sp.wait_ge(m.half_done, m.was["half_done"] + k)
                        elif part == 1:
                            sp.wait_ge(m.h_done, m.was["h_done"] + m.subs * k)
                        else:
                            sp.wait_ge(m.y_done, m.was["y_done"] + m.subs * k)
                        for dst, src in expert_of(m.l, 2 * i + b, m.base + j, part):
                            sp.dma_start(dst, src).then_inc(ld[(m.base + j) % SLOTS], 16)

            def experts_again(m):
                sp.wait_ge(m.more_ready, m.was["more_ready"] + 1)
                count = sp.value_load(more[0:1, 0:1], min_val=0, max_val=m.most)
                with sp.If(count > 0):
                    with sp.Fori(0, m.most) as o:
                        with sp.If(count > o):
                            sp.wait_ge(m.h_done, m.was["h_done"] + m.G)
                            sp.wait_ge(m.y_done, m.was["y_done"] + m.G)
                            e = sp.value_load(more[0:1, bass.ds(o + 1, 1)], min_val=0, max_val=NE - 1)
                            for part in range(3):
                                for dst, src in expert_of(m.l, e, part, part):
                                    sp.dma_start(dst, src).then_inc(m.further_loaded, 16)
                            sp.wait_ge(m.further_pe, after(PE_STEPS, o, "down"))
                            sp.sem_inc(sp_held, 1)
            experts(moes[0])
            experts_again(moes[0])
            load_named(MIX1_STREAM)
            experts(moes[1])
            experts_again(moes[1])
            for t in range(2):
                sp.wait_ge(stored, 16 * (t + 1))

        def use(pe, n, i=0):
            pe.wait_ge(ld[n % SLOTS], 32 * (n // SLOTS + 1) + 32 * i)

        @block.gpsimd
        def _(pool):
            steps = [0]

            def step(ins):
                steps[0] += 1
                ins.then_inc(pool_step, 1)
                pool.wait_ge(pool_step, steps[0])

            pool.memset(bada, 0.0).then_inc(bada_zero, 1)
            step(pool.memset(wg, 0.0))
            pool.memset(bgate[:, :], 0.0).then_inc(bg_zero, 1)
            step(pool.memset(ident[:, :], 0.0))
            step(pool.affine_select(out=ident[:, :], in_=ident[:, :], compare_op=ALU.not_equal, fill=1.0,
                                    base=0, pattern=[[-1, P]], channel_multiplier=1))
            step(pool.memset(masks[:, :, :], 0.0))
            step(pool.affine_select(out=masks[:, 0, :], in_=masks[:, 0, :], compare_op=ALU.is_ge, fill=NEG,
                                    base=0, pattern=[[1, P]], channel_multiplier=-1))
            step(pool.affine_select(out=masks[:, 1, :], in_=masks[:, 1, :], compare_op=ALU.is_ge, fill=NEG,
                                    base=0, pattern=[[-1, P]], channel_multiplier=1))
            step(pool.memset(ones[:, :], 1.0))
            step(pool.affine_select(out=triu[:, :], in_=ones[:, :], compare_op=ALU.is_ge, fill=0.0,
                                    base=-1, pattern=[[1, P]], channel_multiplier=-1))
            step(pool.iota(iota16i[:, :], pattern=[[1, NE]], base=0, channel_multiplier=0))
            step(pool.iota(toki[:, :], pattern=[[P, TILES]], base=0, channel_multiplier=1))
            step(pool.memset(pad, PAD))
            for m in moes:
                pool.dma_start(m.table.rearrange("(p n) o -> p (n o)", p=P), pad).then_inc(table_ready, 16)
            pool.wait_ge(table_ready, 32)
            pool.memset(mhalf[:, :], -0.5).then_inc(consts, 1)
            pool.wait_ge(consts, 1)

            def rstd(n, tiles):
                for i, t in enumerate(tiles):
                    pool.wait_ge(ss_ready, n + i + 1)
                    step(pool.tensor_scalar(stat[:, 1, t:t + 1], stat[:, 0, t:t + 1], 1.0 / D, EPS, ALU.mult, ALU.add))
                    pool.tensor_tensor(stat[:, 2, t:t + 1], stat[:, 1, t:t + 1], mhalf[:, t:t + 1], ALU.pow
                                       ).then_inc(rstd_ready, 1)

            def held():
                pool.sem_inc(pool_held, 1)

            def gather(m, g, par):
                if not isinstance(g, int) or g >= 2:
                    pool.wait_ge(m.tx_done, m.was["tx_done"] + g - 1)
                    held()
                pool.tensor_copy(gi[:, par:par + 1], GIX[:, bass.ds(g, 1)]).then_inc(m.gi_ready, 1)
                pool.wait_ge(m.gi_ready, m.was["gi_ready"] + g + 1)
                held()
                pool.indirect_dma_start(XG[:, par, :], None, m.hhalf,
                                        bass.IndirectOffsetOnAxis(ap=gi[:, par:par + 1], axis=0)
                                        ).then_inc(m.gathered[par], 16)

            def scatter(m, g, par, at):
                if not isinstance(at, int) or at >= 1:
                    pool.wait_ge(m.scattered[par], m.was["scattered"] + 16 * at)
                    held()
                pool.tensor_copy(si[:, par:par + 1], SIX[:, bass.ds(g, 1)]).then_inc(m.si_ready, 1)
                pool.wait_ge(m.si_ready, m.was["si_ready"] + g + 1)
                pool.wait_ge(m.ys_ready, m.was["ys_ready"] + g + 1)
                held()
                pool.indirect_dma_start(m.yhalf, bass.IndirectOffsetOnAxis(ap=si[:, par:par + 1], axis=0),
                                        YS[:, par, :], None, bounds_check=4 * m.T - 1, oob_is_err=False
                                        ).then_inc(m.scattered[par], 16)

            def route_pool(m):
                rstd(m.norms, m.tiles)
                pool.wait_ge(m.addr_ready, m.was["addr_ready"] + 1)
                for r in range(2 * m.nt):
                    pool.indirect_dma_start(m.table, bass.IndirectOffsetOnAxis(ap=m.addr[:, r:r + 1], axis=0),
                                            m.value[:, r:r + 1], None).then_inc(m.filled, 16)
                pool.wait_ge(m.filled, m.was["filled"] + 32 * m.nt)
                rows = m.table.rearrange("(e c s) o -> c e (s o)", e=NE, s=PASS)
                for c in range(m.subs):
                    for h in range(2):
                        pool.dma_start(LST[c:m.G:m.subs, PASS * h:PASS * h + PASS], rows[c]).then_inc(m.list_in, 16)

            LAG = 3

            def passes_pool(m):
                pool.wait_ge(m.lists_ready, m.was["lists_ready"] + 1)
                pool.wait_ge(m.rows_stored, m.was["rows_stored"] + 16 * m.nt)
                n = 2 * m.subs

                def body(i, first):
                    for r in range(n):
                        g = i * n + r
                        gather(m, g, r % 2)
                        if not first or r >= LAG:
                            scatter(m, g - LAG, (r - LAG) % 2, (i * n + r - LAG) // 2 if isinstance(i, int)
                                    else i * (n // 2) + (r - LAG) // 2)
                body(0, True)
                if n < LAG:
                    for r in range(n):
                        g = n + r
                        gather(m, g, r % 2)
                        if g >= LAG:
                            scatter(m, g - LAG, (g - LAG) % 2, (g - LAG) // 2)
                with pool.Fori(1 if n >= LAG else 2, NE // 2) as i:
                    body(i, False)
                for g in range(m.G - LAG, m.G):
                    scatter(m, g, g % 2, g // 2)

            def further_pool(m):
                pool.wait_ge(m.scattered[0], m.was["scattered"] + 8 * m.G)
                pool.wait_ge(m.scattered[1], m.was["scattered"] + 8 * m.G)
                pool.wait_ge(m.more_ready, m.was["more_ready"] + 1)
                count = pool.value_load(more[0:1, 0:1], min_val=0, max_val=m.most)
                rows = m.table.rearrange("(r s) o -> r (o s)", s=PASS)
                with pool.If(count > 0):
                    with pool.Fori(0, m.most) as o:
                        with pool.If(count > o):
                            r = pool.value_load(more[0:1, bass.ds(o + 16, 1)], min_val=0, max_val=NE * CAP // PASS - 1)
                            for h in range(2):
                                pool.dma_start(orow[:, PASS * h:PASS * h + PASS], rows[bass.ds(r, 1), :]).then_inc(m.further_dma, 16)
                            pool.wait_ge(m.further_dve, after(DVE_STEPS, o, "scatter_index"))
                            held()
                            pool.indirect_dma_start(XG[:, 0, :], None, m.hhalf, bass.IndirectOffsetOnAxis(ap=ogi, axis=0)
                                                    ).then_inc(m.further_dma, 16)
                            pool.wait_ge(m.further_act, after(ACT_STEPS, o, "y_kept"))
                            held()
                            pool.indirect_dma_start(m.yhalf, bass.IndirectOffsetOnAxis(ap=osi, axis=0), YS[:, 0, :], None,
                                                    bounds_check=4 * m.T - 1, oob_is_err=False).then_inc(m.further_dma, 16)
                            pool.wait_ge(m.further_dma, 64 * o + 64)
                            held()
                pool.sem_inc(m.passes_over, 1)

            rstd(0, range(TILES))
            for t in range(TILES):
                pool.wait_ge(hss_ready, t + 1)
                step(pool.tensor_scalar(hs[:, t], hs[:, t], 1.0 / DV, EPS, ALU.mult, ALU.add))
                pool.tensor_tensor(hs[:, t], hs[:, t], mhalf[:, :], ALU.pow).then_inc(hr_ready, 1)
            route_pool(moes[0])
            passes_pool(moes[0])
            further_pool(moes[0])
            rstd(8, range(TILES))
            route_pool(moes[1])
            passes_pool(moes[1])
            further_pool(moes[1])
            rstd(14, moes[1].tiles)

        def keep_fwd(act, u):
            h = u // 2
            act.wait_ge(den_ready, u + 1)
            for j in range(TILES):
                ins = act.activation(H[:, j, h, :], ps[:, 5 + j // 2, DVX * (j % 2):DVX * (j % 2) + DV], ACT.Copy,
                                     scale=att[:, u % 2, j:j + 1])
            ins.then_inc(fin_act, 1)

        @block.scalar
        def _(act):
            act.dma_start(cvec[:, 0, :], a["c_ctx"].rearrange("(k p) -> p k", p=P)).then_inc(cv_in, 16)
            act.dma_start(cvec[:, 1, :], a["c"][0].rearrange("(k p) -> p k", p=P)).then_inc(cv_in, 16)
            act.wait_ge(bada_zero, 1)
            for l in range(2):
                for s in range(2):
                    act.dma_start(bada[16 * s + 8 * l:P:32], a["b_ada"][l].rearrange("(g q n) -> q g n", g=3, q=4)
                                  ).then_inc(bada_in, 16)
            for l in range(2):
                act.dma_start(gmix[:, l, :], a["g_mix"][l].rearrange("(k p) -> p k", p=P)).then_inc(small_in, 16)
            act.dma_start(ghead[:, :], a["m_g_head"][0].rearrange("(k p) -> p k", p=P)).then_inc(small_in, 16)
            act.dma_start(brt[:, :], a["b_router"].rearrange("(o e) -> o e", o=1).to_broadcast([P, NE])).then_inc(small_in, 16)
            act.dma_start(wrt[:, :, :], a["w_router"].rearrange("(k p) e -> p k e", p=P)).then_inc(small_in, 16)
            act.dma_start(convw[:, :, :], a["r_conv_w"][0].rearrange("j (k p) -> p j k", p=P)).then_inc(rg_in, 16)
            act.dma_start(convb[:, :], a["r_conv_b"][0].rearrange("(k p) -> p k", p=P)).then_inc(rg_in, 16)
            act.dma_start(lam[:, :, :], a["r_lam"][0].rearrange("d (k p) -> p d k", p=P)).then_inc(rg_in, 16)
            for d in range(2):
                act.dma_start(rbias[:, d, :, :], a["r_b_gate"][0][d].rearrange("n (e p) -> p n e", p=P)).then_inc(rg_in, 16)
            act.wait_ge(pool_step, 1)
            act.wait_ge(bg_zero, 1)
            wgv = m_in[:, 3072:3104].rearrange("(k p) (g h) -> p k g h", p=P, g=4)
            for t in range(2):
                for d in range(2):
                    act.dma_start(wg[:, :, t, d, 0:HEADS], wgv[:, :, 2 * d + t, :]).then_inc(wg_in, 16)
                    act.dma_start(bgate[64 * t + 32 * d:64 * t + 32 * d + HEADS, :],
                                  a["m_b_gate"][0][2 * d + t].rearrange("(h o) -> h o", o=1)).then_inc(wg_in, 16)

            steps = [0]

            def step(ins):
                steps[0] += 1
                ins.then_inc(act_step, 1)
                act.wait_ge(act_step, steps[0])

            def gate2_act(base, tiles):
                for b in range(tiles):
                    s, cb = 2 - tiles // 2 + b // 2, b % 2
                    act.wait_ge(g2_done, base + b + 1)
                    act.activation(gate2[:, s, 512 * cb:512 * cb + 512], ps[:, 3 + b % 2, :], ACT.Copy).then_inc(g2_ready, 1)

            act.wait_ge(cv_in, 32)
            act.activation(cvec[:, :, :], cvec[:, :, :], ACT.Silu).then_inc(silu_ready, 1)

            def square(t, scratch):
                act.activation(scratch, X[:, t, :], ACT.Square, accum_out=stat[:, 0, t:t + 1]).then_inc(ss_ready, 1)

            def norm_mix(l):
                for t in range(TILES):
                    if l == 0:
                        act.wait_ge(x_ready, t + 1)
                        square(t, XN[:, t, :])
                for t in range(TILES):
                    act.wait_ge(rstd_ready, 8 * l + t + 1)
                    act.activation(XN[:, t, :], X[:, t, :], ACT.Copy, scale=stat[:, 2, t:t + 1]).then_inc(xn_ready, 1)
                act.wait_ge(cols_ready, l + 1)
                for b in range(0, 8, 2):
                    s, kp = b // 4, b % 4
                    act.wait_ge(nt_done, 8 * l + b + 1)
                    for kk in range(2):
                        k = 2 * kp + kk
                        ins = act.activation(hT[:, k, 256 * s:256 * s + 256], ps[:, 4 + b % 4, 256 * kk:256 * kk + 256],
                                             ACT.Identity, bias=bcol[:, s, k:k + 1], scale=acol[:, s, k:k + 1])
                    ins.then_inc(nt_act, 1)

            norm_mix(0)

            tm, em = gtmp[0:64, 4, :], gtmp[64:128, 5, :]
            act.wait_ge(lsig_ready, 1)
            step(act.activation(tm, tm, ACT.Exp))
            act.activation(tm, tm, ACT.Ln, bias=1.0).then_inc(lsig_kept, 1)
            for g in range(16):
                if g == 4:
                    act.wait_ge(em_ready, 2)
                    act.activation(em, em, ACT.Exp).then_inc(gates_ready, 1)
                act.wait_ge(proj_done, g + 1)
                if g < 4:
                    ins = act.activation(qT[:, g, :], ps[:, g % 4, :], ACT.Copy, scale=float(DQK) ** -0.5)
                elif g < 8:
                    ins = act.activation(kT[:, g - 4, :], ps[:, g % 4, :], ACT.Copy)
                else:
                    cb, t = (g - 8) // 4, g % 4
                    if g == 8:
                        act.wait_ge(gate_done, 1)
                    ins = act.activation(V[:, t, 4 * cb:4 * cb + 4, 0:DV],
                                         ps[:, g % 4, :].rearrange("p (h v) -> p h v", h=4), ACT.Copy)
                ins.then_inc(proj_kept, 1)

            for u in range(16):
                h, d = u // 2, u % 2
                if u >= 2 and u % 2 == 0:
                    keep_fwd(act, u - 2)
                act.wait_ge(d_done, u + 1)
                wd = W[:, u % 2].rearrange("p s j n -> p (s j) n")[:, 0:16:5, :]
                act.activation(wd, wd, ACT.Exp)
                todo = [(s, j, c) for s in range(TILES)
                        for j, c in runs_of([q for q in PAIRS[d] if q[0] != q[1]], s)]
                for s, j, c in todo:
                    ins = act.activation(W[:, u % 2, s, j:j + c, :], ps[:, 3 + u % 2, P * j:P * (j + c)].rearrange("p (j n) -> p j n", n=P),
                                         ACT.Exp, bias=gcol[:, s, 32 * d + h:32 * d + h + 1])
                ins.then_inc(e_done, 1)
            keep_fwd(act, 14)
            for g in range(8):
                cb, t = g // 4, g % 4
                act.wait_ge(oproj_done, g + 1)
                act.activation(O[:, t, 512 * cb:512 * cb + 512], ps[:, g % 3, :], ACT.Sigmoid).then_inc(og_ready, 1)
            act.wait_ge(o_done, 16)
            gate2_act(0, TILES)

            def route_act(m):
                l, t0 = m.l, m.tiles[0]
                act.wait_ge(y_ready, TILES + l)
                act.dma_start(gffn, a["g_ffn"][l].rearrange("(o n) -> o n", o=1).to_broadcast([P, D])).then_inc(m.gffn_in, 16)
                act.wait_ge(out_added, m.outs + 2)
                square(t0, XN[:, t0, :])
                for b in range(m.nt):
                    s, cb = b // 2, b % 2
                    act.wait_ge(m.rows_done, m.was["rows_done"] + 2 * b + 2)
                    act.activation(m.ab[:, 1, s, 512 * cb:512 * cb + 512], ps[:, 4, :], ACT.Copy).then_inc(m.shift_kept, 1)
                for i in range(m.nt):
                    act.wait_ge(m.h_ready, m.was["h_ready"] + i + 1)
                    act.dma_start(m.hrows[P * i:P * i + P, :], XN[:, t0 + i, :]).then_inc(m.rows_stored, 16)
                    if i + 1 < m.nt:
                        act.wait_ge(out_added, m.outs + 2 * i + 4)
                        square(t0 + i + 1, XN[:, t0 + i + 1, :])
                    act.wait_ge(m.turned, m.was["turned"] + 2 * i + 1)
                    act.activation(hT[:, 0:4, P * (t0 + i):P * (t0 + i) + P], ps[:, 5, :].rearrange("p (k n) -> p k n", k=4),
                                   ACT.Copy).then_inc(m.turn_kept_act, 1)
                act.wait_ge(m.shifted, m.was["shifted"] + 1)
                lg = sm[:, 0, 0:NE * m.nt]
                act.activation(lg, lg, ACT.Exp).then_inc(m.expd, 1)

            def passes_act(m):
                def silu(g, par):
                    act.wait_ge(m.h_done, m.was["h_done"] + g + 1)
                    if not isinstance(g, int) or g >= 2:
                        act.wait_ge(m.u_ready, m.was["u_ready"] + g - 1)
                    act.activation(SG[:, par, :], ps[:, 2 + par, 0:256], ACT.Silu).then_inc(m.silu_done, 1)

                def keep_y(g, par, at):
                    act.wait_ge(m.y_done, m.was["y_done"] + g + 1)
                    if not isinstance(at, int) or at >= 1:
                        act.wait_ge(m.scattered[par], m.was["scattered"] + 16 * at)
                    act.activation(YS[:, par, :], ps[:, 6 + par, :], ACT.Copy).then_inc(m.ys_ready, 1)

                def body(i):
                    n = 2 * m.subs
                    for e in range(2):
                        for r in range(e * m.subs, (e + 1) * m.subs):
                            silu(i * n + r, r % 2)
                        for r in range(e * m.subs, (e + 1) * m.subs):
                            keep_y(i * n + r, r % 2, i * m.subs + r // 2)
                body(0)
                with act.Fori(1, NE // 2) as i:
                    body(i)

            def rglru_act():
                for what, n in RG_ORDER:
                    if what == "x":
                        act.wait_ge(xr_done, n + 1)
                        act.wait_ge(pads, 1)
                        if n >= 2:
                            act.wait_ge(conv_done, n - 1)
                        act.activation(xpad[:, n % 2, :, 2:258], ps[:, n % 2, :].rearrange("p (s n) -> p s n", s=2), ACT.Copy
                                       ).then_inc(xr_kept, 1)
                    elif what == "y":
                        act.wait_ge(yb_done, n + 1)
                        act.activation(YB[:, n, :], ps[:, 2 + n % 2, 0:256], ACT.Gelu_apprx_tanh).then_inc(yb_kept, 1)
                    else:
                        act.wait_ge(lam_ready, 1)
                        for d in range(2):
                            act.wait_ge(rg_done, 2 * n + d + 1)
                            if n >= 1:
                                act.wait_ge(rg_scan, 2 * (n - 1) + d + 1)
                            for e in range(2):
                                ins = act.activation(RB[:, d, e, :], ps[:, 4 + 2 * d + e, :], ACT.Tanh,
                                                     bias=rbias[:, d, n, e:e + 1], scale=0.5)
                            step(ins)
                            act.activation(RB[:, d, 3, :], RB[:, d, 0, :], ACT.Exp, bias=spn[:, d, n:n + 1],
                                           scale=spn[:, d, n:n + 1])
                            step(act.activation(RB[:, d, 2, :], RB[:, d, 0, :], ACT.Tanh, bias=spl[:, d, n:n + 1],
                                                scale=spl[:, d, n:n + 1]))
                            act.activation(RB[:, d, 0, :], RB[:, d, 3, :], ACT.Square).then_inc(rg_tanh, 1)
                        for d in range(2):
                            act.wait_ge(rg_q, 2 * n + d + 1)
                            act.activation(RB[:, d, 2, :], RB[:, d, 2, :], ACT.Sqrt, scale=0.25).then_inc(rg_sqrt, 1)

            def further_act(m):
                act.wait_ge(m.more_ready, m.was["more_ready"] + 1)
                count = act.value_load(more[0:1, 0:1], min_val=0, max_val=m.most)
                with act.If(count > 0):
                    with act.Fori(0, m.most) as o:
                        with act.If(count > o):
                            act.wait_ge(m.further_pe, after(PE_STEPS, o, "up"))
                            act.activation(SG[:, 0, :], ps[:, 2, 0:256], ACT.Silu).then_inc(m.further_act, 1)
                            act.wait_ge(m.further_pe, after(PE_STEPS, o, "down"))
                            act.activation(YS[:, 0, :], ps[:, 6, :], ACT.Copy).then_inc(m.further_act, 1)

            def combine_act(m):
                ns = m.nt // 2
                for b in range(2 * ns):
                    s, cb = 2 - ns + b // 2, b % 2
                    act.wait_ge(m.g5_done, m.was["g5_done"] + b + 1)
                    act.activation(g5[:, s, 512 * cb:512 * cb + 512], ps[:, 3 + b % 2, :], ACT.Copy).then_inc(m.g5_kept, 1)
                act.wait_ge(m.passes_over, m.was["passes_over"] + 1)
                for i in range(m.nt):
                    for k in range(2):
                        act.dma_start(m.yin[i][k], m.yrows[m.T * k + P * i:m.T * k + P * i + P, :]).then_inc(m.y_in[i], 16)
                for i in range(m.nt):
                    act.wait_ge(m.y_in[i], m.was["y_in"] + 32)
                    y0 = m.yin[i][0]
                    act.activation(y0, y0, ACT.Copy, scale=m.weight[:, i:i + 1]).then_inc(m.y_scaled, 1)
                    if i >= 1:
                        act.wait_ge(m.added, m.was["added"] + i)
                        square(m.tiles[i - 1], m.yin[i - 1][0])
                act.wait_ge(m.added, m.was["added"] + m.nt)
                square(m.tiles[m.nt - 1], m.yin[m.nt - 1][0])

            route_act(moes[0])
            passes_act(moes[0])
            further_act(moes[0])
            act.wait_ge(lam_u, 1)
            act.activation(lt[:, 0, :], lt[:, 0, :], ACT.Exp).then_inc(lam_exp, 1)
            act.wait_ge(lam_u, 2)
            act.activation(lt[:, 2, :], lt[:, 1, :], ACT.Ln).then_inc(lam_ln, 1)
            combine_act(moes[0])
            norm_mix(1)
            rglru_act()
            gate2_act(4, 2)
            route_act(moes[1])
            passes_act(moes[1])
            further_act(moes[1])
            act.wait_ge(moes[1].ys_ready, moes[1].was["ys_ready"] + moes[1].G)
            act.dma_start(gffn, a["g_final"].rearrange("(o n) -> o n", o=1).to_broadcast([P, D])).then_inc(gfin_in, 16)
            combine_act(moes[1])
            for i in range(2):
                act.wait_ge(fin_ready, i + 1)
                act.dma_start(out[0, P * i:P * i + P, :], moes[1].yin[i][1]).then_inc(stored, 16)

        @block.tensor
        def _(pe):
            def ada(l, j, bank):
                g, kk = j // 4, j % 4
                c = CHUNK_NO[f"ada{l}", j]
                pe.wait_ge(silu_ready, 2 + l)
                use(pe, c)
                w = slot(c).rearrange("p (k q n) -> p k q n", k=2, q=4)
                for k2 in range(2):
                    k = 2 * kk + k2
                    for q in range(4):
                        ins = pe.matmul(ps[32 * q:32 * q + 32, bank, :], silu_c[:, k, :, :].rearrange("p s r -> p (s r)"),
                                        w[:, k2, q, :], start=(k == 0), stop=(k == KD - 1))
                ins.then_inc(ada_done if kk == 3 else ada_part, 1)

            def modcol(l):
                pe.wait_ge(modr_ready, 1 if l == 0 else 6)
                pe.wait_ge(consts, 1)
                for c in range(4):
                    ins = pe.transpose(ps[:, 3, P * c:P * c + P], modr[:, 0, P * c:P * c + P], ident[:, :])
                ins.then_inc(modcol_done, 1)

            def norm_turn(l):
                for b in range(8):
                    s, kp = b // 4, b % 4
                    pe.wait_ge(xn_ready, TILES * l + 2 * s + 2)
                    if b >= 4:
                        pe.wait_ge(nt_act if b % 2 == 0 else nt_dve, 4 * l + (b - 4) // 2 + 1)
                    for kk in range(2):
                        for t in range(2):
                            k = 2 * kp + kk
                            ins = pe.transpose(ps[:, 4 + b % 4, 256 * kk + P * t:256 * kk + P * t + P],
                                               XN[:, 2 * s + t, P * k:P * k + P], ident[:, :])
                    ins.then_inc(nt_done, 1)

            for j in range(4):
                ada(0, j, 0)
            modcol(0)
            norm_turn(0)

            pe.wait_ge(nt_act, 4)
            pe.wait_ge(nt_dve, 4)
            pe.wait_ge(wg_in, 128)
            for k in range(KD):
                for t in range(2):
                    ins = pe.matmul(ps[64 * t:64 * t + 64, 4, :], wg[:, k, t, :, :].rearrange("p d r -> p (d r)"),
                                    hT[:, k, :], start=(k == 0), stop=(k == KD - 1))
            ins.then_inc(gate_done, 1)
            for g in range(16):
                if g >= 4:
                    pe.wait_ge(proj_kept, g - 3)
                elif g == 3:
                    pe.wait_ge(cols_ready, 1)
                cb = g // 4
                c = CHUNK_NO["in0", cb]
                if g % 4 == 0:
                    use(pe, c)
                w = slot(c).rearrange("p (k n) -> p k n", k=KD)
                for k in range(KD):
                    if g < 8:
                        l_, r_ = w[:, k, P * (g % 4):P * (g % 4) + P], hT[:, k, :]
                    else:
                        l_, r_ = hT[:, k, P * (g % 4):P * (g % 4) + P], w[:, k, :]
                    ins = pe.matmul(ps[:, g % 4, :], l_, r_, start=(k == 0), stop=(k == KD - 1))
                ins.then_inc(proj_done, 1)
                if g < 8:
                    ada(0, 4 + g, 5 + g // 4)
            pe.wait_ge(gates_ready, 1)
            for t in range(TILES):
                ins = pe.transpose(ps[:, 7, P * t:P * t + P], gtmp[:, 5, P * t:P * t + P], ident[:, :])
            ins.then_inc(gturn_done, 1)

            def scores(h):
                p0 = 64 * (h % 2)
                for s in range(TILES):
                    o = ps[:, s, :] if s < 2 else ps[:, 2, 256 * (s - 2):256 * (s - 2) + 256]
                    j0 = 0 if s < 2 else 256
                    ins = pe.matmul(o, kT[p0:p0 + 64, h // 2, P * s:P * s + P], qT[p0:p0 + 64, h // 2, j0:T_ALL],
                                    start=True, stop=True)
                ins.then_inc(s_done, 1)

            def rows(u):
                r = 32 * (u % 2) + u // 2
                if u >= 2:
                    pe.wait_ge(e_done, u - 1)
                pe.matmul(ps[:, 3 + u % 2, :], ident[0:64, r:r + 1].to_broadcast([64, P]), rrow[:, :],
                          start=True, stop=True).then_inc(r_done, 1)

            pe.wait_ge(proj_kept, 16)
            scores(0)
            pe.wait_ge(gcol_ready, 1)
            pe.wait_ge(v_ones, 1)
            rows(0)
            rows(1)
            for u in range(16):
                h, d = u // 2, u % 2
                pe.wait_ge(p_done, u + 1)
                if d == 1 and h + 1 < HEADS:
                    scores(h + 1)
                if u >= 1:
                    pe.wait_ge(fin_act if (u - 1) % 2 == 0 else fin_dve, (u - 1) // 2 + 1)
                for j in range(TILES):
                    keys = (fwd_keys if d == 0 else bwd_keys)(j)
                    for s in keys:
                        ins = pe.matmul(ps[:, 5 + j // 2, DVX * (j % 2):DVX * (j % 2) + DVX], W[:, u % 2, s, j, :],
                                        V[:, s, h, :], start=(s == keys[0]), stop=(s == keys[-1]))
                ins.then_inc(o_done, 1)
                if u + 2 < 16:
                    rows(u + 2)
                if u < ADA_CHUNKS:
                    if u % 4 == 0:
                        pe.wait_ge(modr_ready, 3 + u // 4)
                    ada(1, u, 7)

            for g in range(8):
                cb, t = g // 4, g % 4
                c = CHUNK_NO["in0", 4 + cb]
                if t == 0:
                    use(pe, c)
                if g >= 3:
                    pe.wait_ge(og_ready, g - 2)
                w = slot(c).rearrange("p (k n) -> p k n", k=KD)
                for k in range(KD):
                    ins = pe.matmul(ps[:, g % 3, :], hT[:, k, P * t:P * t + P], w[:, k, :],
                                    start=(k == 0), stop=(k == KD - 1))
                ins.then_inc(oproj_done, 1)

            def bcast(l, col, s, bank):
                r = 32 * (col % 4) + 16 * s + 8 * l
                return pe.matmul(ps[:, bank, :], ident[:, r:r + 1].to_broadcast([P, P]), modr[:, col // 4, :],
                                 start=True, stop=True)

            pe.wait_ge(e_done, 16)
            pe.wait_ge(modr_ready, 6)
            for b in range(4):
                if b >= 2:
                    pe.wait_ge(g2_ready, b - 1)
                bcast(0, 4 + b % 2, b // 2, 3 + b % 2).then_inc(g2_done, 1)

            for t in range(TILES):
                pe.wait_ge(y_ready, t + 1)
                for b in range(2):
                    g = 2 * t + b
                    if g >= 3:
                        pe.wait_ge(yt_kept, g - 2)
                    for kk in range(4):
                        k = 4 * b + kk
                        ins = pe.transpose(ps[:, 5 + g % 3, P * kk:P * kk + P], XN[:, t, P * k:P * k + P], ident[:, :])
                    ins.then_inc(yt_done, 1)
            pe.wait_ge(og_ready, 8)
            pe.wait_ge(yt_kept, 8)
            def route_pe(m, kind, ybuf):
                nt, t0 = m.nt, m.tiles[0]

                def out_piece(i, cb):
                    g, c = 2 * i + cb, CHUNK_NO[kind, cb]
                    if i == 0:
                        use(pe, c)
                    if g >= 3:
                        pe.wait_ge(out_added, m.outs + g - 2)
                    w = slot(c).rearrange("p (k n) -> p k n", k=KD)
                    for k in range(KD):
                        ins = pe.matmul(ps[:, g % 3, :], ybuf(k, i), w[:, k, :], start=(k == 0), stop=(k == KD - 1))
                    ins.then_inc(out_done, 1)

                def rows_of_both():
                    pe.wait_ge(g2_ready, (4, 6)[m.l])
                    for b in range(nt):
                        s, cb = 2 - nt // 2 + b // 2, b % 2
                        if b >= 1:
                            pe.wait_ge(m.scale_kept, m.was["scale_kept"] + b)
                        bcast(m.l, 2 * 4 + cb, s, 3).then_inc(m.rows_done, 1)
                        if b >= 1:
                            pe.wait_ge(m.shift_kept, m.was["shift_kept"] + b)
                        bcast(m.l, 2 * 3 + cb, s, 4).then_inc(m.rows_done, 1)

                def turn_h(i):
                    pe.wait_ge(m.h_ready, m.was["h_ready"] + i + 1)
                    for b in range(2):
                        if i >= 1:
                            pe.wait_ge(m.turn_kept_dve if b else m.turn_kept_act, m.was["turn_kept_act"] + i)
                        for kk in range(4):
                            k = 4 * b + kk
                            ins = pe.transpose(ps[:, 5 + b, P * kk:P * kk + P], XN[:, t0 + i, P * k:P * k + P], ident[:, :])
                        ins.then_inc(m.turned, 1)

                def logits(i):
                    pe.wait_ge(m.turn_kept_act, m.was["turn_kept_act"] + i + 1)
                    pe.wait_ge(m.turn_kept_dve, m.was["turn_kept_dve"] + i + 1)
                    for k in range(KD):
                        ins = pe.matmul(ps[:, 7, NE * i:NE * i + NE], hT[:, k, P * (t0 + i):P * (t0 + i) + P], wrt[:, k, :],
                                        start=(k == 0), stop=(k == KD - 1))
                    return ins

                for i in range(nt):
                    for cb in range(2):
                        out_piece(i, cb)
                    if i == 0:
                        rows_of_both()
                    if i >= 1:
                        turn_h(i - 1)
                    if i >= 2:
                        logits(i - 2)
                turn_h(nt - 1)
                logits(nt - 2)
                logits(nt - 1).then_inc(m.logits_done, 1)
                pe.wait_ge(m.picked, m.was["picked"] + 1)
                both = sm[:, 3, 0:NE * m.nt].rearrange("p (t e) -> p t e", e=NE)
                for i in range(m.nt + 1):
                    o = ps[:, 0, NE * i:NE * i + NE]
                    for j in range(min(i, m.nt - 1) + 1):
                        ins = pe.matmul(o, triu[:, :] if j == i else ones[:, :], both[:, j, :],
                                        start=(j == 0), stop=(j == min(i, m.nt - 1)))
                ins.then_inc(m.pos_done, 1)
                pe.wait_ge(m.list_in, m.was["list_in"] + 32 * m.subs)
                pe.transpose(ps[:, 1, 0:m.G], LST[0:m.G, :], ident[0:m.G, 0:m.G]).then_inc(m.list_turned, 1)

            def up_half(par, h, chunk):
                w = slot(chunk).rearrange("p (k w n) -> p k w n", k=4, w=2)
                for j in range(4):
                    for oh in range(2):
                        ins = pe.matmul(ps[64 * oh:64 * oh + 64, 2 + par, :].rearrange("p (w n) -> p w n", w=2),
                                        XT[:, par, j, 64 * h:64 * h + 64], w[:, j, :, 256 * oh:256 * oh + 256],
                                        start=(h == 0 and j == 0), stop=(h == 1 and j == 3))
                return ins

            def down_all(par, chunk):
                w = slot(chunk).rearrange("p (c n) -> p c n", c=4)
                for kc in range(4):
                    for oh in range(2):
                        ins = pe.matmul(ps[64 * oh:64 * oh + 64, 6 + par, :],
                                        UT[:, par, kc % 2, 64 * (kc // 2):64 * (kc // 2) + 64],
                                        w[:, kc, 512 * oh:512 * oh + 512], start=(kc == 0), stop=(kc == 3))
                return ins

            def passes_pe(m):
                n = 2 * m.subs

                def turn(g, par, at):
                    pe.wait_ge(m.gathered[par], m.was["gathered"] + 16 + 16 * at)
                    if not isinstance(g, int) or g >= 2:
                        pe.wait_ge(m.xt_ready, m.was["xt_ready"] + g - 1)
                    for j in range(4):
                        ins = pe.transpose(ps[:, par, P * j:P * j + P], XG[:, par, P * j:P * j + P], ident[:, :])
                    ins.then_inc(m.tx_done, 1)

                def up(g, par, h, chunk, i, load, sig):
                    if h == 0:
                        pe.wait_ge(m.xt_ready, m.was["xt_ready"] + g + 1)
                        if not isinstance(g, int) or g >= 2:
                            pe.wait_ge(m.u_ready, m.was["u_ready"] + g - 1)
                    if load:
                        use(pe, chunk, i)
                    ins = up_half(par, h, chunk)
                    if sig is not None:
                        ins.then_inc(sig, 1)

                def turn_u(g, par):
                    pe.wait_ge(m.u_ready, m.was["u_ready"] + g + 1)
                    if not isinstance(g, int) or g >= 2:
                        pe.wait_ge(m.ut_ready, m.was["ut_ready"] + g - 1)
                    for c in range(2):
                        ins = pe.transpose(ps[:, 4 + par, P * c:P * c + P], U[:, par, P * c:P * c + P], ident[:, :])
                    ins.then_inc(m.tu_done, 1)

                def down(g, par, chunk, i, load):
                    pe.wait_ge(m.ut_ready, m.was["ut_ready"] + g + 1)
                    if not isinstance(g, int) or g >= 2:
                        pe.wait_ge(m.ys_ready, m.was["ys_ready"] + g - 1)
                    if load:
                        use(pe, chunk, i)
                    down_all(par, chunk).then_inc(m.y_done, 1)

                def body(i, last):
                    for b in range(2):
                        c = m.base + 3 * b
                        r = b * m.subs
                        g = i * n + r
                        at = i * (n // 2)
                        if m.subs == 2:
                            turn(g + 1, 1, at + (r + 1) // 2)
                            up(g, 0, 0, c, i, True, None)
                            up(g, 0, 1, c + 1, i, True, m.h_done)
                            up(g + 1, 1, 0, c, i, False, m.half_done)
                            turn_u(g, 0)
                            up(g + 1, 1, 1, c + 1, i, False, m.h_done)
                            down(g, 0, c + 2, i, True)
                            turn_u(g + 1, 1)
                            if not (last and b == 1):
                                turn(g + 2, 0, at + (r + 2) // 2)
                            down(g + 1, 1, c + 2, i, False)
                        else:
                            up(g, b, 0, c, i, True, m.half_done)
                            up(g, b, 1, c + 1, i, True, m.h_done)
                            if not (last and b == 1):
                                turn(g + 1, 1 - b, at + (r + 1) // 2)
                            turn_u(g, b)
                            down(g, b, c + 2, i, True)

                turn(0, 0, 0)
                body(0, False)
                with pe.Fori(1, NE // 2 - 1) as i:
                    body(i, False)
                body(NE // 2 - 1, True)

            def further_pe(m):
                pe.wait_ge(m.more_ready, m.was["more_ready"] + 1)
                pe.wait_ge(m.ys_ready, m.was["ys_ready"] + m.G)
                count = pe.value_load(more[0:1, 0:1], min_val=0, max_val=m.most)
                with pe.If(count > 0):
                    with pe.Fori(0, m.most) as o:
                        with pe.If(count > o):
                            pe.wait_ge(m.further_dma, 64 * o + 32)
                            pe.matmul(ps[:, 1, 0:1], orow, ones[0:1, 0:1], start=True, stop=True).then_inc(m.further_pe, 1)
                            pe.wait_ge(m.further_dma, 64 * o + 48)
                            for j in range(4):
                                ins = pe.transpose(ps[:, 0, P * j:P * j + P], XG[:, 0, P * j:P * j + P], ident[:, :])
                            ins.then_inc(m.further_pe, 1)
                            pe.wait_ge(m.further_dve, after(DVE_STEPS, o, "xt"))
                            pe.wait_ge(m.further_loaded, 96 * o + 96)
                            for h in range(2):
                                ins = up_half(0, h, h)
                            ins.then_inc(m.further_pe, 1)
                            pe.wait_ge(m.further_dve, after(DVE_STEPS, o, "u"))
                            for c in range(2):
                                ins = pe.transpose(ps[:, 4, P * c:P * c + P], U[:, 0, P * c:P * c + P], ident[:, :])
                            ins.then_inc(m.further_pe, 1)
                            pe.wait_ge(m.further_dve, after(DVE_STEPS, o, "ut"))
                            down_all(0, 2).then_inc(m.further_pe, 1)

            def combine_pe(m):
                ns = m.nt // 2
                pe.wait_ge(m.u_ready, m.was["u_ready"] + m.G)
                pe.wait_ge(m.ut_ready, m.was["ut_ready"] + m.G)
                for b in range(2 * ns):
                    s, cb = 2 - ns + b // 2, b % 2
                    if b >= 2:
                        pe.wait_ge(m.g5_kept, m.was["g5_kept"] + b - 1)
                    bcast(m.l, 2 * 5 + cb, s, 3 + b % 2).then_inc(m.g5_done, 1)

            def rglru_pe():
                gates = slot(N_MIX1 + 2).rearrange("p (d n e q) -> p d n e q", d=2, n=8, e=2)
                for what, n in RG_ORDER:
                    hi = n // 4
                    if what == "g":
                        if n == 0:
                            use(pe, N_MIX1 + 2)
                        pe.wait_ge(conv_done, n + 1)
                        for d in range(2):
                            if n >= 1:
                                pe.wait_ge(rg_tanh, 2 * (n - 1) + d + 1)
                            for e in range(2):
                                ins = pe.matmul(ps[:, 4 + 2 * d + e, :], gates[:, d, n, e, :], XC[:, n, :],
                                                start=True, stop=True)
                            ins.then_inc(rg_done, 1)
                        continue
                    c = N_MIX1 + (0, 3)[hi] if what == "x" else N_MIX1 + (1, 4)[hi]
                    if n % 4 == 0:
                        use(pe, c)
                    w = slot(c).rearrange("p (k n) -> p k n", k=KD)[:, :, P * (n % 4):P * (n % 4) + P]
                    kept, done = (xr_kept, xr_done) if what == "x" else (yb_kept, yb_done)
                    if n >= 2:
                        pe.wait_ge(kept, n - 1)
                    o, t0 = (ps[:, n % 2, :], 0) if what == "x" else (ps[:, 2 + n % 2, 0:256], 256)
                    for k in range(KD):
                        ins = pe.matmul(o, w[:, k, :], hT[:, k, t0:T_ALL], start=(k == 0), stop=(k == KD - 1))
                    ins.then_inc(done, 1)

            route_pe(moes[0], "out0", lambda k, t: hT[:, k, P * t:P * t + P])
            passes_pe(moes[0])
            further_pe(moes[0])
            combine_pe(moes[0])
            pe.wait_ge(moes[0].xt_ready, moes[0].G)
            pe.wait_ge(moes[0].ys_ready, moes[0].G)
            pe.wait_ge(moes[0].g5_kept, 4)
            modcol(1)
            norm_turn(1)
            pe.wait_ge(nt_act, 8)
            pe.wait_ge(nt_dve, 8)
            pe.wait_ge(cols_ready, 2)
            rglru_pe()
            pe.wait_ge(yb_kept, 8)
            pe.wait_ge(rg_tanh, 16)
            for b in range(2):
                bcast(1, 4 + b, 1, 3 + b).then_inc(g2_done, 1)
            pe.wait_ge(y_ready, TILES + 1)
            route_pe(moes[1], "out1", lambda k, t: YT[:, k, P * t:P * t + P])
            passes_pe(moes[1])
            further_pe(moes[1])
            combine_pe(moes[1])

        @block.vector
        def _(dve):
            steps = [0]

            def step(ins):
                steps[0] += 1
                ins.then_inc(dve_step, 1)
                dve.wait_ge(dve_step, steps[0])

            dve.wait_ge(silu_ready, 1)
            step(dve.memset(silu_c[:, :, :, :], 0.0))
            dve.tensor_copy(silu_c[:, :, :, 0:8].rearrange("p k s r -> p s k r"),
                            cvec[:, :, :].unsqueeze(3).to_broadcast([P, 2, KD, 8])).then_inc(silu_ready, 1)
            dve.wait_ge(x_in, 64)
            for t in range(TILES):
                if t < 2:
                    dve.tensor_copy(X[:, t, 0:1], X[:, t, 0:1]).then_inc(x_ready, 1)
                else:
                    dve.wait_ge(pos_in, 32)
                    dve.tensor_tensor(X[:, t, :], X[:, t, :], XN[:, t, :], ALU.add).then_inc(x_ready, 1)
            dve.wait_ge(consts, 1)
            step(dve.tensor_copy(iota16[:, :], iota16i[:, :]))
            step(dve.tensor_copy(tokf[:, :], toki[:, :]))
            step(dve.tensor_scalar(half[:, :], tokf[:, 0:1], 64.0, None, ALU.is_ge))

            def modulation(l, g, bank):
                dve.wait_ge(ada_done, 3 * l + g + 1)
                dve.tensor_tensor(modr[:, g, :], ps[:, bank, :], modr[:, g, :] if l else bada[:, g, :], ALU.add
                                  ).then_inc(modr_ready, 1)

            def columns(l):
                dve.wait_ge(small_in, 80)
                dve.wait_ge(modcol_done, l + 1)
                m = ps[:, 3, :].rearrange("p (c q r) -> p q c r", c=4, q=4)
                for s in range(2):
                    dve.tensor_copy(bcol[:, s, :].rearrange("p (q c) -> p q c", q=2), m[:, 0:2, :, 16 * s + 8 * l])
                    ins = dve.scalar_tensor_tensor(
                        out=acol[:, s, :].rearrange("p (q c) -> p q c", q=2), in0=m[:, 2:4, :, 16 * s + 8 * l],
                        scalar=1.0, in1=gmix[:, l, :].rearrange("p (q c) -> p q c", q=2),
                        op0=ALU.add, op1=ALU.mult)
                ins.then_inc(cols_ready, 1)

            def norm_keep(l):
                dve.wait_ge(cols_ready, l + 1)
                for b in range(1, 8, 2):
                    s, kp = b // 4, b % 4
                    dve.wait_ge(nt_done, 8 * l + b + 1)
                    for kk in range(2):
                        k = 2 * kp + kk
                        ins = dve.tensor_scalar(hT[:, k, 256 * s:256 * s + 256], ps[:, 4 + b % 4, 256 * kk:256 * kk + 256],
                                                acol[:, s, k:k + 1], bcol[:, s, k:k + 1], ALU.mult, ALU.add)
                    ins.then_inc(nt_dve, 1)

            dve.wait_ge(bada_in, 64)
            modulation(0, 0, 0)
            columns(0)
            norm_keep(0)

            dve.wait_ge(gate_done, 1)
            ig, lf, mm, bb, tm, ce = (gtmp[:, i, :] for i in range(6))
            for t, dst in ((0, ig), (1, lf)):
                for d in range(2):
                    r = 64 * t + 32 * d
                    o = dst[32 * d:32 * d + 32].rearrange("p (s n) -> p s n", s=2)
                    i = ps[r:r + 32, 4, :].rearrange("p (s n) -> p s n", s=2)
                    if d:
                        o = o[:, :, ::-1]
                    step(dve.tensor_scalar(o, i, bgate[r:r + 32, 0:1], None, ALU.add))
            g64 = slice(0, 64)
            step(dve.scalar_tensor_tensor(out=tm[g64], in0=lf[g64], scalar=-1.0, in1=lf[g64], op0=ALU.mult, op1=ALU.min))
            ins = dve.tensor_scalar(lf[g64], lf[g64], 0.0, None, ALU.min)
            ins.then_inc(lsig_ready, 1)
            dve.wait_ge(lsig_kept, 1)
            step(dve.tensor_tensor(lf[g64], lf[g64], tm[g64], ALU.subtract))
            step(dve.memset(tm[g64], 0.0))
            step(dve.tensor_tensor_scan(mm[g64], lf[g64], ig[g64], 0.0, ALU.add, ALU.max))
            step(dve.tensor_tensor_scan(bb[g64], lf[g64], tm[g64], 0.0, ALU.add, ALU.add))
            for d in range(2):
                r = slice(32 * d, 32 * d + 32)
                rev = (lambda v: v.rearrange("p (s n) -> p s n", s=2)[:, :, ::-1]) if d else (lambda v: v.rearrange("p (s n) -> p s n", s=2))
                nat = lambda v: v.rearrange("p (s n) -> p s n", s=2)
                step(dve.tensor_tensor(rev(rrow[r, :]), nat(bb[r]), nat(mm[r]), ALU.subtract))
                step(dve.tensor_tensor(rev(ce[r]), nat(ig[r]), nat(bb[r]), ALU.subtract))
                q = slice(64 + 32 * d, 96 + 32 * d)
                dve.tensor_scalar(rev(ce[q]), nat(mm[r]), -1.0, None, ALU.mult).then_inc(em_ready, 1)
            for g in (1, 2):
                modulation(0, g, 4 + g)
            step(dve.tensor_copy(silu_c[:, :, :, 8:16], silu_c[:, :, :, 0:8]))
            dve.memset(silu_c[:, :, :, 0:8], 0.0).then_inc(silu_ready, 1)
            dve.wait_ge(gturn_done, 1)
            dve.tensor_copy(gcol[:, :, :].rearrange("p t c -> p (t c)"), ps[:, 7, :]).then_inc(gcol_ready, 1)
            dve.wait_ge(proj_kept, 16)
            dve.memset(V[:, :, :, DV:DVX], 1.0).then_inc(v_ones, 1)

            def diag(u):
                h, d = u // 2, u % 2
                dve.wait_ge(r_done, u + 1)
                if u >= 2:
                    dve.wait_ge(o_done, u - 1)
                for s in range(TILES):
                    ins = dve.scalar_tensor_tensor(out=W[:, u % 2, s, s, :], in0=ps[:, 3 + u % 2, P * s:P * s + P],
                                                   scalar=gcol[:, s, 32 * d + h:32 * d + h + 1], in1=masks[:, d, :],
                                                   op0=ALU.add, op1=ALU.add)
                ins.then_inc(d_done, 1)

            def prod(u):
                h, d = u // 2, u % 2
                dve.wait_ge(s_done, h + 1)
                dve.wait_ge(e_done, u + 1)
                for s in range(TILES):
                    for j, c in runs_of(PAIRS[d], s):
                        o = P * j if s < 2 else 256 * (s - 2) + P * (j - 2)
                        w = W[:, u % 2, s, j:j + c, :]
                        ins = dve.tensor_tensor(w, ps[:, min(s, 2), o:o + P * c].rearrange("p (j n) -> p j n", n=P), w,
                                                ALU.mult)
                ins.then_inc(p_done, 1)

            def keep(u):
                h, d = u // 2, u % 2
                dve.wait_ge(o_done, u + 1)
                den = ps[:, 5:7, 0:2 * DVX].rearrange("p b (j c) -> p b j c", j=2)[:, :, :, DV]
                e = gcol[:, :, 64 + 32 * d + h].rearrange("p (b j) -> p b j", b=2)
                r = att[:, d, :].rearrange("p (b j) -> p b j", b=2)
                step(dve.scalar_tensor_tensor(out=r, in0=den, scalar=-1.0, in1=e, op0=ALU.mult, op1=ALU.max))
                step(dve.tensor_tensor(r, den, r, ALU.max))
                dve.reciprocal(att[:, d, :], att[:, d, :]).then_inc(den_ready, 1)
                if d == 1:
                    dve.wait_ge(den_ready, u + 1)
                    dve.wait_ge(fin_act, h + 1)
                    for j in range(TILES):
                        ins = dve.scalar_tensor_tensor(out=H[:, j, h, :], in0=ps[:, 5 + j // 2, DVX * (j % 2):DVX * (j % 2) + DV],
                                                       scalar=att[:, d, j:j + 1], in1=H[:, j, h, :],
                                                       op0=ALU.mult, op1=ALU.add)
                    ins.then_inc(fin_dve, 1)

            dve.wait_ge(gcol_ready, 1)
            diag(0)
            diag(1)
            prod(0)
            for u in range(16):
                if u + 1 < 16:
                    prod(u + 1)
                keep(u)
                if u + 2 < 16:
                    diag(u + 2)
                if u < ADA_CHUNKS and u % 4 == 3:
                    modulation(1, u // 4, 7)

            dve.wait_ge(fin_dve, 8)
            for t in range(TILES):
                step(dve.tensor_tensor(sq, H[:, t], H[:, t], ALU.mult))
                dve.tensor_reduce(hs[:, t], sq, AX_X, ALU.add).then_inc(hss_ready, 1)
                dve.wait_ge(hss_ready, t + 1)
            for t in range(TILES):
                dve.wait_ge(hr_ready, t + 1)
                step(dve.tensor_tensor(H[:, t], H[:, t], hs[:, t].unsqueeze(2).to_broadcast([P, HEADS, DV]), ALU.mult))
                dve.wait_ge(og_ready, 4 + t + 1)
                dve.tensor_tensor(XN[:, t, :], XN[:, t, :], O[:, t, :], ALU.mult).then_inc(y_ready, 1)
            for g in range(8):
                t, b = g // 2, g % 2
                dve.wait_ge(yt_done, g + 1)
                dve.tensor_tensor(hT[:, 4 * b:4 * b + 4, P * t:P * t + P],
                                  ps[:, 5 + g % 3, :].rearrange("p (k n) -> p k n", k=4),
                                  ghead[:, 4 * b:4 * b + 4].unsqueeze(2).to_broadcast([P, 4, P]), ALU.mult
                                  ).then_inc(yt_kept, 1)

            def route_dve(m):
                nt, t0, l = m.nt, m.tiles[0], m.l

                def add_out(i):
                    for cb in range(2):
                        g, t, c = 2 * i + cb, t0 + i, slice(512 * cb, 512 * cb + 512)
                        dve.wait_ge(out_done, m.outs + g + 1)
                        if g:
                            dve.wait_ge(out_added, m.outs + g)
                        step(dve.tensor_tensor(gtmp2, ps[:, g % 3, :], gate2[:, t // 2, c], ALU.mult))
                        dve.tensor_tensor(X[:, t, c], X[:, t, c], gtmp2, ALU.add).then_inc(out_added, 1)

                def h_of(i):
                    t, s = t0 + i, i // 2
                    dve.wait_ge(rstd_ready, m.norms + i + 1)
                    step(dve.scalar_tensor_tensor(out=XN[:, t, :], in0=X[:, t, :], scalar=stat[:, 2, t:t + 1],
                                                  in1=m.ab[:, 0, s, :], op0=ALU.mult, op1=ALU.mult))
                    dve.tensor_tensor(XN[:, t, :], XN[:, t, :], m.ab[:, 1, s, :], ALU.add).then_inc(m.h_ready, 1)

                dve.wait_ge(g2_ready, (4, 6)[l])
                add_out(0)
                dve.wait_ge(m.gffn_in, m.was["gffn_in"] + 16)
                for b in range(nt):
                    s, c = b // 2, slice(512 * (b % 2), 512 * (b % 2) + 512)
                    dve.wait_ge(m.rows_done, m.was["rows_done"] + 2 * b + 1)
                    dve.scalar_tensor_tensor(out=m.ab[:, 0, s, c], in0=ps[:, 3, :], scalar=1.0, in1=gffn[:, c],
                                             op0=ALU.add, op1=ALU.mult).then_inc(m.scale_kept, 1)
                dve.wait_ge(m.scale_kept, m.was["scale_kept"] + nt)
                dve.wait_ge(m.shift_kept, m.was["shift_kept"] + nt)
                for i in range(nt):
                    h_of(i)
                    if i + 1 < nt:
                        add_out(i + 1)
                    dve.wait_ge(m.turned, m.was["turned"] + 2 * i + 2)
                    dve.tensor_copy(hT[:, 4:8, P * (t0 + i):P * (t0 + i) + P], ps[:, 6, :].rearrange("p (k n) -> p k n", k=4)
                                    ).then_inc(m.turn_kept_dve, 1)

                def row(n, w):
                    return sm[:, n, 0:w * nt].rearrange("p (t e) -> p t e", e=w)

                def bc(v, w):
                    return v.to_broadcast([P, nt, w])

                lg, sel, pick0, pick = row(0, NE), row(1, NE), row(2, NE), row(3, NE)
                tmp, r1, r2 = row(4, NE), row(5, 1), row(6, 1)
                dve.wait_ge(m.logits_done, m.was["logits_done"] + 1)
                L = ps[:, 7, 0:NE * nt].rearrange("p (t e) -> p t e", e=NE)
                step(dve.tensor_reduce(r1[:, :, 0], L, AX_X, ALU.max))
                dve.tensor_tensor(lg, L, bc(r1, NE), ALU.subtract).then_inc(m.shifted, 1)
                dve.wait_ge(m.expd, m.was["expd"] + 1)
                step(dve.tensor_reduce(r1[:, :, 0], lg, AX_X, ALU.add))
                step(dve.reciprocal(r2, r1))
                step(dve.tensor_tensor(lg, lg, bc(r2, NE), ALU.mult))
                step(dve.tensor_tensor(sel, lg, brt[:, :].unsqueeze(1).to_broadcast([P, nt, NE]), ALU.add))
                q = sm[:, 1, 0:NE * nt].rearrange("p (g a b) -> p g a b", a=2, b=2)
                hi = sm[:, 7, 0:8 * nt].rearrange("p (g a) -> p g a", a=2)
                lo = sm[:, 8, 0:8 * nt].rearrange("p (g a) -> p g a", a=2)
                t1, t2, t3 = (sm[:, x, 0:4 * nt] for x in (9, 10, 11))
                step(dve.tensor_tensor(hi, q[:, :, :, 0], q[:, :, :, 1], ALU.max))
                step(dve.tensor_tensor(lo, q[:, :, :, 0], q[:, :, :, 1], ALU.min))
                step(dve.tensor_tensor(t1, hi[:, :, 0], hi[:, :, 1], ALU.max))
                step(dve.tensor_tensor(t2, hi[:, :, 0], hi[:, :, 1], ALU.min))
                step(dve.tensor_tensor(t3, lo[:, :, 0], lo[:, :, 1], ALU.max))
                step(dve.tensor_tensor(t2, t2, t3, ALU.max))
                step(dve.tensor_tensor(t1, t1, t2, ALU.add))
                gs, eq, first = row(9, 4), row(10, 4), row(11, 4)
                step(dve.tensor_reduce(r1[:, :, 0], gs, AX_X, ALU.max))
                step(dve.tensor_tensor(eq, gs, bc(r1, 4), ALU.is_equal))
                step(dve.tensor_scalar(first[:, 0, :], iota16[:, 0:4], -1.0, 4.0, ALU.mult, ALU.add))
                step(dve.tensor_tensor(eq, eq, first[:, 0:1, :].to_broadcast([P, nt, 4]), ALU.mult))
                step(dve.tensor_reduce(r1[:, :, 0], eq, AX_X, ALU.max))
                step(dve.tensor_tensor(eq, eq, bc(r1, 4), ALU.is_equal))
                eq4 = sm[:, 10, 0:4 * nt].unsqueeze(2).to_broadcast([P, 4 * nt, 4])
                grp = lambda v: v.rearrange("p t (g f) -> p (t g) f", f=4)
                step(dve.tensor_tensor(grp(sel), grp(sel), eq4, ALU.mult))
                step(dve.tensor_scalar(eq, eq, -NEG, NEG, ALU.mult, ALU.add))
                step(dve.tensor_tensor(grp(sel), grp(sel), eq4, ALU.add))
                m8 = row(12, 8)
                i8 = sm[:, 13, 0:8 * nt].bitcast(U32).rearrange("p (t e) -> p t e", e=8)
                for i in range(nt):
                    step(dve.max(m8[:, i, :], sel[:, i, :]))
                    step(dve.max_index(i8[:, i, :], m8[:, i, :], sel[:, i, :]))
                ex = sm[:, 14, 0:2 * nt].rearrange("p (k t) -> p k t", k=2)
                step(dve.tensor_copy(ex.rearrange("p k t -> p t k"), i8[:, :, 0:2]))
                picks = [pick0, row(15, NE)]
                wt = m.weight.rearrange("p (k t) -> p k t", k=2)
                for k in range(2):
                    step(dve.tensor_tensor(picks[k], iota16[:, :].unsqueeze(1).to_broadcast([P, nt, NE]),
                                           ex[:, k, :].unsqueeze(2).to_broadcast([P, nt, NE]), ALU.is_equal))
                dve.tensor_tensor(pick, picks[0], picks[1], ALU.add).then_inc(m.picked, 1)
                for k in range(2):
                    step(dve.tensor_tensor(tmp, lg, picks[k], ALU.mult))
                    step(dve.tensor_reduce(wt[:, k, :], tmp, AX_X, ALU.add))
                step(dve.tensor_tensor(r1[:, :, 0], wt[:, 0, :], wt[:, 1, :], ALU.add))
                step(dve.reciprocal(r2, r1))
                step(dve.tensor_tensor(wt, wt, r2[:, :, 0].unsqueeze(1).to_broadcast([P, 2, nt]), ALU.mult))
                vt = m.value.rearrange("p (k t) -> p k t", k=2)
                step(dve.tensor_copy(vt[:, 0, :], tokf[:, 0:nt]))
                step(dve.tensor_scalar(vt[:, 1, :], tokf[:, 0:nt], float(m.T), None, ALU.add))
                dve.wait_ge(m.pos_done, m.was["pos_done"] + 1)
                pos = row(16, NE)
                step(dve.tensor_copy(sm[:, 16:18, :].rearrange("p a n -> p (a n)")[:, 0:NE * (nt + 1)], ps[:, 0, 0:NE * (nt + 1)]))
                pl = sm[:, 18, 0:2 * nt].rearrange("p (k t) -> p k t", k=2)
                for k in range(2):
                    step(dve.tensor_tensor(tmp, pos, picks[k], ALU.mult))
                    step(dve.tensor_reduce(pl[:, k, :], tmp, AX_X, ALU.add))
                dve.scalar_tensor_tensor(out=m.addr.rearrange("p (k t) -> p k t", k=2), in0=ex, scalar=float(CAP), in1=pl,
                                         op0=ALU.mult, op1=ALU.add).then_inc(m.addr_ready, 1)
                dve.wait_ge(m.list_turned, m.was["list_turned"] + 1)
                G = m.G
                v, ge = sm[:, 19, 0:G], sm[:, 20, 0:G]
                step(dve.tensor_copy(v, ps[:, 1, 0:G]))
                half_rows(v, ge, G, GIX[:, 0:G], SIX[:, 0:G], m.T, m.lists_ready)
                list_further(m, sm[0:1, 16:18, :].rearrange("p a n -> p (a n)")[:, NE * nt:NE * (nt + 1)])

            def half_rows(v, ge, G, gix, six, T, ready):
                step(dve.tensor_scalar(ge, v, float(T), float(T), ALU.is_ge, ALU.mult))
                step(dve.tensor_tensor(ge, v, ge, ALU.subtract))
                step(dve.tensor_scalar(ge, ge, float(T - 1), 2.0, ALU.min, ALU.mult))
                step(dve.tensor_scalar(gix, ge, half[:, 0:1], None, ALU.add))
                dve.tensor_scalar(six, v, 2.0, half[:, 0:1], ALU.mult, ALU.add).then_inc(ready, 1)

            def list_further(m, total):
                F, M = m.further, m.most
                place = iota16[0:1, 0:M]
                flat = lambda n, w: sm[0:1, n:n + 4, :].rearrange("p a n -> p (a n)")[:, 0:w]
                bounds, x, upto_e = sm[0:1, 4, 0:F], sm[0:1, 5, 0:NE], sm[0:1, 6, 0:NE]
                expert, row, before = sm[0:1, 7, 0:M], sm[0:1, 8, 0:M], sm[0:1, 9, 0:M]
                over = flat(10, NE * F).rearrange("p (e k) -> p e k", k=F)
                past = flat(21, M * NE).rearrange("p (o e) -> p o e", e=NE)
                step(dve.tensor_scalar(bounds, iota16[0:1, 0:F], float(PASS), float(PASS * m.subs), ALU.mult, ALU.add))
                step(dve.tensor_tensor(over, total.unsqueeze(2).to_broadcast([1, NE, F]),
                                       bounds.unsqueeze(1).to_broadcast([1, NE, F]), ALU.is_gt))
                step(dve.tensor_reduce(x, over, AX_X, ALU.add))
                step(dve.tensor_tensor_scan(upto_e, ones[0:1, 0:NE], x, 0.0, ALU.mult, ALU.add))
                step(dve.tensor_tensor(past, upto_e.unsqueeze(1).to_broadcast([1, M, NE]),
                                       place.unsqueeze(2).to_broadcast([1, M, NE]), ALU.is_le))
                step(dve.tensor_reduce(expert, past, AX_X, ALU.add))
                step(dve.tensor_tensor(past, past, x.unsqueeze(1).to_broadcast([1, M, NE]), ALU.mult))
                step(dve.tensor_reduce(before, past, AX_X, ALU.add))
                step(dve.tensor_scalar(expert, expert, float(NE - 1), None, ALU.min))
                step(dve.scalar_tensor_tensor(out=row, in0=expert, scalar=float(CAP // PASS), in1=place,
                                              op0=ALU.mult, op1=ALU.add))
                step(dve.tensor_tensor(row, row, before, ALU.subtract))
                step(dve.tensor_scalar(row, row, float(m.subs), float(NE * CAP // PASS - 1), ALU.add, ALU.min))
                step(dve.tensor_copy(more[0:1, 0:1], upto_e[:, NE - 1:NE]))
                step(dve.tensor_copy(more[0:1, 1:1 + M], expert))
                dve.tensor_copy(more[0:1, 16:16 + M], row).then_inc(m.more_ready, 1)

            def passes_dve(m):
                def keep_xt(g, par):
                    dve.wait_ge(m.tx_done, m.was["tx_done"] + g + 1)
                    if not isinstance(g, int) or g >= 2:
                        dve.wait_ge(m.h_done, m.was["h_done"] + g - 1)
                    dve.tensor_copy(XT[:, par, :, :].rearrange("p j n -> p (j n)"), ps[:, par, :]).then_inc(m.xt_ready, 1)

                def mul(g, par):
                    dve.wait_ge(m.silu_done, m.was["silu_done"] + g + 1)
                    if not isinstance(g, int) or g >= 2:
                        dve.wait_ge(m.tu_done, m.was["tu_done"] + g - 1)
                    dve.tensor_tensor(U[:, par, :], ps[:, 2 + par, 256:512], SG[:, par, :], ALU.mult).then_inc(m.u_ready, 1)

                def keep_ut(g, par):
                    dve.wait_ge(m.tu_done, m.was["tu_done"] + g + 1)
                    if not isinstance(g, int) or g >= 2:
                        dve.wait_ge(m.y_done, m.was["y_done"] + g - 1)
                    dve.tensor_copy(UT[:, par, :, :].rearrange("p c n -> p (c n)"), ps[:, 4 + par, 0:256]).then_inc(m.ut_ready, 1)

                def body(i, last):
                    for b in range(2):
                        g = i * 2 * m.subs + b * m.subs
                        if m.subs == 2:
                            keep_xt(g + 1, 1)
                            mul(g, 0)
                            keep_ut(g, 0)
                            mul(g + 1, 1)
                            keep_ut(g + 1, 1)
                            if not (last and b == 1):
                                keep_xt(g + 2, 0)
                        else:
                            mul(g, b)
                            if not (last and b == 1):
                                keep_xt(g + 1, 1 - b)
                            keep_ut(g, b)

                keep_xt(0, 0)
                body(0, False)
                with dve.Fori(1, NE // 2 - 1) as i:
                    body(i, False)
                body(NE // 2 - 1, True)

            def further_dve(m):
                dve.wait_ge(m.more_ready, m.was["more_ready"] + 1)
                count = dve.value_load(more[0:1, 0:1], min_val=0, max_val=m.most)
                with dve.If(count > 0):
                    with dve.Fori(0, m.most) as o:
                        with dve.If(count > o):
                            dve.wait_ge(m.further_pe, after(PE_STEPS, o, "column"))
                            v, ge = ov[:, 0:1], ov[:, 1:2]
                            dve.tensor_copy(v, ps[:, 1, 0:1]).then_inc(m.further_dve, 1)
                            dve.wait_ge(m.further_dve, after(DVE_STEPS, o, "v"))
                            dve.tensor_scalar(ge, v, float(m.T), float(m.T), ALU.is_ge, ALU.mult).then_inc(m.further_dve, 1)
                            dve.wait_ge(m.further_dve, after(DVE_STEPS, o, "second"))
                            dve.tensor_tensor(ge, v, ge, ALU.subtract).then_inc(m.further_dve, 1)
                            dve.wait_ge(m.further_dve, after(DVE_STEPS, o, "token"))
                            dve.tensor_scalar(ge, ge, float(m.T - 1), 2.0, ALU.min, ALU.mult).then_inc(m.further_dve, 1)
                            dve.wait_ge(m.further_dve, after(DVE_STEPS, o, "row"))
                            dve.tensor_scalar(ogi, ge, half[:, 0:1], None, ALU.add).then_inc(m.further_dve, 1)
                            dve.tensor_scalar(osi, v, 2.0, half[:, 0:1], ALU.mult, ALU.add).then_inc(m.further_dve, 1)
                            dve.wait_ge(m.further_pe, after(PE_STEPS, o, "turned"))
                            dve.tensor_copy(XT[:, 0, :, :].rearrange("p j n -> p (j n)"), ps[:, 0, :]).then_inc(m.further_dve, 1)
                            dve.wait_ge(m.further_act, after(ACT_STEPS, o, "silu"))
                            dve.tensor_tensor(U[:, 0, :], ps[:, 2, 256:512], SG[:, 0, :], ALU.mult).then_inc(m.further_dve, 1)
                            dve.wait_ge(m.further_pe, after(PE_STEPS, o, "u_turned"))
                            dve.tensor_copy(UT[:, 0, :, :].rearrange("p c n -> p (c n)"), ps[:, 4, 0:256]).then_inc(m.further_dve, 1)

            def combine_dve(m):
                dve.wait_ge(m.g5_kept, m.was["g5_kept"] + m.nt)
                for i, t in enumerate(m.tiles):
                    y0, y1 = m.yin[i]
                    dve.wait_ge(m.y_scaled, m.was["y_scaled"] + i + 1)
                    step(dve.scalar_tensor_tensor(out=y1, in0=y1, scalar=m.weight[:, m.nt + i:m.nt + i + 1], in1=y0,
                                                  op0=ALU.mult, op1=ALU.add))
                    step(dve.tensor_tensor(y1, y1, g5[:, t // 2, :], ALU.mult))
                    dve.tensor_tensor(X[:, t, :], X[:, t, :], y1, ALU.add).then_inc(m.added, 1)

            def conv(n):
                dve.wait_ge(xr_kept, n + 1)
                x = xpad[:, n % 2]
                y = XC[:, n, :].rearrange("p (s n) -> p s n", s=2)
                step(dve.tensor_scalar(y, x[:, :, 0:256], convw[:, 0, n:n + 1], convb[:, n:n + 1], ALU.mult, ALU.add))
                for j in range(1, 4):
                    ins = dve.scalar_tensor_tensor(out=y, in0=x[:, :, j:j + 256], scalar=convw[:, j, n:n + 1], in1=y,
                                                   op0=ALU.mult, op1=ALU.add)
                    if j < 3:
                        step(ins)
                ins.then_inc(conv_done, 1)

            def scans(n):
                for d in range(2):
                    dve.wait_ge(rg_tanh, 2 * n + d + 1)
                    dve.scalar_tensor_tensor(out=RB[:, d, 2, :], in0=RB[:, d, 0, :], scalar=1.0, in1=RB[:, d, 2, :],
                                             op0=ALU.add, op1=ALU.mult).then_inc(rg_q, 1)
                for d in range(2):
                    ti, sq_, dec = RB[:, d, 1, :], RB[:, d, 2, :], RB[:, d, 3, :]
                    step(dve.scalar_tensor_tensor(out=ti, in0=ti, scalar=1.0, in1=XC[:, n, :], op0=ALU.add, op1=ALU.mult))
                    dve.wait_ge(rg_sqrt, 2 * n + d + 1)
                    step(dve.tensor_tensor(ti, ti, sq_, ALU.mult))
                    h = hfb[:, d, :]
                    dve.wait_ge(rg_q, 2 * n + 2)
                    if d == 0:
                        dve.tensor_tensor_scan(h, dec, ti, 0.0, ALU.mult, ALU.add).then_inc(rg_scan, 1)
                    else:
                        step(dve.tensor_tensor_scan(h[:, 0:256][:, ::-1], dec[:, 0:256][:, ::-1], ti[:, 0:256][:, ::-1],
                                                    0.0, ALU.mult, ALU.add))
                        dve.tensor_tensor_scan(h[:, 256:512][:, ::-1], dec[:, 256:512][:, ::-1], ti[:, 256:512][:, ::-1],
                                               h[:, 0:1], ALU.mult, ALU.add).then_inc(rg_scan, 1)
                dve.wait_ge(rg_scan, 2 * n + 2)
                step(dve.tensor_tensor(YT[:, n, :], hfb[:, 0, 256:512], hfb[:, 1, 256:512], ALU.add))
                dve.wait_ge(yb_kept, n + 1)
                ins = dve.tensor_tensor(YT[:, n, :], YT[:, n, :], YB[:, n, :], ALU.mult)
                if n == 7:
                    ins.then_inc(y_ready, 1)

            def rglru_params():
                dve.wait_ge(rg_in, 80)
                lm = lam[:, :, :].rearrange("p d k -> p (d k)")
                e, u, ln, z = (lt[:, i, :] for i in range(4))
                dve.scalar_tensor_tensor(out=e, in0=lm, scalar=-1.0, in1=lm, op0=ALU.mult, op1=ALU.min).then_inc(lam_u, 1)
                dve.wait_ge(lam_exp, 1)
                dve.tensor_scalar(u, e, 1.0, None, ALU.add).then_inc(lam_u, 1)
                dve.wait_ge(lam_ln, 1)
                step(dve.tensor_scalar(u, u, 1.0, None, ALU.subtract))
                step(dve.tensor_scalar(z, u, 0.0, None, ALU.is_equal))
                step(dve.tensor_tensor(ln, ln, z, ALU.add))
                step(dve.tensor_tensor(u, u, z, ALU.add))
                step(dve.reciprocal(u, u))
                step(dve.tensor_tensor(ln, ln, u, ALU.mult))
                step(dve.tensor_tensor(ln, ln, e, ALU.mult))
                step(dve.tensor_scalar(z, lm, -1.0, 0.0, ALU.mult, ALU.max))
                step(dve.tensor_tensor(ln, ln, z, ALU.add))
                step(dve.tensor_scalar(spl[:, :, :].rearrange("p d k -> p (d k)"), ln, 0.5 * RGLRU_C, None, ALU.mult))
                step(dve.tensor_scalar(spn[:, :, :].rearrange("p d k -> p (d k)"), ln, -0.5 * RGLRU_C, None, ALU.mult))
                rb = rbias[:, :, :, :].rearrange("p d n e -> p (d n e)")
                dve.tensor_scalar(rb, rb, 0.5, None, ALU.mult).then_inc(lam_ready, 1)

            route_dve(moes[0])
            passes_dve(moes[0])
            further_dve(moes[0])
            rglru_params()
            columns(1)
            combine_dve(moes[0])
            norm_keep(1)
            dve.memset(xpad[:, :, :, :], 0.0).then_inc(pads, 1)
            for what, n in RG_ORDER:
                if what == "x":
                    conv(n)
                elif what == "g":
                    scans(n)
            route_dve(moes[1])
            passes_dve(moes[1])
            further_dve(moes[1])
            combine_dve(moes[1])
            dve.wait_ge(gfin_in, 16)
            for i, t in enumerate(moes[1].tiles):
                dve.wait_ge(rstd_ready, 14 + i + 1)
                dve.scalar_tensor_tensor(out=moes[1].yin[i][1], in0=X[:, t, :], scalar=stat[:, 2, t:t + 1], in1=gffn,
                                         op0=ALU.mult, op1=ALU.mult).then_inc(fin_ready, 1)


def position_table(n_tokens, dim, grid_w=64, base=10000.0):
    rows = n_tokens // grid_w
    r, col = np.meshgrid(np.arange(rows, dtype=np.float32), np.arange(grid_w, dtype=np.float32), indexing="ij")
    quarter = dim // 4
    freqs = np.exp(np.float32(-np.log(base)) * np.arange(quarter, dtype=np.float32) / np.float32(quarter))
    enc = lambda p: np.concatenate([np.sin(p.reshape(-1, 1) * freqs), np.cos(p.reshape(-1, 1) * freqs)], -1)
    return np.concatenate([enc(r), enc(col)], -1).astype(np.float32)


INPUTS = ["x", "c", "ctx", "c_ctx", "w_ada", "b_ada", "g_mix", "g_ffn", "g_final", "m_w_in", "m_b_gate", "m_g_head",
          "m_w_out", "r_w_in", "r_conv_w", "r_conv_b", "r_w_gate", "r_b_gate", "r_lam", "r_w_out", "w_router",
          "b_router", "e_w1", "e_w3", "e_w2"]


def kernel(**inputs):
    import concourse.bacc as bacc
    from concourse.bass_utils import run_bass_kernel_spmd

    nc = bacc.Bacc("TRN2", target_bir_lowering=False, num_devices=1)
    arrays = {name: np.ascontiguousarray(inputs[name]) for name in INPUTS}
    arrays["pos"] = position_table(SEQ, D)
    args = {name: nc.dram_tensor("in_" + name, v.shape, F32, kind="ExternalInput").ap() for name, v in arrays.items()}
    out = nc.dram_tensor("out", (1, SEQ, D), F32, kind="ExternalOutput")
    build(nc, args, out.ap())
    r = run_bass_kernel_spmd(nc, [{"in_" + name: v for name, v in arrays.items()}], core_ids=[0])
    return r.results[0]["out"]
```

```python
from contextlib import ExitStack

import numpy as np

import concourse.bass as bass
from concourse import mybir

F32 = mybir.dt.float32
F32R = mybir.dt.float32r
U32 = mybir.dt.uint32
I32 = mybir.dt.int32
ALU = mybir.AluOpType
ACT = mybir.ActivationFunctionType
AX_X = mybir.AxisListType.X

P = 128
D = 1024
KD = D // P
SEQ = 256
TILES = 4
T_ALL = TILES * P
HEADS = 8
DQK = 64
DV = 128
DVX = DV + 1
NE = 16
DE = 512
EPS = 1e-6
NEG = -1e30
RGLRU_C = 8.0
SLOTS = 6
CHUNK = 4096
PASS = 64
CAP = 512
PAD = 1.0e6

ADA_CHUNKS = 12
HOLD = 4
STREAM0 = ([("ada0", 0, 4, None), ("ada0", 1, 5, None), ("ada0", 2, 2, None), ("ada0", 3, 3, None), ("in0", 0, 0, 1),
            ("ada0", 4, 4, None), ("ada0", 5, 5, None), ("in0", 1, 2, 3)]
           + [("ada0", j, 4 + j % 2, None) for j in range(6, 10)] + [("in0", 2, 0, 1)]
           + [("ada0", 10, 4, None), ("ada0", 11, 5, None), ("hold", 0, HOLD, None), ("in0", 3, 2, 3), ("in0", 4, 0, 1), ("in0", 5, 2, 3)]
           + [("ada1", j, (5, 0, 1, 2, 3)[j % 5], None) for j in range(ADA_CHUNKS)]
           + [("out0", 0, 1, 2), ("out0", 1, 3, 5)])
STREAM1 = [("in1", j, j, None) for j in range(5)] + [("out1", 0, 5, None), ("out1", 1, 0, None)]


def plan(stream):
    at, before, high_before, loads, last = {}, {}, {}, {}, {}
    count = [0] * SLOTS
    for n, (kind, _, slot, high) in enumerate(stream):
        at[n], before[n] = slot, last.get(slot)
        count[slot] += kind != "hold"
        loads[n] = count[slot]
        last[slot] = n
        if high is not None:
            high_before[n], last[high] = last.get(high), n
    return at, before, high_before, loads


N_MOE0 = len(STREAM0)
N_MIX1 = N_MOE0 + 3 * NE
N_MOE1 = N_MIX1 + len(STREAM1)
STREAM = (STREAM0 + [("moe0", j, j % SLOTS, None) for j in range(3 * NE)]
          + STREAM1 + [("moe1", j, (j + 1) % SLOTS, None) for j in range(3 * (NE - 1))])
SLOT_OF, BEFORE, HIGH_BEFORE, LOADS = plan(STREAM)
CHUNK_NO = {(kind, j): n for n, (kind, j, _, _) in enumerate(STREAM)}


def fwd_keys(j):
    return list(range(j + 1))


def bwd_keys(j):
    return [[0, 1], [1], [0, 1, 2, 3], [0, 1, 3]][j]


PAIRS = [[(s, j) for s in range(TILES) for j in range(TILES) if s in keys(j)] for keys in (fwd_keys, bwd_keys)]


def runs_of(pairs, s):
    js = [j for (a, j) in pairs if a == s]
    out = []
    for j in js:
        if out and out[-1][0] + out[-1][1] == j:
            out[-1][1] += 1
        else:
            out.append([j, 1])
    return [tuple(r) for r in out]


def build(nc, a, out):
    ctx = ExitStack()
    with ctx:
        def sb(name, shape, dt=F32):
            return ctx.enter_context(nc.sbuf_tensor(name, shape, dt))

        def twice(name, shape):
            guard = nc.sbuf_tensor(name, shape, F32)
            plain = guard.__enter__()
            guard.__exit__(None, None, None)
            return plain, sb(name + "_r", shape, F32R)

        def sem(name):
            return ctx.enter_context(nc.semaphore(name))

        ctx.enter_context(nc.allow_non_contiguous_dma("columns of small vectors"))

        ps = ctx.enter_context(nc.psum_tensor("ps", [P, 8, 512], F32))
        ring, ring_r = twice("ring", [P, SLOTS, CHUNK])
        X = sb("X", [P, TILES, D])
        hT, hT_r = twice("hT", [P, KD, T_ALL])
        XN, XN_r = twice("XN", [P, TILES, D])
        QK, QK_r = twice("QK", [P, 8, T_ALL])
        VR, VR_r = twice("VR", [P, TILES * HEADS * DVX])
        WR, WR_r = twice("WR", [P, 2 * 16 * P])
        modr = sb("modr", [P, 3, 512])
        ident = sb("ident", [P, P])
        masks = sb("masks", [P, 2, P])
        triu = sb("triu", [P, P])
        ones = sb("ones", [P, P])
        wrt, wrt_r = twice("wrt", [P, KD, NE])
        gcol, gcol_r = twice("gcol", [P, TILES, P])
        rrow_r = sb("rrow", [P, T_ALL], F32R)
        both_rows = wrt_r[:, :, :].rearrange("p k e -> p (k e)")[:, 0:64]
        silu_c = sb("silu_c", [P, KD, 2, 16])
        cvec = sb("cvec", [P, 2, KD])
        acol = sb("acol", [P, 2, KD])
        bcol = sb("bcol", [P, 2, KD])
        gmix = sb("gmix", [P, 2, KD])
        ghead = sb("ghead", [P, KD])
        bgate = sb("bgate", [P, 1])
        brt = sb("brt", [P, NE])
        iota16i = sb("iota16i", [P, NE], I32)
        iota16 = sb("iota16", [P, NE])
        toki = sb("toki", [P, TILES], I32)
        tokf = sb("tokf", [P, TILES])
        half = sb("half", [P, 1])
        mhalf = sb("mhalf", [P, HEADS])
        stat = sb("stat", [P, 8, TILES])
        att = sb("att", [P, 2, TILES])

        V = VR[:, :].rearrange("p (t h c) -> p t h c", t=TILES, h=HEADS)
        bada = WR[:, 2560:4096].rearrange("p (g n) -> p g n", g=3)
        wg = VR[:, 1536:2560].rearrange("p (k t d r) -> p k t d r", k=KD, t=2, d=2)
        H = XN[:, :, :].rearrange("p t (h v) -> p t h v", h=HEADS)
        qT, kT = QK[:, 0:4, :], QK[:, 4:8, :]
        O = ring[:, HOLD, :].rearrange("p (t n) -> p t n", t=TILES)
        NH = XN_r[:, :, :].rearrange("p a b -> p (a b)").rearrange("p (k n) -> p k n", k=KD)
        YH = QK_r[:, :, :]
        HL = hT_r[:, :, :]
        flat_ = lambda v: v[:, :, :].rearrange("p a b -> p (a b)")
        W = WR[:, :].rearrange("p (u s j n) -> p u s j n", u=2, s=TILES, j=TILES)
        gtmp = WR[:, 0:3072].rearrange("p (a n) -> p a n", a=6)
        gate2 = WR[:, 0:2048].rearrange("p (s n) -> p s n", s=2)
        gtmp2 = WR[:, 2048:2560]
        hs = sb("hs", [P, HEADS, TILES])
        hss_ready, hr_ready = sem("head_squares"), sem("head_roots")

        ld = [sem(f"chunk_loaded{i}") for i in range(SLOTS)]
        x_in, cv_in, pos_in = sem("x_in"), sem("cv_in"), sem("pos_in")
        bada_in, small_in = sem("bada_in"), sem("small_in")
        wg_zero, wg_in = sem("wg_zero"), sem("wg_in")
        bg_zero, bada_zero = sem("bg_zero"), sem("bada_zero")
        consts, pool_step = sem("consts"), sem("pool_step")
        dve_step, act_step = sem("dve_step"), sem("act_step")
        silu_ready, ada_done, modr_ready = sem("silu_ready"), sem("ada_done"), sem("modr_ready")
        ada_part = sem("ada_part")
        modcol_done, cols_ready = sem("modcol_done"), sem("cols_ready")
        x_ready, ss_ready, rstd_ready, xn_ready = sem("x_ready"), sem("ss_ready"), sem("rstd_ready"), sem("xn_ready")
        nt_done, nt_act, nt_dve = sem("norm_turned"), sem("norm_kept_act"), sem("norm_kept_dve")
        gate_done, proj_done, proj_kept = sem("gate_done"), sem("proj_done"), sem("proj_kept")
        gates_ready, gturn_done, gcol_ready = sem("gates_ready"), sem("gturn_done"), sem("gcol_ready")
        v_ones, lsig_ready, lsig_kept, em_ready = sem("v_ones"), sem("lsig_ready"), sem("lsig_kept"), sem("em_ready")
        s_done, r_done, d_done, e_done, p_done, o_done = (
            sem("att_scores"), sem("att_rows"), sem("att_diag"), sem("att_exp"), sem("att_prod"), sem("att_out"))
        den_ready, fin_act, fin_dve = sem("att_den"), sem("att_kept_act"), sem("att_kept_dve")
        nh_ready, nl_ready = sem("tokens_high"), sem("tokens_low")
        wh_ready, wl_ready = sem("weights_high"), sem("weights_low")
        yh_ready, yl_ready = sem("heads_high"), sem("heads_low")
        g2_done, g2_ready = sem("gate2_done"), sem("gate2_ready")
        y_ready, yt_done, yt_kept = sem("mix_ready"), sem("mix_turned"), sem("mix_kept")
        out_done, out_added = sem("out_done"), sem("out_added")
        stored = sem("stored")

        table_ready, pool_held, sp_held, rg_in = sem("table_ready"), sem("pool_held"), sem("sp_held"), sem("rg_in")

        g5 = QK[:, 0:4, :].rearrange("p a b -> p (a b)").rearrange("p (s n) -> p s n", s=2)
        gffn = WR[:, 2560:2560 + D]
        XG = VR[:, 0:1024].rearrange("p (a n) -> p a n", a=2)
        XT = VR[:, 1024:2048].rearrange("p (a j n) -> p a j n", a=2, j=4)
        YS = VR[:, 2048:3072].rearrange("p (a n) -> p a n", a=2)
        SG = VR[:, 3072:3584].rearrange("p (a n) -> p a n", a=2)
        U = VR[:, 3584:4096].rearrange("p (a n) -> p a n", a=2)
        UT = WR[:, 1024:1536].rearrange("p (a c n) -> p a c n", a=2, c=2)
        sm = WR[:, 1536:4096].rearrange("p (a n) -> p a n", n=64)
        XG_W = VR[:, 0:1024]
        XH = VR[:, 1024:2048].rearrange("p (k n) -> p k n", k=KD)
        XH_R = VR_r[:, 1024:2048].rearrange("p (k n) -> p k n", k=KD)
        XL_R = VR_r[:, 2048:3072].rearrange("p (k n) -> p k n", k=KD)
        UH_R = WR_r[:, 1024:1536].rearrange("p (c n) -> p c n", c=4)
        UL_R = gcol_r[:, :, :]
        HI_R = [t[:, :, :].rearrange("p a b -> p (a b)") for t in (hT_r, XN_r, QK_r)]
        XL = VR[:, 2048:3072].rearrange("p (k n) -> p k n", k=KD)
        YS_W = VR[:, 3072:4096]
        SG_W, U_W = WR[:, 0:512], WR[:, 512:1024]
        UH = WR[:, 1024:1536].rearrange("p (c n) -> p c n", c=4)
        UL = gcol[:, :, :]
        HI = [t[:, :, :].rearrange("p a b -> p (a b)") for t in (hT, XN, QK)]
        ASIDE = [t[:, :, :].rearrange("p a b -> p (a b)") for t in (hT, XN, QK)]
        aside_in = [sem(f"aside_in{part}") for part in range(3)]
        hi_ready, lo_ready, xh_ready, uh_ready, w1_done = sem("hi_ready"), sem("lo_ready"), sem("xh_ready"), sem("uh_ready"), sem("w1_done")
        lraw = WR[0:NE, 2560:3072]
        GIX = sm[:, 36, 0:32].bitcast(U32)
        SIX = sm[:, 36, 32:64].bitcast(U32)
        gi = sm[:, 37, 0:2].bitcast(U32)
        si = sm[:, 37, 2:4].bitcast(U32)
        slot_i = sm[:, 26:28, :].rearrange("p a n -> p (a n)").bitcast(I32)
        slot_f = sm[:, 28:30, :].rearrange("p a n -> p (a n)")
        VAL_R = WR_r[:, 1536 + 24 * 64:1536 + 25 * 64]
        pad = VR[:, 2560:2624]
        more = sb("more", [1, 32], I32)
        orow = sm[0:1, 33:35, :].rearrange("p a n -> p (a n)")
        ov = sm[:, 35, 0:8]
        ogi, osi = sm[:, 35, 8:9].bitcast(U32), sm[:, 35, 9:10].bitcast(U32)

        block = ctx.enter_context(nc.Block())

        XC = XN[:, :, :].rearrange("p a b -> p (a b)").rearrange("p (n t) -> p n t", n=8)
        YB = QK[:, 0:4, :].rearrange("p a b -> p (a b)").rearrange("p (n t) -> p n t", n=8)
        YT = QK[:, 4:8, :].rearrange("p a b -> p (a b)").rearrange("p (n t) -> p n t", n=8)
        RB = VR[:, 0:4096].rearrange("p (d a n) -> p d a n", d=2, a=4)
        xpad = WR[:, 2560:3600].rearrange("p (u s n) -> p u s n", u=2, s=2)
        hfb = WR[:, 0:1024].rearrange("p (d n) -> p d n", d=2)
        convw, convb = sb("convw", [P, 4, KD]), sb("convb", [P, KD])
        rbias, lam = sb("rbias", [P, 2, KD, 2]), sb("lam", [P, 2, KD])
        spl, spn = sb("spl", [P, 2, KD]), sb("spn", [P, 2, KD])
        lt = masks[:, 0, 0:8 * KD].rearrange("p (i n) -> p i n", i=4)
        xr_done, yb_done, rg_done = sem("xr_done"), sem("yb_done"), sem("rg_done")
        xr_kept, yb_kept, conv_done, pads = sem("xr_kept"), sem("yb_kept"), sem("conv_done"), sem("pads")
        lam_exp, lam_u, lam_ln, lam_ready = sem("lam_exp"), sem("lam_u"), sem("lam_ln"), sem("lam_ready")
        rg_tanh, rg_q, rg_sqrt, rg_scan = sem("rg_tanh"), sem("rg_q"), sem("rg_sqrt"), sem("rg_scan")
        gfin_in, fin_ready = sem("gfin_in"), sem("fin_ready")
        RG_ORDER = [("x", 0)] + [(w, n) for m in range(8) for w, n in (("x", m + 1), ("g", m), ("y", m)) if n < 8]

        MOE_SIGNALS = dict(
            gffn_in=lambda m: 16, rows_done=lambda m: 2 * m.nt, scale_kept=lambda m: m.nt, shift_kept=lambda m: m.nt,
            h_ready=lambda m: m.nt, rows_stored=lambda m: 16 * m.nt, turned=lambda m: 2 * m.nt,
            turn_kept_act=lambda m: m.nt, turn_kept_dve=lambda m: m.nt, logits_done=lambda m: 1, logits_raw=lambda m: 1, logits_kept=lambda m: 1,
            shifted=lambda m: 1, expd=lambda m: 1, picked=lambda m: 1, pos_done=lambda m: 1, addr_ready=lambda m: 1,
            filled=lambda m: 32 * m.nt, slots_listed=lambda m: 1, hot_ready=lambda m: NE, hot_used=lambda m: NE,
            lists_ready=lambda m: 1, gi_ready=lambda m: m.G, si_ready=lambda m: m.G, tx_done=lambda m: m.G * m.turns,
            xt_ready=lambda m: m.G * m.turns, half_done=lambda m: NE, h_done=lambda m: m.G, silu_done=lambda m: m.G,
            u_ready=lambda m: m.G, tu_done=lambda m: m.G, ut_ready=lambda m: m.G * m.turns, y_done=lambda m: m.G,
            ys_ready=lambda m: m.G, g5_done=lambda m: m.nt, g5_kept=lambda m: m.nt, y_in=lambda m: 32,
            y_scaled=lambda m: m.nt, added=lambda m: m.nt, more_ready=lambda m: 1, passes_over=lambda m: 1, gathered=lambda m: 8 * m.G, scattered=lambda m: 8 * m.G)
        SEVERAL = dict(gathered=2, scattered=2, y_in=TILES)
        moe_sems = {name: [sem(f"{name}{i}") for i in range(SEVERAL[name])] if name in SEVERAL else sem(name)
                    for name in MOE_SIGNALS}

        class Moe:
            def __init__(self, l, tiles, slots, base):
                self.l, self.tiles, self.slots, self.base = l, tiles, slots, base
                self.nt = len(tiles)
                self.T = P * self.nt
                self.norms = (4, 12)[l]
                self.outs = (0, 8)[l]
                self.first, self.in_ring = (0, NE) if l == 0 else (1, NE - 1)
                self.G = NE
                self.turns = slots // PASS
                hot = VR_r[:, 0:4096].rearrange("p (b t n) -> p b t n", t=self.nt, n=P)
                self.hot = [hot[:, b] for b in range(4096 // (P * self.nt))]
                self.hrows = nc.dram_tensor(f"hrows{l}", [self.T, D], F32, kind="Internal").ap()
                self.yrows = nc.dram_tensor(f"yrows{l}", [2 * self.T, D], F32, kind="Internal").ap()
                self.table = nc.dram_tensor(f"table{l}", [NE * CAP, 1], F32, kind="Internal").ap()
                self.hhalf = self.hrows.rearrange("t (h n) -> (t h) n", h=2)
                self.yhalf = self.yrows.rearrange("t (h n) -> (t h) n", h=2)
                self.was = {name: (per(moes[0]) if l else 0) for name, per in MOE_SIGNALS.items()}
                self.gffn_in = moe_sems["gffn_in"]
                self.rows_done = moe_sems["rows_done"]
                self.scale_kept = moe_sems["scale_kept"]
                self.shift_kept = moe_sems["shift_kept"]
                self.h_ready = moe_sems["h_ready"]
                self.rows_stored = moe_sems["rows_stored"]
                self.turned = moe_sems["turned"]
                self.turn_kept_act = moe_sems["turn_kept_act"]
                self.turn_kept_dve = moe_sems["turn_kept_dve"]
                self.logits_done = moe_sems["logits_done"]
                self.logits_raw = moe_sems["logits_raw"]
                self.logits_kept = moe_sems["logits_kept"]
                self.shifted = moe_sems["shifted"]
                self.expd = moe_sems["expd"]
                self.picked = moe_sems["picked"]
                self.pos_done = moe_sems["pos_done"]
                self.addr_ready = moe_sems["addr_ready"]
                self.filled = moe_sems["filled"]
                self.slots_listed = moe_sems["slots_listed"]
                self.hot_ready = moe_sems["hot_ready"]
                self.hot_used = moe_sems["hot_used"]
                self.lists_ready = moe_sems["lists_ready"]
                self.gi_ready = moe_sems["gi_ready"]
                self.si_ready = moe_sems["si_ready"]
                self.tx_done = moe_sems["tx_done"]
                self.xt_ready = moe_sems["xt_ready"]
                self.half_done = moe_sems["half_done"]
                self.h_done = moe_sems["h_done"]
                self.silu_done = moe_sems["silu_done"]
                self.u_ready = moe_sems["u_ready"]
                self.tu_done = moe_sems["tu_done"]
                self.ut_ready = moe_sems["ut_ready"]
                self.y_done = moe_sems["y_done"]
                self.ys_ready = moe_sems["ys_ready"]
                self.g5_done = moe_sems["g5_done"]
                self.g5_kept = moe_sems["g5_kept"]
                self.y_in = moe_sems["y_in"]
                self.y_scaled = moe_sems["y_scaled"]
                self.added = moe_sems["added"]
                self.more_ready = moe_sems["more_ready"]
                self.passes_over = moe_sems["passes_over"]
                self.gathered = moe_sems["gathered"]
                self.scattered = moe_sems["scattered"]

                (self.further_pe, self.further_act, self.further_dve, self.further_dma, self.further_loaded) = (
                    [sem(f"{name}{l}") for name in FURTHER_SIGNALS])
                self.further = (self.T - slots) // PASS
                self.most = max(min(n * self.further, (2 * self.T - n * (slots - PASS + 1)) // PASS)
                                for n in range(1, NE + 1))
                self.ab = (ring[:, HOLD, :] if l == 0 else QK[:, 0:4, :].rearrange("p a b -> p (a b)")).rearrange(
                    "p (v s n) -> p v s n", v=2, s=self.nt // 2)
                self.yin = [(XN[:, 2 * i, :], XN[:, 2 * i + 1, :]) if i < 2 else
                            (VR[:, 2048 * (i - 2):2048 * (i - 2) + D], VR[:, 2048 * (i - 2) + D:2048 * (i - 2) + 2 * D])
                            for i in range(self.nt)]
                self.addr = sm[:, 30, 0:2 * self.nt].bitcast(U32)
                self.value = sm[:, 31, 0:2 * self.nt]
                self.weight = sm[:, 32, 0:2 * self.nt]

        FURTHER_SIGNALS = ("further_pe", "further_act", "further_dve", "further_dma", "further_loaded")
        PE_STEPS = ("column", "turned", "up", "u_turned", "down")
        ACT_STEPS = ("silu", "y_kept")
        DVE_STEPS = ("v", "second", "token", "row", "gather_index", "scatter_index", "xt", "u", "ut")

        def after(steps, o, name):
            return len(steps) * o + steps.index(name) + 1

        moes = []
        moes.append(Moe(0, [0, 1, 2, 3], 128, N_MOE0))
        moes.append(Moe(1, [2, 3], 64, N_MOE1))
        def slot(n):
            return ring[:, SLOT_OF[n], :]

        def slot_r(n):
            return ring_r[:, SLOT_OF[n], :]

        def high_r(n):
            return ring_r[:, STREAM[n][3], :]

        def cols_of(w, n, cb):
            v = w.rearrange("(k p) n -> p k n", p=P)
            d = slot(n).rearrange("p (k n) -> p k n", k=KD)
            return [(d[:, 4 * h:4 * h + 4, :], v[:, 4 * h:4 * h + 4, 512 * cb:512 * cb + 512]) for h in range(2)]

        def ada_of(l, n, j):
            g, kk = j // 4, j % 4
            v = a["w_ada"][l].rearrange("(k p) n -> p k n", p=P)
            d = slot(n).rearrange("p (k n) -> p k n", k=2)
            return [(d[:, h, :], v[:, 2 * kk + h, 2048 * g:2048 * g + 2048]) for h in range(2)]

        def expert_of(l, e, dst, part):
            if part < 2:
                d = dst.rearrange("p (k w n) -> p k w n", k=4, w=2)
                return [(d[:, :, w, :], a[name][l, e].rearrange("(k p) n -> p k n", p=P)[:, 4 * part:4 * part + 4, :])
                        for w, name in enumerate(("e_w1", "e_w3"))]
            d = dst.rearrange("p (c n) -> p c n", c=4)
            v = a["e_w2"][l, e].rearrange("(c p) n -> p c n", p=P)
            return [(d[:, 2 * h:2 * h + 2, :], v[:, 2 * h:2 * h + 2, :]) for h in range(2)]

        m_in, r_in = a["m_w_in"][0], a["r_w_in"][0]
        r_gate = a["r_w_gate"][0].rearrange("d n p e -> p d n e")

        def used(n):
            kind, j = STREAM[n][:2]
            if kind == "hold":
                return moes[0].h_ready, TILES
            if kind in ("ada0", "ada1"):
                l, g, kk = int(kind[3]), j // 4, j % 4
                return (ada_done, 3 * l + g + 1) if kk == 3 else (ada_part, 9 * l + 3 * g + kk + 1)
            if kind == "in0":
                return proj_done, 4 * j + 4
            if kind == "out0":
                return out_done, 2 * TILES - 1 + j
            if kind == "in1":
                return [(xr_done, 4), (yb_done, 4), (rg_done, 16), (xr_done, 8), (yb_done, 8)][j]
            if kind == "out1":
                return out_done, 3 * TILES - 1 + j
            for m in moes:
                if m.base <= n < m.base + 3 * m.in_ring:
                    e, part = m.first + (n - m.base) // 3, (n - m.base) % 3
                    return [(m.half_done, m.was["half_done"] + e + 1), (m.h_done, m.was["h_done"] + e + 1),
                            (m.y_done, m.was["y_done"] + e + 1)][part]
            raise ValueError(n)

        @block.sync
        def _(sp):
            def load(n, parts):
                if BEFORE[n] is not None:
                    sp.wait_ge(*used(BEFORE[n]))
                for dst, src in parts:
                    sp.dma_start(dst, src).then_inc(ld[SLOT_OF[n]], 16)

            def load_named(stream):
                for kind, j, _, _ in stream:
                    if kind == "hold":
                        continue
                    n = CHUNK_NO[kind, j]
                    if kind == "in1" and j == 2:
                        sp.wait_ge(moes[0].y_in[TILES - 1], 32)
                    if kind in ("ada0", "ada1"):
                        load(n, ada_of(int(kind[3]), n, j))
                    elif kind == "in0":
                        load(n, cols_of(m_in, n, j))
                    elif kind == "in1" and j == 2:
                        d = slot(n).rearrange("p (d n e) -> p d n e", d=2, n=8)
                        load(n, [(d[:, i], r_gate[:, i]) for i in range(2)])
                    elif kind == "in1":
                        load(n, cols_of(r_in, n, {0: 2, 1: 0, 3: 3, 4: 1}[j]))
                    else:
                        load(n, cols_of(a["m_w_out" if kind == "out0" else "r_w_out"][0], n, j))

            for t in range(TILES):
                src = a["ctx"][0] if t < 2 else a["x"][0]
                sp.dma_start(X[:, t, :], src[P * (t % 2):P * (t % 2) + P, :]).then_inc(x_in, 16)
            for t in range(2):
                sp.dma_start(XN[:, 2 + t, :], a["pos"][P * t:P * t + P, :]).then_inc(pos_in, 16)
            load_named(STREAM0)

            def experts(m):
                def static(r):
                    for part in range(3):
                        load(m.base + 3 * r + part, expert_of(m.l, m.first + r, slot(m.base + 3 * r + part), part))

                static(0)
                static(1)
                if m.l == 1:
                    sp.wait_ge(m.logits_done, m.was["logits_done"] + 1)
                    sp.wait_ge(m.rows_stored, m.was["rows_stored"] + 16 * m.nt)
                    sp.wait_ge(m.h_ready, m.was["h_ready"] + m.nt)
                    for part in range(3):
                        if part == 2:
                            sp.wait_ge(m.gathered[0], m.was["gathered"] + 16)
                        for dst, src in expert_of(m.l, 0, ASIDE[part], part):
                            sp.dma_start(dst, src).then_inc(aside_in[part], 16)
                with sp.Fori(1, m.in_ring // 2) as i:
                    for j in range(6):
                        b, part = j // 3, j % 3
                        k = m.first + 2 * (i - 1) + b + 1
                        if part == 0:
                            sp.wait_ge(m.half_done, m.was["half_done"] + k)
                        elif part == 1:
                            sp.wait_ge(m.h_done, m.was["h_done"] + k)
                        else:
                            sp.wait_ge(m.y_done, m.was["y_done"] + k)
                        for dst, src in expert_of(m.l, 2 * i + m.first + b, slot(m.base + j), part):
                            sp.dma_start(dst, src).then_inc(ld[SLOT_OF[m.base + j]], 16)
                if m.in_ring % 2:
                    static(m.in_ring - 1)

            def experts_again(m):
                sp.wait_ge(m.more_ready, m.was["more_ready"] + 1)
                count = sp.value_load(more[0:1, 0:1], min_val=0, max_val=m.most)
                with sp.If(count > 0):
                    with sp.Fori(0, m.most) as o:
                        with sp.If(count > o):
                            sp.wait_ge(m.h_done, m.was["h_done"] + m.G)
                            sp.wait_ge(m.y_done, m.was["y_done"] + m.G)
                            e = sp.value_load(more[0:1, bass.ds(o + 1, 1)], min_val=0, max_val=NE - 1)
                            for part in range(3):
                                for dst, src in expert_of(m.l, e, ring[:, part, :], part):
                                    sp.dma_start(dst, src).then_inc(m.further_loaded, 16)
                            sp.wait_ge(m.further_pe, after(PE_STEPS, o, "down"))
                            sp.sem_inc(sp_held, 1)
            experts(moes[0])
            experts_again(moes[0])
            load_named(STREAM1)
            experts(moes[1])
            experts_again(moes[1])
            for t in range(2):
                sp.wait_ge(stored, 16 * (t + 1))

        def use(pe, n, i=0):
            pe.wait_ge(ld[SLOT_OF[n]], 32 * LOADS[n] + 32 * i)

        def split_high(act, kind, j):
            n = CHUNK_NO[kind, j]
            use(act, n)
            if HIGH_BEFORE[n] is not None:
                act.wait_ge(*used(HIGH_BEFORE[n]))
            act.activation(high_r(n), slot(n), ACT.Copy).then_inc(wh_ready, 1)

        def split_low(eng, kind, j, n):
            c = CHUNK_NO[kind, j]
            eng.wait_ge(wh_ready, n + 1)
            eng.tensor_tensor(slot_r(c), slot(c), high_r(c), ALU.subtract).then_inc(wl_ready, 1)

        @block.gpsimd
        def _(pool):
            steps = [0]

            def step(ins):
                steps[0] += 1
                ins.then_inc(pool_step, 1)
                pool.wait_ge(pool_step, steps[0])

            pool.memset(bada, 0.0).then_inc(bada_zero, 1)
            step(pool.memset(wg, 0.0))
            pool.memset(bgate[:, :], 0.0).then_inc(bg_zero, 1)
            step(pool.memset(ident[:, :], 0.0))
            step(pool.affine_select(out=ident[:, :], in_=ident[:, :], compare_op=ALU.not_equal, fill=1.0,
                                    base=0, pattern=[[-1, P]], channel_multiplier=1))
            step(pool.memset(masks[:, :, :], 0.0))
            step(pool.affine_select(out=masks[:, 0, :], in_=masks[:, 0, :], compare_op=ALU.is_ge, fill=NEG,
                                    base=0, pattern=[[1, P]], channel_multiplier=-1))
            step(pool.affine_select(out=masks[:, 1, :], in_=masks[:, 1, :], compare_op=ALU.is_ge, fill=NEG,
                                    base=0, pattern=[[-1, P]], channel_multiplier=1))
            step(pool.memset(ones[:, :], 1.0))
            step(pool.affine_select(out=triu[:, :], in_=ones[:, :], compare_op=ALU.is_ge, fill=0.0,
                                    base=-1, pattern=[[1, P]], channel_multiplier=-1))
            step(pool.iota(iota16i[:, :], pattern=[[1, NE]], base=0, channel_multiplier=0))
            step(pool.iota(toki[:, :], pattern=[[P, TILES]], base=0, channel_multiplier=1))
            step(pool.memset(pad, PAD))
            for m in moes:
                pool.dma_start(m.table.rearrange("(p n) o -> p (n o)", p=P), pad).then_inc(table_ready, 16)
            pool.wait_ge(table_ready, 32)
            pool.memset(mhalf[:, :], -0.5).then_inc(consts, 1)
            pool.wait_ge(consts, 1)

            def rstd(n, tiles):
                for i, t in enumerate(tiles):
                    pool.wait_ge(ss_ready, n + i + 1)
                    step(pool.tensor_scalar(stat[:, 1, t:t + 1], stat[:, 0, t:t + 1], 1.0 / D, EPS, ALU.mult, ALU.add))
                    pool.tensor_tensor(stat[:, 2, t:t + 1], stat[:, 1, t:t + 1], mhalf[:, t:t + 1], ALU.pow
                                       ).then_inc(rstd_ready, 1)

            def held():
                pool.sem_inc(pool_held, 1)

            def gather(m, g, par):
                if not isinstance(g, int) or g >= 2:
                    pool.wait_ge(m.tx_done, m.was["tx_done"] + g - 1)
                    held()
                pool.tensor_copy(gi[:, par:par + 1], GIX[:, bass.ds(g, 1)]).then_inc(m.gi_ready, 1)
                pool.wait_ge(m.gi_ready, m.was["gi_ready"] + g + 1)
                held()
                pool.indirect_dma_start(XG[:, par, :], None, m.hhalf,
                                        bass.IndirectOffsetOnAxis(ap=gi[:, par:par + 1], axis=0)
                                        ).then_inc(m.gathered[par], 16)

            def gather_wide(m, g, par):
                if not isinstance(g, int) or g >= 1:
                    pool.wait_ge(m.tx_done, m.was["tx_done"] + 2 * g)
                    held()
                pool.tensor_copy(gi[:, par:par + 1], GIX[:, bass.ds(g, 1)]).then_inc(m.gi_ready, 1)
                pool.wait_ge(m.gi_ready, m.was["gi_ready"] + g + 1)
                held()
                pool.indirect_dma_start(XG_W, None, m.hrows, bass.IndirectOffsetOnAxis(ap=gi[:, par:par + 1], axis=0)
                                        ).then_inc(m.gathered[par], 16)

            def scatter_wide(m, g, par, at):
                if not isinstance(at, int) or at >= 1:
                    pool.wait_ge(m.scattered[par], m.was["scattered"] + 16 * at)
                    held()
                pool.tensor_copy(si[:, par:par + 1], SIX[:, bass.ds(g, 1)]).then_inc(m.si_ready, 1)
                pool.wait_ge(m.si_ready, m.was["si_ready"] + g + 1)
                pool.wait_ge(m.ys_ready, m.was["ys_ready"] + g + 1)
                held()
                pool.indirect_dma_start(m.yrows, bass.IndirectOffsetOnAxis(ap=si[:, par:par + 1], axis=0), YS_W, None,
                                        bounds_check=2 * m.T - 1, oob_is_err=False).then_inc(m.scattered[par], 16)

            def scatter(m, g, par, at):
                if not isinstance(at, int) or at >= 1:
                    pool.wait_ge(m.scattered[par], m.was["scattered"] + 16 * at)
                    held()
                pool.tensor_copy(si[:, par:par + 1], SIX[:, bass.ds(g, 1)]).then_inc(m.si_ready, 1)
                pool.wait_ge(m.si_ready, m.was["si_ready"] + g + 1)
                pool.wait_ge(m.ys_ready, m.was["ys_ready"] + g + 1)
                held()
                pool.indirect_dma_start(m.yhalf, bass.IndirectOffsetOnAxis(ap=si[:, par:par + 1], axis=0),
                                        YS[:, par, :], None, bounds_check=4 * m.T - 1, oob_is_err=False
                                        ).then_inc(m.scattered[par], 16)

            def route_pool(m):
                rstd(m.norms, m.tiles)
                pool.wait_ge(m.scale_kept, m.was["scale_kept"] + m.nt)
                pool.iota(slot_i, pattern=[[0, P // m.slots], [1, m.slots]], base=0, channel_multiplier=0
                          ).then_inc(m.slots_listed, 1)

            def fill_table(m):
                pool.wait_ge(m.addr_ready, m.was["addr_ready"] + 1)
                for r in range(2 * m.nt):
                    pool.indirect_dma_start(m.table, bass.IndirectOffsetOnAxis(ap=m.addr[:, r:r + 1], axis=0),
                                            m.value[:, r:r + 1], None).then_inc(m.filled, 16)

            def passes_pool(m):
                pool.wait_ge(m.lists_ready, m.was["lists_ready"] + 1)
                pool.wait_ge(m.rows_stored, m.was["rows_stored"] + 16 * m.nt)
                lag = 2 if m.l == 0 else 3
                get, put = (gather_wide, scatter_wide) if m.l == 0 else (gather, scatter)
                for g in range(4):
                    get(m, g, g % 2)
                    if g == lag - 1:
                        fill_table(m)
                    if g >= lag:
                        put(m, g - lag, (g - lag) % 2, (g - lag) // 2)
                with pool.Fori(2, NE // 2) as i:
                    for r in range(2):
                        get(m, 2 * i + r, r)
                        put(m, 2 * i + r - lag, (r - lag) % 2, i + (r - lag) // 2)
                for g in range(m.G - lag, m.G):
                    put(m, g, g % 2, g // 2)

            def further_pool(m):
                pool.wait_ge(m.filled, m.was["filled"] + 32 * m.nt)
                pool.wait_ge(m.scattered[0], m.was["scattered"] + 8 * m.G)
                pool.wait_ge(m.scattered[1], m.was["scattered"] + 8 * m.G)
                pool.wait_ge(m.more_ready, m.was["more_ready"] + 1)
                count = pool.value_load(more[0:1, 0:1], min_val=0, max_val=m.most)
                rows = m.table.rearrange("(r s) o -> r (o s)", s=PASS)
                with pool.If(count > 0):
                    with pool.Fori(0, m.most) as o:
                        with pool.If(count > o):
                            r = pool.value_load(more[0:1, bass.ds(o + 16, 1)], min_val=0, max_val=NE * CAP // PASS - 1)
                            for h in range(2):
                                pool.dma_start(orow[:, PASS * h:PASS * h + PASS], rows[bass.ds(r, 1), :]).then_inc(m.further_dma, 16)
                            pool.wait_ge(m.further_dve, after(DVE_STEPS, o, "scatter_index"))
                            held()
                            pool.indirect_dma_start(XG[:, 0, :], None, m.hhalf, bass.IndirectOffsetOnAxis(ap=ogi, axis=0)
                                                    ).then_inc(m.further_dma, 16)
                            pool.wait_ge(m.further_act, after(ACT_STEPS, o, "y_kept"))
                            held()
                            pool.indirect_dma_start(m.yhalf, bass.IndirectOffsetOnAxis(ap=osi, axis=0), YS[:, 0, :], None,
                                                    bounds_check=4 * m.T - 1, oob_is_err=False).then_inc(m.further_dma, 16)
                            pool.wait_ge(m.further_dma, 64 * o + 64)
                            held()
                pool.sem_inc(m.passes_over, 1)

            rstd(0, range(TILES))
            for h in range(HEADS):
                pool.wait_ge(hss_ready, h + 1)
                step(pool.tensor_scalar(hs[:, h], hs[:, h], 1.0 / DV, EPS, ALU.mult, ALU.add))
                pool.tensor_tensor(hs[:, h], hs[:, h], mhalf[:, 0:TILES], ALU.pow).then_inc(hr_ready, 1)
                if h in (3, 4):
                    split_low(pool, "out0", h - 3, 6 + h - 3)
            route_pool(moes[0])
            passes_pool(moes[0])
            further_pool(moes[0])
            rstd(8, range(TILES))
            route_pool(moes[1])
            passes_pool(moes[1])
            further_pool(moes[1])
            rstd(14, moes[1].tiles)

        def keep_fwd(act, u):
            h = u // 2
            act.wait_ge(den_ready, u + 1)
            for j in range(TILES):
                ins = act.activation(H[:, j, h, :], ps[:, 5 + j // 2, DVX * (j % 2):DVX * (j % 2) + DV], ACT.Copy,
                                     scale=att[:, u % 2, j:j + 1])
            ins.then_inc(fin_act, 1)

        @block.scalar
        def _(act):
            act.dma_start(cvec[:, 0, :], a["c_ctx"].rearrange("(k p) -> p k", p=P)).then_inc(cv_in, 16)
            act.dma_start(cvec[:, 1, :], a["c"][0].rearrange("(k p) -> p k", p=P)).then_inc(cv_in, 16)
            act.wait_ge(bada_zero, 1)
            for l in range(2):
                for s in range(2):
                    act.dma_start(bada[16 * s + 8 * l:P:32], a["b_ada"][l].rearrange("(g q n) -> q g n", g=3, q=4)
                                  ).then_inc(bada_in, 16)
            for l in range(2):
                act.dma_start(gmix[:, l, :], a["g_mix"][l].rearrange("(k p) -> p k", p=P)).then_inc(small_in, 16)
            act.dma_start(ghead[:, :], a["m_g_head"][0].rearrange("(k p) -> p k", p=P)).then_inc(small_in, 16)
            act.dma_start(brt[:, :], a["b_router"].rearrange("(o e) -> o e", o=1).to_broadcast([P, NE])).then_inc(small_in, 16)
            act.dma_start(convw[:, :, :], a["r_conv_w"][0].rearrange("j (k p) -> p j k", p=P)).then_inc(rg_in, 16)
            act.dma_start(convb[:, :], a["r_conv_b"][0].rearrange("(k p) -> p k", p=P)).then_inc(rg_in, 16)
            act.dma_start(lam[:, :, :], a["r_lam"][0].rearrange("d (k p) -> p d k", p=P)).then_inc(rg_in, 16)
            for d in range(2):
                act.dma_start(rbias[:, d, :, :], a["r_b_gate"][0][d].rearrange("n (e p) -> p n e", p=P)).then_inc(rg_in, 16)
            act.wait_ge(pool_step, 1)
            act.wait_ge(bg_zero, 1)
            wgv = m_in[:, 3072:3104].rearrange("(k p) (g h) -> p k g h", p=P, g=4)
            for t in range(2):
                for d in range(2):
                    act.dma_start(wg[:, :, t, d, 0:HEADS], wgv[:, :, 2 * d + t, :]).then_inc(wg_in, 16)
                    act.dma_start(bgate[64 * t + 32 * d:64 * t + 32 * d + HEADS, :],
                                  a["m_b_gate"][0][2 * d + t].rearrange("(h o) -> h o", o=1)).then_inc(wg_in, 16)

            steps = [0]

            def step(ins):
                steps[0] += 1
                ins.then_inc(act_step, 1)
                act.wait_ge(act_step, steps[0])

            def gate2_act(base, tiles):
                for b in range(tiles):
                    s, cb = 2 - tiles // 2 + b // 2, b % 2
                    act.wait_ge(g2_done, base + b + 1)
                    act.activation(gate2[:, s, 512 * cb:512 * cb + 512], ps[:, 3 + b % 2, :], ACT.Copy).then_inc(g2_ready, 1)

            act.wait_ge(cv_in, 32)
            act.activation(cvec[:, :, :], cvec[:, :, :], ACT.Silu).then_inc(silu_ready, 1)

            def square(t, scratch):
                act.activation(scratch, X[:, t, :], ACT.Square, accum_out=stat[:, 0, t:t + 1]).then_inc(ss_ready, 1)

            def normalize(l, t):
                act.wait_ge(rstd_ready, 8 * l + t + 1)
                act.activation(XN[:, t, :], X[:, t, :], ACT.Copy, scale=stat[:, 2, t:t + 1]).then_inc(xn_ready, 1)

            def keep_turned(l, s):
                act.wait_ge(cols_ready, l + 1)
                for kp in (0, 2):
                    act.wait_ge(nt_done, 8 * l + 4 * s + kp + 1)
                    for kk in range(2):
                        k = 2 * kp + kk
                        ins = act.activation(hT[:, k, 256 * s:256 * s + 256], ps[:, 4 + kp, 256 * kk:256 * kk + 256],
                                             ACT.Identity, bias=bcol[:, s, k:k + 1], scale=acol[:, s, k:k + 1])
                    ins.then_inc(nt_act, 1)

            for t in range(TILES):
                act.wait_ge(x_ready, t + 1)
                square(t, XN[:, t, :])
            for t in range(TILES):
                normalize(0, t)
            for s in range(2):
                keep_turned(0, s)
            act.wait_ge(nt_dve, 4)
            act.wait_ge(nt_act, 4)
            act.wait_ge(nt_done, 8)
            act.activation(flat_(XN_r), flat_(hT), ACT.Copy).then_inc(nh_ready, 1)
            split_high(act, "in0", 0)

            tm, em = gtmp[0:64, 4, :], gtmp[64:128, 5, :]
            act.wait_ge(lsig_ready, 1)
            step(act.activation(tm, tm, ACT.Exp))
            act.activation(tm, tm, ACT.Ln, bias=1.0).then_inc(lsig_kept, 1)
            for g in range(24):
                if g == 4:
                    act.wait_ge(em_ready, 2)
                    act.activation(em, em, ACT.Exp).then_inc(gates_ready, 1)
                act.wait_ge(proj_done, g + 1)
                if g < 4:
                    ins = act.activation(qT[:, g, :], ps[:, g % 4, :], ACT.Copy, scale=float(DQK) ** -0.5)
                elif g < 8:
                    ins = act.activation(kT[:, g - 4, :], ps[:, g % 4, :], ACT.Copy)
                elif g >= 16:
                    cb, t = (g - 16) // 4, g % 4
                    if g == 16:
                        act.wait_ge(*used(BEFORE[CHUNK_NO["hold", 0]]))
                    ins = act.activation(O[:, t, 512 * cb:512 * cb + 512], ps[:, g % 4, :], ACT.Sigmoid)
                else:
                    cb, t = (g - 8) // 4, g % 4
                    if g == 8:
                        act.wait_ge(gate_done, 1)
                    ins = act.activation(V[:, t, 4 * cb:4 * cb + 4, 0:DV],
                                         ps[:, g % 4, :].rearrange("p (h v) -> p h v", h=4), ACT.Copy)
                ins.then_inc(proj_kept, 1)
                if g % 4 == 1 and g < 20:
                    split_high(act, "in0", g // 4 + 1)

            def head_squares(h):
                act.wait_ge(fin_dve, h + 1)
                if h >= 1:
                    act.wait_ge(hss_ready, h)
                for t in range(TILES):
                    ins = act.activation(QK[:, 0, P * t:P * t + P], H[:, t, h, :], ACT.Square, accum_out=hs[:, h, t:t + 1])
                ins.then_inc(hss_ready, 1)

            for u in range(16):
                h, d = u // 2, u % 2
                if u >= 2 and u % 2 == 0:
                    keep_fwd(act, u - 2)
                    if u >= 6:
                        for h_ in ([0, 1] if u == 6 else [u // 2 - 2]):
                            head_squares(h_)
                act.wait_ge(d_done, u + 1)
                wd = W[:, u % 2].rearrange("p s j n -> p (s j) n")[:, 0:16:5, :]
                act.activation(wd, wd, ACT.Exp)
                todo = [(s, j, c) for s in range(TILES)
                        for j, c in runs_of([q for q in PAIRS[d] if q[0] != q[1]], s)]
                for s, j, c in todo:
                    ins = act.activation(W[:, u % 2, s, j:j + c, :], ps[:, 4 - u % 2, P * j:P * (j + c)].rearrange("p (j n) -> p j n", n=P),
                                         ACT.Exp, bias=gcol[:, s, 32 * d + h:32 * d + h + 1])
                ins.then_inc(e_done, 1)
                if u in (10, 12):
                    split_high(act, "out0", (u - 10) // 2)
            keep_fwd(act, 14)
            act.wait_ge(r_done, 16)
            act.dma_start(wrt[:, :, :], a["w_router"].rearrange("(k p) e -> p k e", p=P)).then_inc(small_in, 16)
            head_squares(6)
            head_squares(7)
            act.wait_ge(o_done, 16)
            gate2_act(0, TILES)
            for t in range(TILES):
                act.wait_ge(yt_kept, 2 * t + 2)
                act.activation(YH[:, :, P * t:P * t + P], hT[:, :, P * t:P * t + P], ACT.Copy).then_inc(yh_ready, 1)

            def route_act(m):
                l, t0 = m.l, m.tiles[0]
                act.wait_ge(y_ready, HEADS + KD * l)
                act.dma_start(gffn, a["g_ffn"][l].rearrange("(o n) -> o n", o=1).to_broadcast([P, D])).then_inc(m.gffn_in, 16)
                act.wait_ge(out_added, m.outs + 2)
                square(t0, XN[:, t0, :])
                for b in range(m.nt):
                    s, cb = b // 2, b % 2
                    act.wait_ge(m.rows_done, m.was["rows_done"] + 2 * b + 2)
                    act.activation(m.ab[:, 1, s, 512 * cb:512 * cb + 512], ps[:, 4, :], ACT.Copy).then_inc(m.shift_kept, 1)
                for i in range(m.nt):
                    act.wait_ge(m.h_ready, m.was["h_ready"] + i + 1)
                    act.dma_start(m.hrows[P * i:P * i + P, :], XN[:, t0 + i, :]).then_inc(m.rows_stored, 16)
                    if i + 1 < m.nt:
                        act.wait_ge(out_added, m.outs + 2 * i + 4)
                        square(t0 + i + 1, XN[:, t0 + i + 1, :])
                    act.wait_ge(m.turned, m.was["turned"] + 2 * i + 1)
                    act.activation(hT[:, 0:4, P * (t0 + i):P * (t0 + i) + P], ps[:, 5, :].rearrange("p (k n) -> p k n", k=4),
                                   ACT.Copy).then_inc(m.turn_kept_act, 1)
                act.wait_ge(m.shifted, m.was["shifted"] + 1)
                lg = sm[:, 0, 0:NE * m.nt]
                act.activation(lg, lg, ACT.Exp).then_inc(m.expd, 1)

            def passes_act(m):
                def silu(g, par):
                    act.wait_ge(m.h_done, m.was["h_done"] + g + 1)
                    if not isinstance(g, int) or g >= 2:
                        act.wait_ge(m.u_ready, m.was["u_ready"] + g - 1)
                    act.activation(SG[:, par, :], ps[:, 2 + par, 0:256], ACT.Silu).then_inc(m.silu_done, 1)

                def keep_y(g, par, at):
                    act.wait_ge(m.y_done, m.was["y_done"] + g + 1)
                    if not isinstance(at, int) or at >= 1:
                        act.wait_ge(m.scattered[par], m.was["scattered"] + 16 * at)
                    act.activation(YS[:, par, :], ps[:, 6 + par, :], ACT.Copy).then_inc(m.ys_ready, 1)

                def body(i):
                    for b in range(2):
                        silu(2 * i + b, b)
                        keep_y(2 * i + b, b, i)
                body(0)
                with act.Fori(1, NE // 2) as i:
                    body(i)

            def passes_wide_act(m):
                def high(i, b, part):
                    n = m.base + 3 * b + part
                    use(act, n, i)
                    if not isinstance(i, int) or 2 * i + b >= 1:
                        act.wait_ge((m.half_done, m.h_done, m.y_done)[part], 2 * i + b)
                    act.activation(HI_R[part], slot(n), ACT.Copy).then_inc(hi_ready, 1)

                def tokens_high(i, b, piece):
                    act.wait_ge(m.tx_done, 4 * i + 2 * b + piece + 1)
                    act.activation(XH_R[:, 4 * piece:4 * piece + 4, :].rearrange("p k n -> p (k n)"),
                                   ps[:, piece, :], ACT.Copy).then_inc(xh_ready, 1)

                def body(i, last):
                    for b in range(2):
                        g = 2 * i + b
                        ni, nb = (i, 1) if b == 0 else (i + 1, 0)
                        more_come = not (last and b == 1)
                        if more_come:
                            high(ni, nb, 0)
                        act.wait_ge(w1_done, g + 1)
                        act.activation(SG_W, ps[:, 2, :], ACT.Silu).then_inc(m.silu_done, 1)
                        if more_come:
                            tokens_high(ni, nb, 0)
                        act.wait_ge(m.tu_done, g + 1)
                        for c in (0, 2):
                            act.activation(UH_R[:, c:c + 2, :].rearrange("p c n -> p (c n)"),
                                           ps[:, 4 + c // 2, 0:2 * P], ACT.Copy).then_inc(uh_ready, 1)
                        if more_come:
                            tokens_high(ni, nb, 1)
                            high(ni, nb, 1)
                        act.wait_ge(m.y_done, g + 1)
                        if not isinstance(g, int) or g >= 1:
                            act.wait_ge(m.scattered[1 - b], 16 * i + (16 if b else 0))
                        act.activation(YS_W[:, 0:512], ps[:, 6, :], ACT.Copy)
                        act.activation(YS_W[:, 512:1024], ps[:, 7, :], ACT.Copy).then_inc(m.ys_ready, 1)
                        if more_come:
                            high(ni, nb, 2)

                act.wait_ge(m.logits_done, 1)
                high(0, 0, 0)
                act.wait_ge(m.rows_stored, 16 * m.nt)
                high(0, 0, 1)
                act.wait_ge(m.h_ready, m.nt)
                high(0, 0, 2)
                for piece in range(2):
                    tokens_high(0, 0, piece)
                body(0, False)
                with act.Fori(1, NE // 2 - 1) as i:
                    body(i, False)
                body(NE // 2 - 1, True)

            def rglru_act():
                for what, n in RG_ORDER:
                    if what == "x":
                        act.wait_ge(xr_done, n + 1)
                        act.wait_ge(pads, 1)
                        if n >= 2:
                            act.wait_ge(conv_done, n - 1)
                        act.activation(xpad[:, n % 2, :, 2:258], ps[:, n % 2, :].rearrange("p (s n) -> p s n", s=2), ACT.Copy
                                       ).then_inc(xr_kept, 1)
                    elif what == "y":
                        act.wait_ge(yb_done, n + 1)
                        act.activation(YB[:, n, :], ps[:, 2 + n % 2, 0:256], ACT.Gelu_apprx_tanh).then_inc(yb_kept, 1)
                    else:
                        act.wait_ge(lam_ready, 1)
                        for d in range(2):
                            act.wait_ge(rg_done, 2 * n + d + 1)
                            if n >= 1:
                                act.wait_ge(rg_scan, 2 * (n - 1) + d + 1)
                            for e in range(2):
                                ins = act.activation(RB[:, d, e, :], ps[:, 4 + 2 * d + e, :], ACT.Tanh,
                                                     bias=rbias[:, d, n, e:e + 1], scale=0.5)
                            step(ins)
                            act.activation(RB[:, d, 3, :], RB[:, d, 0, :], ACT.Exp, bias=spn[:, d, n:n + 1],
                                           scale=spn[:, d, n:n + 1])
                            step(act.activation(RB[:, d, 2, :], RB[:, d, 0, :], ACT.Tanh, bias=spl[:, d, n:n + 1],
                                                scale=spl[:, d, n:n + 1]))
                            act.activation(RB[:, d, 0, :], RB[:, d, 3, :], ACT.Square).then_inc(rg_tanh, 1)
                        for d in range(2):
                            act.wait_ge(rg_q, 2 * n + d + 1)
                            act.activation(RB[:, d, 2, :], RB[:, d, 2, :], ACT.Sqrt, scale=0.25).then_inc(rg_sqrt, 1)

            def further_act(m):
                act.wait_ge(m.more_ready, m.was["more_ready"] + 1)
                count = act.value_load(more[0:1, 0:1], min_val=0, max_val=m.most)
                with act.If(count > 0):
                    with act.Fori(0, m.most) as o:
                        with act.If(count > o):
                            act.wait_ge(m.further_pe, after(PE_STEPS, o, "up"))
                            act.activation(SG[:, 0, :], ps[:, 2, 0:256], ACT.Silu).then_inc(m.further_act, 1)
                            act.wait_ge(m.further_pe, after(PE_STEPS, o, "down"))
                            act.activation(YS[:, 0, :], ps[:, 6, :], ACT.Copy).then_inc(m.further_act, 1)

            def combine_act(m):
                ns = m.nt // 2
                for b in range(2 * ns):
                    s, cb = 2 - ns + b // 2, b % 2
                    act.wait_ge(m.g5_done, m.was["g5_done"] + b + 1)
                    act.activation(g5[:, s, 512 * cb:512 * cb + 512], ps[:, 3 + b % 2, :], ACT.Copy).then_inc(m.g5_kept, 1)
                act.wait_ge(m.passes_over, m.was["passes_over"] + 1)
                for i in range(m.nt):
                    for k in range(2):
                        act.dma_start(m.yin[i][k], m.yrows[m.T * k + P * i:m.T * k + P * i + P, :]).then_inc(m.y_in[i], 16)
                for i in range(m.nt):
                    act.wait_ge(m.y_in[i], m.was["y_in"] + 32)
                    y0 = m.yin[i][0]
                    act.activation(y0, y0, ACT.Copy, scale=m.weight[:, i:i + 1]).then_inc(m.y_scaled, 1)
                    if i >= 1:
                        act.wait_ge(m.added, m.was["added"] + i)
                        square(m.tiles[i - 1], m.yin[i - 1][0])
                    if i == 2:
                        normalize(1, 0)
                        normalize(1, 1)
                if m.l == 0:
                    keep_turned(1, 0)
                act.wait_ge(m.added, m.was["added"] + m.nt)
                square(m.tiles[m.nt - 1], m.yin[m.nt - 1][0])
                if m.l == 0:
                    normalize(1, 2)
                    normalize(1, 3)
                    keep_turned(1, 1)

            route_act(moes[0])
            passes_wide_act(moes[0])
            further_act(moes[0])
            act.wait_ge(lam_u, 1)
            act.activation(lt[:, 0], lt[:, 0], ACT.Exp).then_inc(lam_exp, 1)
            act.wait_ge(lam_u, 2)
            act.activation(lt[:, 2, :], lt[:, 1, :], ACT.Ln).then_inc(lam_ln, 1)
            combine_act(moes[0])
            rglru_act()
            gate2_act(4, 2)
            route_act(moes[1])
            passes_act(moes[1])
            further_act(moes[1])
            act.wait_ge(moes[1].ys_ready, moes[1].was["ys_ready"] + moes[1].G)
            act.dma_start(gffn, a["g_final"].rearrange("(o n) -> o n", o=1).to_broadcast([P, D])).then_inc(gfin_in, 16)
            combine_act(moes[1])
            for i in range(2):
                act.wait_ge(fin_ready, i + 1)
                act.dma_start(out[0, P * i:P * i + P, :], moes[1].yin[i][1]).then_inc(stored, 16)

        @block.tensor
        def _(pe):
            def ada(l, j, bank):
                g, kk = j // 4, j % 4
                c = CHUNK_NO[f"ada{l}", j]
                pe.wait_ge(silu_ready, 2 + l)
                use(pe, c)
                w = slot(c).rearrange("p (k q n) -> p k q n", k=2, q=4)
                for k2 in range(2):
                    k = 2 * kk + k2
                    for q in range(4):
                        ins = pe.matmul(ps[32 * q:32 * q + 32, bank, :], silu_c[:, k, :, :].rearrange("p s r -> p (s r)"),
                                        w[:, k2, q, :], start=(k == 0), stop=(k == KD - 1))
                ins.then_inc(ada_done if kk == 3 else ada_part, 1)

            def modcol(l):
                pe.wait_ge(modr_ready, 1 if l == 0 else 6)
                pe.wait_ge(consts, 1)
                for c in range(4):
                    ins = pe.transpose(ps[:, 3, P * c:P * c + P], modr[:, 0, P * c:P * c + P], ident[:, :])
                ins.then_inc(modcol_done, 1)

            def norm_turn(l):
                for b in range(8):
                    s, kp = b // 4, b % 4
                    pe.wait_ge(xn_ready, TILES * l + 2 * s + 2)
                    if b >= 4:
                        pe.wait_ge(nt_act if b % 2 == 0 else nt_dve, 4 * l + (b - 4) // 2 + 1)
                    for kk in range(2):
                        for t in range(2):
                            k = 2 * kp + kk
                            ins = pe.transpose(ps[:, 4 + b % 4, 256 * kk + P * t:256 * kk + P * t + P],
                                               XN[:, 2 * s + t, P * k:P * k + P], ident[:, :])
                    ins.then_inc(nt_done, 1)

            for j in range(4):
                ada(0, j, 0)
            modcol(0)
            norm_turn(0)

            pe.wait_ge(nt_act, 4)
            pe.wait_ge(nt_dve, 4)
            pe.wait_ge(wg_in, 128)
            for k in range(KD):
                for t in range(2):
                    ins = pe.matmul(ps[64 * t:64 * t + 64, 4, :], wg[:, k, t, :, :].rearrange("p d r -> p (d r)"),
                                    hT[:, k, :], start=(k == 0), stop=(k == KD - 1))
            ins.then_inc(gate_done, 1)
            def rows(u):
                r = 32 * (u % 2) + u // 2
                if u >= 2:
                    pe.wait_ge(e_done, u - 1)
                pe.matmul(ps[:, 4 - u % 2, :], both_rows[:, r:r + 1].to_broadcast([P, P]), rrow_r[:, :],
                          start=True, stop=True).then_inc(r_done, 1)

            for j in (4, 5):
                ada(0, j, 5)
            for g in range(24):
                if g == 0:
                    pe.wait_ge(nh_ready, 1)
                if g >= 4:
                    pe.wait_ge(proj_kept, g - 3)
                elif g == 3:
                    pe.wait_ge(cols_ready, 1)
                cb = g // 4
                c = CHUNK_NO["in0", cb]
                if g % 4 == 0:
                    pe.wait_ge(wh_ready, cb + 1)
                w_high, w_low = [v.rearrange("p (k n) -> p k n", k=KD) for v in (high_r(c), slot_r(c))]
                cols = slice(P * (g % 4), P * (g % 4) + P)
                for i, (x, w) in enumerate([(NH, w_high), (HL, w_high), (NH, w_low)]):
                    if g == 0 and i == 1:
                        pe.wait_ge(nl_ready, 1)
                    if g % 4 == 0 and i == 2:
                        pe.wait_ge(wl_ready, cb + 1)
                    for k in range(KD):
                        l_, r_ = (w[:, k, cols], x[:, k, :]) if g < 8 else (x[:, k, cols], w[:, k, :])
                        ins = pe.matmul(ps[:, g % 4, :], l_, r_, start=(k == 0 and i == 0), stop=(k == KD - 1 and i == 2))
                ins.then_inc(proj_done, 1)
                if g in (0, 1, 3, 4, 6, 7):
                    j = 6 + (0, 1, 3, 4, 6, 7).index(g)
                    ada(0, j, 5 + (j - 4) // 4)
                if g == 16:
                    pe.wait_ge(gates_ready, 1)
                    for t in range(TILES):
                        ins = pe.transpose(ps[:, 7, P * t:P * t + P], gtmp[:, 5, P * t:P * t + P], ident[:, :])
                    ins.then_inc(gturn_done, 1)
                if g == 22:
                    pe.wait_ge(gcol_ready, 1)
                    rows(0)

            def scores(h):
                p0 = 64 * (h % 2)
                for s in range(TILES):
                    o = ps[:, s, :] if s < 2 else ps[:, 2, 256 * (s - 2):256 * (s - 2) + 256]
                    j0 = 0 if s < 2 else 256
                    ins = pe.matmul(o, kT[p0:p0 + 64, h // 2, P * s:P * s + P], qT[p0:p0 + 64, h // 2, j0:T_ALL],
                                    start=True, stop=True)
                ins.then_inc(s_done, 1)

            pe.wait_ge(proj_kept, 24)
            scores(0)
            pe.wait_ge(v_ones, 1)
            rows(1)
            for u in range(16):
                h, d = u // 2, u % 2
                pe.wait_ge(p_done, u + 1)
                if d == 1 and h + 1 < HEADS:
                    scores(h + 1)
                if u >= 1:
                    pe.wait_ge(fin_act if (u - 1) % 2 == 0 else fin_dve, (u - 1) // 2 + 1)
                for j in range(TILES):
                    keys = (fwd_keys if d == 0 else bwd_keys)(j)
                    for s in keys:
                        ins = pe.matmul(ps[:, 5 + j // 2, DVX * (j % 2):DVX * (j % 2) + DVX], W[:, u % 2, s, j, :],
                                        V[:, s, h, :], start=(s == keys[0]), stop=(s == keys[-1]))
                ins.then_inc(o_done, 1)
                if u + 2 < 16:
                    rows(u + 2)
                if u < ADA_CHUNKS:
                    if u % 4 == 0:
                        pe.wait_ge(modr_ready, 3 + u // 4)
                    ada(1, u, 7)

            def bcast(l, col, s, bank):
                r = 32 * (col % 4) + 16 * s + 8 * l
                return pe.matmul(ps[:, bank, :], ident[:, r:r + 1].to_broadcast([P, P]), modr[:, col // 4, :],
                                 start=True, stop=True)

            pe.wait_ge(e_done, 16)
            pe.wait_ge(modr_ready, 6)
            for b in range(4):
                if b >= 2:
                    pe.wait_ge(g2_ready, b - 1)
                bcast(0, 4 + b % 2, b // 2, 3 + b % 2).then_inc(g2_done, 1)

            for t in range(TILES):
                pe.wait_ge(y_ready, HEADS)
                for b in range(2):
                    g = 2 * t + b
                    if g >= 3:
                        pe.wait_ge(yt_kept, g - 2)
                    for kk in range(4):
                        k = 4 * b + kk
                        ins = pe.transpose(ps[:, 5 + g % 3, P * kk:P * kk + P], XN[:, t, P * k:P * k + P], ident[:, :])
                    ins.then_inc(yt_done, 1)
            def route_pe(m, kind):
                nt, t0 = m.nt, m.tiles[0]

                def out_piece(i, cb):
                    g, c = 2 * i + cb, CHUNK_NO[kind, cb]
                    if g >= 3:
                        pe.wait_ge(out_added, m.outs + g - 2)
                    pe.wait_ge(yh_ready, i + 1)
                    pe.wait_ge(wh_ready, 6 + cb + 1)
                    w_high, w_low = [v.rearrange("p (k n) -> p k n", k=KD) for v in (high_r(c), slot_r(c))]
                    for n, (y, w) in enumerate([(YH, w_high), (YH, w_low), (HL, w_high)]):
                        if n == 1:
                            pe.wait_ge(wl_ready, 6 + cb + 1)
                        if n == 2:
                            pe.wait_ge(yl_ready, i + 1)
                        for k in range(KD):
                            ins = pe.matmul(ps[:, g % 3, :], y[:, k, P * i:P * i + P], w[:, k, :],
                                            start=(n == 0 and k == 0), stop=(n == 2 and k == KD - 1))
                    ins.then_inc(out_done, 1)

                def out_blocks(g, blocks):
                    i, c = g // 2, CHUNK_NO[kind, g % 2]
                    w = slot(c).rearrange("p (k n) -> p k n", k=KD)
                    for k in blocks:
                        if g == 0:
                            pe.wait_ge(y_ready, HEADS + k + 1)
                        ins = pe.matmul(ps[:, g % 3, :], YT[:, k, P * i:P * i + P], w[:, k, :],
                                        start=(k == 0), stop=(k == KD - 1))
                    if k == KD - 1:
                        ins.then_inc(out_done, 1)

                def rows_of_both():
                    pe.wait_ge(g2_ready, (4, 6)[m.l])
                    for b in range(nt):
                        s, cb = 2 - nt // 2 + b // 2, b % 2
                        if b >= 1:
                            pe.wait_ge(m.scale_kept, m.was["scale_kept"] + b)
                        bcast(m.l, 2 * 4 + cb, s, 3).then_inc(m.rows_done, 1)
                        if b >= 1:
                            pe.wait_ge(m.shift_kept, m.was["shift_kept"] + b)
                        bcast(m.l, 2 * 3 + cb, s, 4).then_inc(m.rows_done, 1)

                def turn_h(i):
                    pe.wait_ge(m.h_ready, m.was["h_ready"] + i + 1)
                    for b in range(2):
                        if i >= 1:
                            pe.wait_ge(m.turn_kept_dve if b else m.turn_kept_act, m.was["turn_kept_act"] + i)
                        for kk in range(4):
                            k = 4 * b + kk
                            ins = pe.transpose(ps[:, 5 + b, P * kk:P * kk + P], XN[:, t0 + i, P * k:P * k + P], ident[:, :])
                        ins.then_inc(m.turned, 1)

                def logits(i):
                    pe.wait_ge(m.turn_kept_act, m.was["turn_kept_act"] + i + 1)
                    pe.wait_ge(m.turn_kept_dve, m.was["turn_kept_dve"] + i + 1)
                    pe.wait_ge(small_in, 80)
                    for k in range(KD):
                        ins = pe.matmul(ps[0:NE, 7, P * i:P * i + P], wrt[:, k, :], hT[:, k, P * (t0 + i):P * (t0 + i) + P],
                                        start=(k == 0), stop=(k == KD - 1))
                    return ins

                if m.l == 1:
                    for cb in range(2):
                        use(pe, CHUNK_NO[kind, cb])
                    pe.wait_ge(xr_kept, KD)
                    pe.wait_ge(yb_kept, KD - 1)
                    for g in range(3):
                        out_blocks(g, range(KD - 1))
                    pe.wait_ge(yb_kept, KD)
                    pe.wait_ge(rg_tanh, 2 * KD)
                    for b in range(2):
                        bcast(1, 4 + b, 1, 3 + b).then_inc(g2_done, 1)
                    for g in range(2):
                        out_blocks(g, [KD - 1])
                    rows_of_both()
                    out_blocks(2, [KD - 1])
                    pe.wait_ge(out_added, m.outs + 1)
                    out_blocks(3, range(KD))
                    turn_h(0)
                for i in range(nt if m.l == 0 else 0):
                    for cb in range(2):
                        out_piece(i, cb)
                    if i == 0:
                        rows_of_both()
                    if i >= 1:
                        turn_h(i - 1)
                    if i >= 2:
                        logits(i - 2)
                logits(nt - 2)
                turn_h(nt - 1)
                logits(nt - 1).then_inc(m.logits_raw, 1)
                pe.wait_ge(m.logits_kept, m.was["logits_kept"] + 1)
                for i in range(nt):
                    ins = pe.transpose(ps[:, 1, NE * i:NE * i + NE], lraw[:, P * i:P * i + P], ident[0:NE, 0:NE])
                ins.then_inc(m.logits_done, 1)
                pe.wait_ge(m.picked, m.was["picked"] + 1)
                both = sm[:, 3, 0:NE * m.nt].rearrange("p (t e) -> p t e", e=NE)
                pe.matmul(ps[:, 0, 0:NE * m.nt], triu[:, :], sm[:, 3, 0:NE * m.nt], start=True, stop=False)
                for j in range(m.nt - 1):
                    later = m.nt - 1 - j
                    ins = pe.matmul(ps[:, 0, NE * (j + 1):NE * m.nt].rearrange("p (t e) -> p t e", e=NE), ones[:, :],
                                    both[:, j:j + 1, :].to_broadcast([P, later, NE]), start=False, stop=(later == 1))
                ins.then_inc(m.pos_done, 1)
                for j in range(m.nt):
                    pe.matmul(ps[:, 2, 0:NE], ones[:, :], both[:, j, :], start=(j == 0), stop=(j == m.nt - 1))
                for e in range(NE):
                    pe.wait_ge(m.hot_ready, m.was["hot_ready"] + e + 1)
                    for t in range(m.nt):
                        ins = pe.matmul(ps[:, 1, 2 * e:2 * e + 2], m.hot[e % len(m.hot)][:, t, :],
                                        VAL_R[:, NE * t + e:NE * t + e + 1].to_broadcast([P, 2]),
                                        start=(t == 0), stop=(t == m.nt - 1))
                    ins.then_inc(m.hot_used, 1)

            def up_half(par, h, chunk):
                w = chunk.rearrange("p (k w n) -> p k w n", k=4, w=2)
                for j in range(4):
                    for oh in range(2):
                        ins = pe.matmul(ps[64 * oh:64 * oh + 64, 2 + par, :].rearrange("p (w n) -> p w n", w=2),
                                        XT[:, par, j, 64 * h:64 * h + 64], w[:, j, :, 256 * oh:256 * oh + 256],
                                        start=(h == 0 and j == 0), stop=(h == 1 and j == 3))
                return ins

            def down_all(par, chunk):
                w = chunk.rearrange("p (c n) -> p c n", c=4)
                for kc in range(4):
                    for oh in range(2):
                        ins = pe.matmul(ps[64 * oh:64 * oh + 64, 6 + par, :],
                                        UT[:, par, kc % 2, 64 * (kc // 2):64 * (kc // 2) + 64],
                                        w[:, kc, 512 * oh:512 * oh + 512], start=(kc == 0), stop=(kc == 3))
                return ins

            def passes_wide_pe(m):
                def turn(i, b, piece):
                    g = 2 * i + b
                    pe.wait_ge(m.gathered[b], 16 * i + 16)
                    if not isinstance(g, int) or g >= 1:
                        pe.wait_ge(m.xt_ready, 2 * g)
                    for j in range(4):
                        k = 4 * piece + j
                        ins = pe.transpose(ps[:, piece, P * j:P * j + P], XG_W[:, P * k:P * k + P], ident[:, :])
                    ins.then_inc(m.tx_done, 1)

                def product(bank, blocks, first, last, low_at):
                    for n in range(3):
                        if n == 2 and low_at is not None:
                            pe.wait_ge(lo_ready, low_at)
                        for i, (high, low, w_high, w_low) in enumerate(blocks):
                            x, w = [(high, w_high), (low, w_high), (high, w_low)][n]
                            ins = pe.matmul(ps[:, bank, :], x, w, start=(first and n == 0 and i == 0),
                                            stop=(last and n == 2 and i == len(blocks) - 1))
                    return ins

                def up(i, b, part):
                    g = 2 * i + b
                    if part == 0:
                        pe.wait_ge(m.xt_ready, 2 * g + 2)
                    pe.wait_ge(hi_ready, 3 * g + part + 1)
                    halves = [v.rearrange("p (k w n) -> p k w n", k=4, w=2) for v in (HI_R[part], slot_r(m.base + 3 * b + part))]
                    for w in range(2):
                        ins = product(2 + w, [(XH_R[:, 4 * part + j, :], XL_R[:, 4 * part + j, :], halves[0][:, j, w, :],
                                               halves[1][:, j, w, :]) for j in range(4)], part == 0, part == 1,
                                      3 * g + part + 1 if w == 0 else None)
                        if part and w == 0:
                            ins.then_inc(w1_done, 1)
                    ins.then_inc(m.h_done if part else m.half_done, 1)

                def turn_u(g):
                    pe.wait_ge(m.u_ready, g + 1)
                    for c in range(4):
                        ins = pe.transpose(ps[:, 4 + c // 2, P * (c % 2):P * (c % 2) + P], U_W[:, P * c:P * c + P], ident[:, :])
                    ins.then_inc(m.tu_done, 1)

                def down(i, b):
                    g = 2 * i + b
                    pe.wait_ge(lo_ready, 3 * g + 3)
                    if not isinstance(g, int) or g >= 1:
                        pe.wait_ge(m.ys_ready, g)
                    halves = [v.rearrange("p (c o n) -> p c o n", c=4, o=2) for v in (HI_R[2], slot_r(m.base + 3 * b + 2))]
                    for c in (0, 2):
                        pe.wait_ge(m.ut_ready, 2 * g + c // 2 + 1)
                        for o in range(2):
                            ins = product(6 + o, [(UH_R[:, cc, :], UL_R[:, cc, :], halves[0][:, cc, o, :],
                                                   halves[1][:, cc, o, :]) for cc in (c, c + 1)], c == 0, c == 2, None)
                    ins.then_inc(m.y_done, 1)

                def body(i, last):
                    for b in range(2):
                        ni, nb = (i, 1) if b == 0 else (i + 1, 0)
                        more_come = not (last and b == 1)
                        up(i, b, 0)
                        up(i, b, 1)
                        if more_come:
                            turn(ni, nb, 0)
                        turn_u(2 * i + b)
                        if more_come:
                            turn(ni, nb, 1)
                        down(i, b)

                turn(0, 0, 0)
                turn(0, 0, 1)
                body(0, False)
                with pe.Fori(1, NE // 2 - 1) as i:
                    body(i, False)
                body(NE // 2 - 1, True)

            def passes_pe(m):
                def turn(g, par, at):
                    pe.wait_ge(m.gathered[par], m.was["gathered"] + 16 + 16 * at)
                    if not isinstance(g, int) or g >= 2:
                        pe.wait_ge(m.xt_ready, m.was["xt_ready"] + g - 1)
                    for j in range(4):
                        ins = pe.transpose(ps[:, par, P * j:P * j + P], XG[:, par, P * j:P * j + P], ident[:, :])
                    ins.then_inc(m.tx_done, 1)

                def up(g, par, h, chunk, i, sig):
                    if h == 0:
                        pe.wait_ge(m.xt_ready, m.was["xt_ready"] + g + 1)
                        if not isinstance(g, int) or g >= 2:
                            pe.wait_ge(m.u_ready, m.was["u_ready"] + g - 1)
                    up_half(par, h, weights(h, chunk, i)).then_inc(sig, 1)

                def turn_u(g, par):
                    pe.wait_ge(m.u_ready, m.was["u_ready"] + g + 1)
                    if not isinstance(g, int) or g >= 2:
                        pe.wait_ge(m.ut_ready, m.was["ut_ready"] + g - 1)
                    for c in range(2):
                        ins = pe.transpose(ps[:, 4 + par, P * c:P * c + P], U[:, par, P * c:P * c + P], ident[:, :])
                    ins.then_inc(m.tu_done, 1)

                def down(g, par, chunk, i):
                    pe.wait_ge(m.ut_ready, m.was["ut_ready"] + g + 1)
                    if not isinstance(g, int) or g >= 2:
                        pe.wait_ge(m.ys_ready, m.was["ys_ready"] + g - 1)
                    down_all(par, weights(2, chunk, i)).then_inc(m.y_done, 1)

                def weights(part, chunk, i):
                    if chunk is None:
                        pe.wait_ge(aside_in[part], 32)
                        return ASIDE[part]
                    use(pe, chunk + part, i)
                    return slot(chunk + part)

                def one(g, par, chunk, i, after_next):
                    up(g, par, 0, chunk, i, m.half_done)
                    up(g, par, 1, chunk, i, m.h_done)
                    if after_next is not None:
                        turn(g + 1, 1 - par, after_next)
                    turn_u(g, par)
                    down(g, par, chunk, i)

                def body(i):
                    for b in range(2):
                        one(2 * i + 1 + b, 1 - b, m.base + 3 * b, i, i + 1)

                turn(0, 0, 0)
                one(0, 0, None, 0, 0)
                body(0)
                with pe.Fori(1, m.in_ring // 2) as i:
                    body(i)
                one(NE - 1, 1, m.base + 3 * (m.in_ring - 1), 0, None)

            def further_pe(m):
                pe.wait_ge(m.more_ready, m.was["more_ready"] + 1)
                pe.wait_ge(m.ys_ready, m.was["ys_ready"] + m.G)
                count = pe.value_load(more[0:1, 0:1], min_val=0, max_val=m.most)
                with pe.If(count > 0):
                    with pe.Fori(0, m.most) as o:
                        with pe.If(count > o):
                            pe.wait_ge(m.further_dma, 64 * o + 32)
                            pe.matmul(ps[:, 1, 0:1], orow, ones[0:1, 0:1], start=True, stop=True).then_inc(m.further_pe, 1)
                            pe.wait_ge(m.further_dma, 64 * o + 48)
                            for j in range(4):
                                ins = pe.transpose(ps[:, 0, P * j:P * j + P], XG[:, 0, P * j:P * j + P], ident[:, :])
                            ins.then_inc(m.further_pe, 1)
                            pe.wait_ge(m.further_dve, after(DVE_STEPS, o, "xt"))
                            pe.wait_ge(m.further_loaded, 96 * o + 96)
                            for h in range(2):
                                ins = up_half(0, h, ring[:, h, :])
                            ins.then_inc(m.further_pe, 1)
                            pe.wait_ge(m.further_dve, after(DVE_STEPS, o, "u"))
                            for c in range(2):
                                ins = pe.transpose(ps[:, 4, P * c:P * c + P], U[:, 0, P * c:P * c + P], ident[:, :])
                            ins.then_inc(m.further_pe, 1)
                            pe.wait_ge(m.further_dve, after(DVE_STEPS, o, "ut"))
                            down_all(0, ring[:, 2, :]).then_inc(m.further_pe, 1)

            def combine_pe(m):
                ns = m.nt // 2
                pe.wait_ge(m.u_ready, m.was["u_ready"] + m.G)
                pe.wait_ge(m.ut_ready, m.was["ut_ready"] + m.G * m.turns)
                for b in range(2 * ns):
                    s, cb = 2 - ns + b // 2, b % 2
                    if b >= 2:
                        pe.wait_ge(m.g5_kept, m.was["g5_kept"] + b - 1)
                    bcast(m.l, 2 * 5 + cb, s, 3 + b % 2).then_inc(m.g5_done, 1)

            def rglru_pe():
                gates = slot(N_MIX1 + 2).rearrange("p (d n e q) -> p d n e q", d=2, n=8, e=2)
                for what, n in RG_ORDER:
                    hi = n // 4
                    if what == "g":
                        if n == 0:
                            use(pe, N_MIX1 + 2)
                        pe.wait_ge(conv_done, n + 1)
                        for d in range(2):
                            if n >= 1:
                                pe.wait_ge(rg_tanh, 2 * (n - 1) + d + 1)
                            for e in range(2):
                                ins = pe.matmul(ps[:, 4 + 2 * d + e, :], gates[:, d, n, e, :], XC[:, n, :],
                                                start=True, stop=True)
                            ins.then_inc(rg_done, 1)
                        continue
                    c = N_MIX1 + (0, 3)[hi] if what == "x" else N_MIX1 + (1, 4)[hi]
                    if n % 4 == 0:
                        use(pe, c)
                    w = slot(c).rearrange("p (k n) -> p k n", k=KD)[:, :, P * (n % 4):P * (n % 4) + P]
                    kept, done = (xr_kept, xr_done) if what == "x" else (yb_kept, yb_done)
                    if n >= 2:
                        pe.wait_ge(kept, n - 1)
                    o, t0 = (ps[:, n % 2, :], 0) if what == "x" else (ps[:, 2 + n % 2, 0:256], 256)
                    for k in range(KD):
                        ins = pe.matmul(o, w[:, k, :], hT[:, k, t0:T_ALL], start=(k == 0), stop=(k == KD - 1))
                    ins.then_inc(done, 1)

            route_pe(moes[0], "out0")
            passes_wide_pe(moes[0])
            further_pe(moes[0])
            combine_pe(moes[0])
            pe.wait_ge(moes[0].ys_ready, moes[0].G)
            pe.wait_ge(moes[0].g5_kept, 4)
            modcol(1)
            norm_turn(1)
            pe.wait_ge(nt_act, 8)
            pe.wait_ge(nt_dve, 8)
            pe.wait_ge(cols_ready, 2)
            rglru_pe()
            route_pe(moes[1], "out1")
            passes_pe(moes[1])
            further_pe(moes[1])
            combine_pe(moes[1])

        @block.vector
        def _(dve):
            steps = [0]

            def step(ins):
                steps[0] += 1
                ins.then_inc(dve_step, 1)
                dve.wait_ge(dve_step, steps[0])

            dve.wait_ge(silu_ready, 1)
            step(dve.memset(silu_c[:, :, :, :], 0.0))
            dve.tensor_copy(silu_c[:, :, :, 0:8].rearrange("p k s r -> p s k r"),
                            cvec[:, :, :].unsqueeze(3).to_broadcast([P, 2, KD, 8])).then_inc(silu_ready, 1)
            dve.wait_ge(x_in, 64)
            for t in range(TILES):
                if t < 2:
                    dve.tensor_copy(X[:, t, 0:1], X[:, t, 0:1]).then_inc(x_ready, 1)
                else:
                    dve.wait_ge(pos_in, 32)
                    dve.tensor_tensor(X[:, t, :], X[:, t, :], XN[:, t, :], ALU.add).then_inc(x_ready, 1)
            dve.wait_ge(consts, 1)
            step(dve.tensor_copy(iota16[:, :], iota16i[:, :]))
            step(dve.tensor_copy(tokf[:, :], toki[:, :]))
            step(dve.tensor_scalar(half[:, :], tokf[:, 0:1], 64.0, None, ALU.is_ge))

            def modulation(l, g, bank):
                dve.wait_ge(ada_done, 3 * l + g + 1)
                dve.tensor_tensor(modr[:, g, :], ps[:, bank, :], modr[:, g, :] if l else bada[:, g, :], ALU.add
                                  ).then_inc(modr_ready, 1)

            def columns(l):
                dve.wait_ge(small_in, 64)
                dve.wait_ge(modcol_done, l + 1)
                m = ps[:, 3, :].rearrange("p (c q r) -> p q c r", c=4, q=4)
                for s in range(2):
                    dve.tensor_copy(bcol[:, s, :].rearrange("p (q c) -> p q c", q=2), m[:, 0:2, :, 16 * s + 8 * l])
                    ins = dve.scalar_tensor_tensor(
                        out=acol[:, s, :].rearrange("p (q c) -> p q c", q=2), in0=m[:, 2:4, :, 16 * s + 8 * l],
                        scalar=1.0, in1=gmix[:, l, :].rearrange("p (q c) -> p q c", q=2),
                        op0=ALU.add, op1=ALU.mult)
                ins.then_inc(cols_ready, 1)

            def norm_keep(l):
                dve.wait_ge(cols_ready, l + 1)
                for b in range(1, 8, 2):
                    s, kp = b // 4, b % 4
                    dve.wait_ge(nt_done, 8 * l + b + 1)
                    for kk in range(2):
                        k = 2 * kp + kk
                        ins = dve.tensor_scalar(hT[:, k, 256 * s:256 * s + 256], ps[:, 4 + b % 4, 256 * kk:256 * kk + 256],
                                                acol[:, s, k:k + 1], bcol[:, s, k:k + 1], ALU.mult, ALU.add)
                    ins.then_inc(nt_dve, 1)

            dve.wait_ge(bada_in, 64)
            modulation(0, 0, 0)
            columns(0)
            norm_keep(0)

            dve.wait_ge(gate_done, 1)
            dve.wait_ge(nh_ready, 1)
            dve.tensor_tensor(flat_(hT_r), flat_(hT), flat_(XN_r), ALU.subtract).then_inc(nl_ready, 1)
            split_low(dve, "in0", 0, 0)

            ig, lf, mm, bb, tm, ce = (gtmp[:, i, :] for i in range(6))
            for t, dst in ((0, ig), (1, lf)):
                for d in range(2):
                    r = 64 * t + 32 * d
                    o = dst[32 * d:32 * d + 32].rearrange("p (s n) -> p s n", s=2)
                    i = ps[r:r + 32, 4, :].rearrange("p (s n) -> p s n", s=2)
                    if d:
                        o = o[:, :, ::-1]
                    step(dve.tensor_scalar(o, i, bgate[r:r + 32, 0:1], None, ALU.add))
            g64 = slice(0, 64)
            step(dve.scalar_tensor_tensor(out=tm[g64], in0=lf[g64], scalar=-1.0, in1=lf[g64], op0=ALU.mult, op1=ALU.min))
            ins = dve.tensor_scalar(lf[g64], lf[g64], 0.0, None, ALU.min)
            ins.then_inc(lsig_ready, 1)
            dve.wait_ge(lsig_kept, 1)
            step(dve.tensor_tensor(lf[g64], lf[g64], tm[g64], ALU.subtract))
            step(dve.memset(tm[g64], 0.0))
            step(dve.tensor_tensor_scan(mm[g64], lf[g64], ig[g64], 0.0, ALU.add, ALU.max))
            step(dve.tensor_tensor_scan(bb[g64], lf[g64], tm[g64], 0.0, ALU.add, ALU.add))
            for d in range(2):
                r = slice(32 * d, 32 * d + 32)
                rev = (lambda v: v.rearrange("p (s n) -> p s n", s=2)[:, :, ::-1]) if d else (lambda v: v.rearrange("p (s n) -> p s n", s=2))
                nat = lambda v: v.rearrange("p (s n) -> p s n", s=2)
                step(dve.tensor_tensor(rev(tm[r, :]), nat(bb[r]), nat(mm[r]), ALU.subtract))
                step(dve.tensor_tensor(rev(ce[r]), nat(ig[r]), nat(bb[r]), ALU.subtract))
                q = slice(64 + 32 * d, 96 + 32 * d)
                dve.tensor_scalar(rev(ce[q]), nat(mm[r]), -1.0, None, ALU.mult).then_inc(em_ready, 1)
            step(dve.tensor_copy(rrow_r[0:64, :], tm[g64]))
            dve.tensor_tensor(rrow_r[64:128, :], tm[g64], rrow_r[0:64, :], ALU.subtract)
            dve.tensor_tensor(both_rows, ident[:, 0:64], ident[:, 64:128], ALU.add)
            for g in (1, 2):
                split_low(dve, "in0", g, g)
                modulation(0, g, 4 + g)
            step(dve.tensor_copy(silu_c[:, :, :, 8:16], silu_c[:, :, :, 0:8]))
            dve.memset(silu_c[:, :, :, 0:8], 0.0).then_inc(silu_ready, 1)
            split_low(dve, "in0", 3, 3)
            split_low(dve, "in0", 4, 4)
            dve.wait_ge(gturn_done, 1)
            dve.tensor_copy(gcol[:, :, :].rearrange("p t c -> p (t c)"), ps[:, 7, :]).then_inc(gcol_ready, 1)
            dve.wait_ge(gate_done, 1)
            dve.memset(V[:, :, :, DV:DVX], 1.0).then_inc(v_ones, 1)
            split_low(dve, "in0", 5, 5)

            def diag(u):
                h, d = u // 2, u % 2
                dve.wait_ge(r_done, u + 1)
                if u >= 2:
                    dve.wait_ge(o_done, u - 1)
                for s in range(TILES):
                    ins = dve.scalar_tensor_tensor(out=W[:, u % 2, s, s, :], in0=ps[:, 4 - u % 2, P * s:P * s + P],
                                                   scalar=gcol[:, s, 32 * d + h:32 * d + h + 1], in1=masks[:, d, :],
                                                   op0=ALU.add, op1=ALU.add)
                ins.then_inc(d_done, 1)

            def prod(u):
                h, d = u // 2, u % 2
                dve.wait_ge(s_done, h + 1)
                dve.wait_ge(e_done, u + 1)
                for s in range(TILES):
                    for j, c in runs_of(PAIRS[d], s):
                        o = P * j if s < 2 else 256 * (s - 2) + P * (j - 2)
                        w = W[:, u % 2, s, j:j + c, :]
                        ins = dve.tensor_tensor(w, ps[:, min(s, 2), o:o + P * c].rearrange("p (j n) -> p j n", n=P), w,
                                                ALU.mult)
                ins.then_inc(p_done, 1)

            def keep(u):
                h, d = u // 2, u % 2
                dve.wait_ge(o_done, u + 1)
                den = ps[:, 5:7, 0:2 * DVX].rearrange("p b (j c) -> p b j c", j=2)[:, :, :, DV]
                e = gcol[:, :, 64 + 32 * d + h].rearrange("p (b j) -> p b j", b=2)
                r = att[:, d, :].rearrange("p (b j) -> p b j", b=2)
                step(dve.scalar_tensor_tensor(out=r, in0=den, scalar=-1.0, in1=e, op0=ALU.mult, op1=ALU.max))
                step(dve.tensor_tensor(r, den, r, ALU.max))
                dve.reciprocal(att[:, d, :], att[:, d, :]).then_inc(den_ready, 1)
                if d == 1:
                    dve.wait_ge(den_ready, u + 1)
                    dve.wait_ge(fin_act, h + 1)
                    for j in range(TILES):
                        ins = dve.scalar_tensor_tensor(out=H[:, j, h, :], in0=ps[:, 5 + j // 2, DVX * (j % 2):DVX * (j % 2) + DV],
                                                       scalar=att[:, d, j:j + 1], in1=H[:, j, h, :],
                                                       op0=ALU.mult, op1=ALU.add)
                    ins.then_inc(fin_dve, 1)

            def gate_head(h):
                dve.wait_ge(hr_ready, h + 1)
                for t in range(TILES):
                    ins = dve.scalar_tensor_tensor(out=H[:, t, h, :], in0=H[:, t, h, :], scalar=hs[:, h, t:t + 1],
                                                   in1=O[:, t, DV * h:DV * h + DV], op0=ALU.mult, op1=ALU.mult)
                ins.then_inc(y_ready, 1)

            dve.wait_ge(gcol_ready, 1)
            diag(0)
            diag(1)
            prod(0)
            for u in range(16):
                if u + 1 < 16:
                    prod(u + 1)
                keep(u)
                if u + 2 < 16:
                    diag(u + 2)
                if u < ADA_CHUNKS and u % 4 == 3:
                    modulation(1, u // 4, 7)
                if u % 2 == 1 and u >= 7:
                    gate_head(u // 2 - 3)

            for h in range(HEADS - 3, HEADS):
                gate_head(h)

            def heads_low(t):
                dve.wait_ge(yh_ready, t + 1)
                c = slice(P * t, P * t + P)
                dve.tensor_tensor(HL[:, :, c], hT[:, :, c], YH[:, :, c], ALU.subtract).then_inc(yl_ready, 1)

            for g in range(8):
                t, b = g // 2, g % 2
                dve.wait_ge(yt_done, g + 1)
                dve.tensor_tensor(hT[:, 4 * b:4 * b + 4, P * t:P * t + P],
                                  ps[:, 5 + g % 3, :].rearrange("p (k n) -> p k n", k=4),
                                  ghead[:, 4 * b:4 * b + 4].unsqueeze(2).to_broadcast([P, 4, P]), ALU.mult
                                  ).then_inc(yt_kept, 1)
                if b == 1 and t >= 1:
                    heads_low(t - 1)
            heads_low(TILES - 1)

            def route_dve(m):
                nt, t0, l = m.nt, m.tiles[0], m.l

                def add_out(i):
                    for cb in range(2):
                        g, t, c = 2 * i + cb, t0 + i, slice(512 * cb, 512 * cb + 512)
                        dve.wait_ge(out_done, m.outs + g + 1)
                        if g:
                            dve.wait_ge(out_added, m.outs + g)
                        step(dve.tensor_tensor(gtmp2, ps[:, g % 3, :], gate2[:, t // 2, c], ALU.mult))
                        dve.tensor_tensor(X[:, t, c], X[:, t, c], gtmp2, ALU.add).then_inc(out_added, 1)

                def h_of(i):
                    t, s = t0 + i, i // 2
                    dve.wait_ge(rstd_ready, m.norms + i + 1)
                    step(dve.scalar_tensor_tensor(out=XN[:, t, :], in0=X[:, t, :], scalar=stat[:, 2, t:t + 1],
                                                  in1=m.ab[:, 0, s, :], op0=ALU.mult, op1=ALU.mult))
                    dve.tensor_tensor(XN[:, t, :], XN[:, t, :], m.ab[:, 1, s, :], ALU.add).then_inc(m.h_ready, 1)

                dve.wait_ge(g2_ready, (4, 6)[l])
                add_out(0)
                dve.wait_ge(m.gffn_in, m.was["gffn_in"] + 16)
                for b in range(nt):
                    s, c = b // 2, slice(512 * (b % 2), 512 * (b % 2) + 512)
                    dve.wait_ge(m.rows_done, m.was["rows_done"] + 2 * b + 1)
                    dve.scalar_tensor_tensor(out=m.ab[:, 0, s, c], in0=ps[:, 3, :], scalar=1.0, in1=gffn[:, c],
                                             op0=ALU.add, op1=ALU.mult).then_inc(m.scale_kept, 1)
                dve.wait_ge(m.scale_kept, m.was["scale_kept"] + nt)
                dve.wait_ge(m.shift_kept, m.was["shift_kept"] + nt)
                for i in range(nt):
                    h_of(i)
                    if i + 1 < nt:
                        add_out(i + 1)
                    dve.wait_ge(m.turned, m.was["turned"] + 2 * i + 2)
                    dve.tensor_copy(hT[:, 4:8, P * (t0 + i):P * (t0 + i) + P], ps[:, 6, :].rearrange("p (k n) -> p k n", k=4)
                                    ).then_inc(m.turn_kept_dve, 1)

                def row(n, w):
                    return sm[:, n, 0:w * nt].rearrange("p (t e) -> p t e", e=w)

                def bc(v, w):
                    return v.to_broadcast([P, nt, w])

                lg, sel, pick0, pick = row(0, NE), row(1, NE), row(2, NE), row(3, NE)
                tmp, r1, r2 = row(4, NE), row(5, 1), row(6, 1)
                dve.wait_ge(m.logits_raw, m.was["logits_raw"] + 1)
                dve.tensor_copy(lraw[:, 0:P * nt], ps[0:NE, 7, 0:P * nt]).then_inc(m.logits_kept, 1)
                dve.wait_ge(m.logits_done, m.was["logits_done"] + 1)
                L = ps[:, 1, 0:NE * nt].rearrange("p (t e) -> p t e", e=NE)
                step(dve.tensor_reduce(r1[:, :, 0], L, AX_X, ALU.max))
                dve.tensor_tensor(lg, L, bc(r1, NE), ALU.subtract).then_inc(m.shifted, 1)
                dve.wait_ge(m.expd, m.was["expd"] + 1)
                step(dve.tensor_reduce(r1[:, :, 0], lg, AX_X, ALU.add))
                step(dve.reciprocal(r2, r1))
                step(dve.tensor_tensor(lg, lg, bc(r2, NE), ALU.mult))
                step(dve.tensor_tensor(sel, lg, brt[:, :].unsqueeze(1).to_broadcast([P, nt, NE]), ALU.add))
                q = sm[:, 1, 0:NE * nt].rearrange("p (g a b) -> p g a b", a=2, b=2)
                hi = sm[:, 7, 0:8 * nt].rearrange("p (g a) -> p g a", a=2)
                lo = sm[:, 8, 0:8 * nt].rearrange("p (g a) -> p g a", a=2)
                t1, t2, t3 = (sm[:, x, 0:4 * nt] for x in (9, 10, 11))
                step(dve.tensor_tensor(hi, q[:, :, :, 0], q[:, :, :, 1], ALU.max))
                step(dve.tensor_tensor(lo, q[:, :, :, 0], q[:, :, :, 1], ALU.min))
                step(dve.tensor_tensor(t1, hi[:, :, 0], hi[:, :, 1], ALU.max))
                step(dve.tensor_tensor(t2, hi[:, :, 0], hi[:, :, 1], ALU.min))
                step(dve.tensor_tensor(t3, lo[:, :, 0], lo[:, :, 1], ALU.max))
                step(dve.tensor_tensor(t2, t2, t3, ALU.max))
                step(dve.tensor_tensor(t1, t1, t2, ALU.add))
                gs, eq, first = row(9, 4), row(10, 4), row(11, 4)
                step(dve.tensor_reduce(r1[:, :, 0], gs, AX_X, ALU.max))
                step(dve.tensor_tensor(eq, gs, bc(r1, 4), ALU.is_equal))
                step(dve.tensor_scalar(first[:, 0, :], iota16[:, 0:4], -1.0, 4.0, ALU.mult, ALU.add))
                step(dve.tensor_tensor(eq, eq, first[:, 0:1, :].to_broadcast([P, nt, 4]), ALU.mult))
                step(dve.tensor_reduce(r1[:, :, 0], eq, AX_X, ALU.max))
                step(dve.tensor_tensor(eq, eq, bc(r1, 4), ALU.is_equal))
                eq4 = sm[:, 10, 0:4 * nt].unsqueeze(2).to_broadcast([P, 4 * nt, 4])
                grp = lambda v: v.rearrange("p t (g f) -> p (t g) f", f=4)
                step(dve.tensor_tensor(grp(sel), grp(sel), eq4, ALU.mult))
                step(dve.tensor_scalar(eq, eq, -NEG, NEG, ALU.mult, ALU.add))
                step(dve.tensor_tensor(grp(sel), grp(sel), eq4, ALU.add))
                m8 = row(12, 8)
                i8 = sm[:, 13, 0:8 * nt].bitcast(U32).rearrange("p (t e) -> p t e", e=8)
                for i in range(nt):
                    step(dve.max(m8[:, i, :], sel[:, i, :]))
                    step(dve.max_index(i8[:, i, :], m8[:, i, :], sel[:, i, :]))
                ex = sm[:, 14, 0:2 * nt].rearrange("p (k t) -> p k t", k=2)
                step(dve.tensor_copy(ex.rearrange("p k t -> p t k"), i8[:, :, 0:2]))
                picks = [pick0, row(15, NE)]
                wt = m.weight.rearrange("p (k t) -> p k t", k=2)
                for k in range(2):
                    step(dve.tensor_tensor(picks[k], iota16[:, :].unsqueeze(1).to_broadcast([P, nt, NE]),
                                           ex[:, k, :].unsqueeze(2).to_broadcast([P, nt, NE]), ALU.is_equal))
                dve.tensor_tensor(pick, picks[0], picks[1], ALU.add).then_inc(m.picked, 1)
                for k in range(2):
                    step(dve.tensor_tensor(tmp, lg, picks[k], ALU.mult))
                    step(dve.tensor_reduce(wt[:, k, :], tmp, AX_X, ALU.add))
                step(dve.tensor_tensor(r1[:, :, 0], wt[:, 0, :], wt[:, 1, :], ALU.add))
                step(dve.reciprocal(r2, r1))
                step(dve.tensor_tensor(wt, wt, r2[:, :, 0].unsqueeze(1).to_broadcast([P, 2, nt]), ALU.mult))
                vt = m.value.rearrange("p (k t) -> p k t", k=2)
                step(dve.tensor_copy(vt[:, 0, :], tokf[:, 0:nt]))
                step(dve.tensor_scalar(vt[:, 1, :], tokf[:, 0:nt], float(m.T), None, ALU.add))
                val, far = row(19, NE), row(20, NE)
                step(dve.tensor_scalar(val, picks[1], float(m.T), 1.0, ALU.mult, ALU.add))
                dve.tensor_tensor(VAL_R[:, 0:NE * nt].rearrange("p (t e) -> p t e", e=NE), val,
                                  tokf[:, 0:nt].unsqueeze(2).to_broadcast([P, nt, NE]), ALU.add)
                step(dve.tensor_scalar(far, pick, -PAD, PAD, ALU.mult, ALU.add))
                dve.wait_ge(m.slots_listed, m.was["slots_listed"] + 1)
                step(dve.tensor_copy(slot_f, slot_i))
                dve.wait_ge(m.pos_done, m.was["pos_done"] + 1)
                pos, place = row(16, NE), row(18, NE)
                dve.tensor_copy(sm[:, 16, 0:NE * nt], ps[:, 0, 0:NE * nt])
                step(dve.tensor_tensor(place, ps[:, 0, 0:NE * nt].rearrange("p (t e) -> p t e", e=NE), far, ALU.add))
                for e in range(NE):
                    if e >= len(m.hot):
                        dve.wait_ge(m.hot_used, m.was["hot_used"] + e - len(m.hot) + 1)
                    dve.tensor_tensor(m.hot[e % len(m.hot)], place[:, :, e:e + 1].to_broadcast([P, nt, P]),
                                      slot_f.unsqueeze(1).to_broadcast([P, nt, P]), ALU.is_equal).then_inc(m.hot_ready, 1)
                dve.wait_ge(m.hot_used, m.was["hot_used"] + NE)
                G = m.G
                v, ge = sm[:, 19, 0:G], sm[:, 20, 0:G]
                listed = ps[:, 1, 0:2 * G].rearrange("p (g two) -> p g two", two=2)[:, :, 0]
                step(dve.tensor_scalar(ge, listed, 0.0, PAD, ALU.is_equal, ALU.mult))
                step(dve.scalar_tensor_tensor(out=v, in0=listed, scalar=-1.0, in1=ge, op0=ALU.add, op1=ALU.add))
                (rows_of if m.l == 0 else half_rows)(v, ge, G, GIX[:, 0:G], SIX[:, 0:G], m.T, m.lists_ready)
                step(dve.tensor_copy(sm[0:1, 17, 0:NE], ps[0:1, 2, 0:NE]))

            def table_places(m):
                nt = m.nt
                row = lambda n, w: sm[:, n, 0:w * nt].rearrange("p (t w) -> p t w", w=w)
                pos, tmp = row(16, NE), row(4, NE)
                ex = sm[:, 14, 0:2 * nt].rearrange("p (k t) -> p k t", k=2)
                picks = [row(2, NE), row(15, NE)]
                pl = sm[:, 18, 0:2 * nt].rearrange("p (k t) -> p k t", k=2)
                for k in range(2):
                    step(dve.tensor_tensor(tmp, pos, picks[k], ALU.mult))
                    step(dve.tensor_reduce(pl[:, k, :], tmp, AX_X, ALU.add))
                dve.scalar_tensor_tensor(out=m.addr.rearrange("p (k t) -> p k t", k=2), in0=ex, scalar=float(CAP), in1=pl,
                                         op0=ALU.mult, op1=ALU.add).then_inc(m.addr_ready, 1)

            def rows_of(v, ge, G, gix, six, T, ready):
                step(dve.tensor_scalar(ge, v, float(T), float(T), ALU.is_ge, ALU.mult))
                step(dve.tensor_tensor(ge, v, ge, ALU.subtract))
                step(dve.tensor_scalar(gix, ge, float(T - 1), None, ALU.min))
                dve.tensor_copy(six, v).then_inc(ready, 1)

            def half_rows(v, ge, G, gix, six, T, ready):
                step(dve.tensor_scalar(ge, v, float(T), float(T), ALU.is_ge, ALU.mult))
                step(dve.tensor_tensor(ge, v, ge, ALU.subtract))
                step(dve.tensor_scalar(ge, ge, float(T - 1), 2.0, ALU.min, ALU.mult))
                step(dve.tensor_scalar(gix, ge, half[:, 0:1], None, ALU.add))
                dve.tensor_scalar(six, v, 2.0, half[:, 0:1], ALU.mult, ALU.add).then_inc(ready, 1)

            def list_further(m):
                F, M = m.further, m.most
                place, total = iota16[0:1, 0:M], sm[0:1, 17, 0:NE]
                flat = lambda n, w: sm[0:1, n:n + 4, :].rearrange("p a n -> p (a n)")[:, 0:w]
                bounds, x, upto_e = sm[0:1, 4, 0:F], sm[0:1, 5, 0:NE], sm[0:1, 6, 0:NE]
                expert, row, before = sm[0:1, 7, 0:M], sm[0:1, 8, 0:M], sm[0:1, 9, 0:M]
                over = flat(10, NE * F).rearrange("p (e k) -> p e k", k=F)
                past = flat(21, M * NE).rearrange("p (o e) -> p o e", e=NE)
                step(dve.tensor_scalar(bounds, iota16[0:1, 0:F], float(PASS), float(m.slots), ALU.mult, ALU.add))
                step(dve.tensor_tensor(over, total.unsqueeze(2).to_broadcast([1, NE, F]),
                                       bounds.unsqueeze(1).to_broadcast([1, NE, F]), ALU.is_gt))
                step(dve.tensor_reduce(x, over, AX_X, ALU.add))
                step(dve.tensor_tensor_scan(upto_e, ones[0:1, 0:NE], x, 0.0, ALU.mult, ALU.add))
                step(dve.tensor_tensor(past, upto_e.unsqueeze(1).to_broadcast([1, M, NE]),
                                       place.unsqueeze(2).to_broadcast([1, M, NE]), ALU.is_le))
                step(dve.tensor_reduce(expert, past, AX_X, ALU.add))
                step(dve.tensor_tensor(past, past, x.unsqueeze(1).to_broadcast([1, M, NE]), ALU.mult))
                step(dve.tensor_reduce(before, past, AX_X, ALU.add))
                step(dve.tensor_scalar(expert, expert, float(NE - 1), None, ALU.min))
                step(dve.scalar_tensor_tensor(out=row, in0=expert, scalar=float(CAP // PASS), in1=place,
                                              op0=ALU.mult, op1=ALU.add))
                step(dve.tensor_tensor(row, row, before, ALU.subtract))
                step(dve.tensor_scalar(row, row, float(m.slots // PASS), float(NE * CAP // PASS - 1), ALU.add, ALU.min))
                step(dve.tensor_copy(more[0:1, 0:1], upto_e[:, NE - 1:NE]))
                step(dve.tensor_copy(more[0:1, 1:1 + M], expert))
                dve.tensor_copy(more[0:1, 16:16 + M], row).then_inc(m.more_ready, 1)

            def passes_wide_dve(m):
                def low(i, b, part):
                    dve.wait_ge(hi_ready, 6 * i + 3 * b + part + 1)
                    n = m.base + 3 * b + part
                    dve.tensor_tensor(slot_r(n), slot(n), HI_R[part], ALU.subtract).then_inc(lo_ready, 1)

                def tokens_low(i, b, piece):
                    dve.wait_ge(xh_ready, 4 * i + 2 * b + piece + 1)
                    flat = lambda v: v[:, 4 * piece:4 * piece + 4, :].rearrange("p k n -> p (k n)")
                    dve.tensor_tensor(flat(XL_R), ps[:, piece, :], flat(XH_R), ALU.subtract).then_inc(m.xt_ready, 1)

                def body(i, last):
                    for b in range(2):
                        g = 2 * i + b
                        ni, nb = (i, 1) if b == 0 else (i + 1, 0)
                        more_come = not (last and b == 1)
                        dve.wait_ge(m.silu_done, g + 1)
                        dve.wait_ge(m.h_done, g + 1)
                        dve.tensor_tensor(U_W, ps[:, 3, :], SG_W, ALU.mult).then_inc(m.u_ready, 1)
                        if more_come:
                            tokens_low(ni, nb, 0)
                        for c in (0, 2):
                            dve.wait_ge(uh_ready, 2 * g + c // 2 + 1)
                            flat = lambda v: v[:, c:c + 2, :].rearrange("p c n -> p (c n)")
                            dve.tensor_tensor(flat(UL_R), ps[:, 4 + c // 2, 0:2 * P], flat(UH_R), ALU.subtract
                                              ).then_inc(m.ut_ready, 1)
                        if more_come:
                            tokens_low(ni, nb, 1)
                            low(ni, nb, 0)
                            low(ni, nb, 1)
                            low(ni, nb, 2)

                low(0, 0, 0)
                for piece in range(2):
                    tokens_low(0, 0, piece)
                low(0, 0, 1)
                low(0, 0, 2)
                table_places(m)
                list_further(m)
                body(0, False)
                with dve.Fori(1, NE // 2 - 1) as i:
                    body(i, False)
                body(NE // 2 - 1, True)

            def passes_dve(m):
                def keep_xt(g, par):
                    dve.wait_ge(m.tx_done, m.was["tx_done"] + g + 1)
                    if not isinstance(g, int) or g >= 2:
                        dve.wait_ge(m.h_done, m.was["h_done"] + g - 1)
                    dve.tensor_copy(XT[:, par, :, :].rearrange("p j n -> p (j n)"), ps[:, par, :]).then_inc(m.xt_ready, 1)

                def mul(g, par):
                    dve.wait_ge(m.silu_done, m.was["silu_done"] + g + 1)
                    if not isinstance(g, int) or g >= 2:
                        dve.wait_ge(m.tu_done, m.was["tu_done"] + g - 1)
                    dve.tensor_tensor(U[:, par, :], ps[:, 2 + par, 256:512], SG[:, par, :], ALU.mult).then_inc(m.u_ready, 1)

                def keep_ut(g, par):
                    dve.wait_ge(m.tu_done, m.was["tu_done"] + g + 1)
                    if not isinstance(g, int) or g >= 2:
                        dve.wait_ge(m.y_done, m.was["y_done"] + g - 1)
                    dve.tensor_copy(UT[:, par, :, :].rearrange("p c n -> p (c n)"), ps[:, 4 + par, 0:256]).then_inc(m.ut_ready, 1)

                def body(i, last):
                    for b in range(2):
                        g = 2 * i + b
                        mul(g, b)
                        if not (last and b == 1):
                            keep_xt(g + 1, 1 - b)
                        keep_ut(g, b)

                keep_xt(0, 0)
                body(0, False)
                with dve.Fori(1, NE // 2 - 1) as i:
                    body(i, False)
                body(NE // 2 - 1, True)

            def further_dve(m):
                dve.wait_ge(m.more_ready, m.was["more_ready"] + 1)
                count = dve.value_load(more[0:1, 0:1], min_val=0, max_val=m.most)
                with dve.If(count > 0):
                    with dve.Fori(0, m.most) as o:
                        with dve.If(count > o):
                            dve.wait_ge(m.further_pe, after(PE_STEPS, o, "column"))
                            v, ge = ov[:, 0:1], ov[:, 1:2]
                            dve.tensor_copy(v, ps[:, 1, 0:1]).then_inc(m.further_dve, 1)
                            dve.wait_ge(m.further_dve, after(DVE_STEPS, o, "v"))
                            dve.tensor_scalar(ge, v, float(m.T), float(m.T), ALU.is_ge, ALU.mult).then_inc(m.further_dve, 1)
                            dve.wait_ge(m.further_dve, after(DVE_STEPS, o, "second"))
                            dve.tensor_tensor(ge, v, ge, ALU.subtract).then_inc(m.further_dve, 1)
                            dve.wait_ge(m.further_dve, after(DVE_STEPS, o, "token"))
                            dve.tensor_scalar(ge, ge, float(m.T - 1), 2.0, ALU.min, ALU.mult).then_inc(m.further_dve, 1)
                            dve.wait_ge(m.further_dve, after(DVE_STEPS, o, "row"))
                            dve.tensor_scalar(ogi, ge, half[:, 0:1], None, ALU.add).then_inc(m.further_dve, 1)
                            dve.tensor_scalar(osi, v, 2.0, half[:, 0:1], ALU.mult, ALU.add).then_inc(m.further_dve, 1)
                            dve.wait_ge(m.further_pe, after(PE_STEPS, o, "turned"))
                            dve.tensor_copy(XT[:, 0, :, :].rearrange("p j n -> p (j n)"), ps[:, 0, :]).then_inc(m.further_dve, 1)
                            dve.wait_ge(m.further_act, after(ACT_STEPS, o, "silu"))
                            dve.tensor_tensor(U[:, 0, :], ps[:, 2, 256:512], SG[:, 0, :], ALU.mult).then_inc(m.further_dve, 1)
                            dve.wait_ge(m.further_pe, after(PE_STEPS, o, "u_turned"))
                            dve.tensor_copy(UT[:, 0, :, :].rearrange("p c n -> p (c n)"), ps[:, 4, 0:256]).then_inc(m.further_dve, 1)

            def combine_dve(m):
                dve.wait_ge(m.g5_kept, m.was["g5_kept"] + m.nt)
                for i, t in enumerate(m.tiles):
                    y0, y1 = m.yin[i]
                    dve.wait_ge(m.y_scaled, m.was["y_scaled"] + i + 1)
                    step(dve.scalar_tensor_tensor(out=y1, in0=y1, scalar=m.weight[:, m.nt + i:m.nt + i + 1], in1=y0,
                                                  op0=ALU.mult, op1=ALU.add))
                    step(dve.tensor_tensor(y1, y1, g5[:, t // 2, :], ALU.mult))
                    dve.tensor_tensor(X[:, t, :], X[:, t, :], y1, ALU.add).then_inc(m.added, 1)

            def conv(n):
                dve.wait_ge(xr_kept, n + 1)
                x = xpad[:, n % 2]
                y = XC[:, n, :].rearrange("p (s n) -> p s n", s=2)
                step(dve.tensor_scalar(y, x[:, :, 0:256], convw[:, 0, n:n + 1], convb[:, n:n + 1], ALU.mult, ALU.add))
                for j in range(1, 4):
                    ins = dve.scalar_tensor_tensor(out=y, in0=x[:, :, j:j + 256], scalar=convw[:, j, n:n + 1], in1=y,
                                                   op0=ALU.mult, op1=ALU.add)
                    if j < 3:
                        step(ins)
                ins.then_inc(conv_done, 1)

            def scans(n):
                for d in range(2):
                    dve.wait_ge(rg_tanh, 2 * n + d + 1)
                    dve.scalar_tensor_tensor(out=RB[:, d, 2, :], in0=RB[:, d, 0, :], scalar=1.0, in1=RB[:, d, 2, :],
                                             op0=ALU.add, op1=ALU.mult).then_inc(rg_q, 1)
                for d in range(2):
                    ti, sq_, dec = RB[:, d, 1, :], RB[:, d, 2, :], RB[:, d, 3, :]
                    step(dve.scalar_tensor_tensor(out=ti, in0=ti, scalar=1.0, in1=XC[:, n, :], op0=ALU.add, op1=ALU.mult))
                    dve.wait_ge(rg_sqrt, 2 * n + d + 1)
                    step(dve.tensor_tensor(ti, ti, sq_, ALU.mult))
                    h = hfb[:, d, :]
                    dve.wait_ge(rg_q, 2 * n + 2)
                    if d == 0:
                        dve.tensor_tensor_scan(h, dec, ti, 0.0, ALU.mult, ALU.add).then_inc(rg_scan, 1)
                    else:
                        step(dve.tensor_tensor_scan(h[:, 0:256][:, ::-1], dec[:, 0:256][:, ::-1], ti[:, 0:256][:, ::-1],
                                                    0.0, ALU.mult, ALU.add))
                        dve.tensor_tensor_scan(h[:, 256:512][:, ::-1], dec[:, 256:512][:, ::-1], ti[:, 256:512][:, ::-1],
                                               h[:, 0:1], ALU.mult, ALU.add).then_inc(rg_scan, 1)
                dve.wait_ge(rg_scan, 2 * n + 2)
                step(dve.tensor_tensor(YT[:, n, :], hfb[:, 0, 256:512], hfb[:, 1, 256:512], ALU.add))
                dve.wait_ge(yb_kept, n + 1)
                dve.tensor_tensor(YT[:, n, :], YT[:, n, :], YB[:, n, :], ALU.mult).then_inc(y_ready, 1)

            def rglru_params():
                dve.wait_ge(rg_in, 80)
                lm = lam[:, :, :].rearrange("p d k -> p (d k)")
                e, u, ln, z = (lt[:, i, :] for i in range(4))
                dve.scalar_tensor_tensor(out=e, in0=lm, scalar=-1.0, in1=lm, op0=ALU.mult, op1=ALU.min).then_inc(lam_u, 1)
                dve.wait_ge(lam_exp, 1)
                dve.tensor_scalar(u, e, 1.0, None, ALU.add).then_inc(lam_u, 1)
                dve.wait_ge(lam_ln, 1)
                step(dve.tensor_scalar(u, u, 1.0, None, ALU.subtract))
                step(dve.tensor_scalar(z, u, 0.0, None, ALU.is_equal))
                step(dve.tensor_tensor(ln, ln, z, ALU.add))
                step(dve.tensor_tensor(u, u, z, ALU.add))
                step(dve.reciprocal(u, u))
                step(dve.tensor_tensor(ln, ln, u, ALU.mult))
                step(dve.tensor_tensor(ln, ln, e, ALU.mult))
                step(dve.tensor_scalar(z, lm, -1.0, 0.0, ALU.mult, ALU.max))
                step(dve.tensor_tensor(ln, ln, z, ALU.add))
                step(dve.tensor_scalar(spl[:, :, :].rearrange("p d k -> p (d k)"), ln, 0.5 * RGLRU_C, None, ALU.mult))
                step(dve.tensor_scalar(spn[:, :, :].rearrange("p d k -> p (d k)"), ln, -0.5 * RGLRU_C, None, ALU.mult))
                rb = rbias[:, :, :, :].rearrange("p d n e -> p (d n e)")
                dve.tensor_scalar(rb, rb, 0.5, None, ALU.mult).then_inc(lam_ready, 1)

            route_dve(moes[0])
            passes_wide_dve(moes[0])
            further_dve(moes[0])
            rglru_params()
            columns(1)
            combine_dve(moes[0])
            norm_keep(1)
            dve.memset(xpad[:, :, :, :], 0.0).then_inc(pads, 1)
            for what, n in RG_ORDER:
                if what == "x":
                    conv(n)
                elif what == "g":
                    scans(n)
            route_dve(moes[1])
            table_places(moes[1])
            list_further(moes[1])
            passes_dve(moes[1])
            further_dve(moes[1])
            combine_dve(moes[1])
            dve.wait_ge(gfin_in, 16)
            for i, t in enumerate(moes[1].tiles):
                dve.wait_ge(rstd_ready, 14 + i + 1)
                dve.scalar_tensor_tensor(out=moes[1].yin[i][1], in0=X[:, t, :], scalar=stat[:, 2, t:t + 1], in1=gffn,
                                         op0=ALU.mult, op1=ALU.mult).then_inc(fin_ready, 1)


def position_table(n_tokens, dim, grid_w=64, base=10000.0):
    rows = n_tokens // grid_w
    r, col = np.meshgrid(np.arange(rows, dtype=np.float32), np.arange(grid_w, dtype=np.float32), indexing="ij")
    quarter = dim // 4
    freqs = np.exp(np.float32(-np.log(base)) * np.arange(quarter, dtype=np.float32) / np.float32(quarter))
    enc = lambda p: np.concatenate([np.sin(p.reshape(-1, 1) * freqs), np.cos(p.reshape(-1, 1) * freqs)], -1)
    return np.concatenate([enc(r), enc(col)], -1).astype(np.float32)


INPUTS = ["x", "c", "ctx", "c_ctx", "w_ada", "b_ada", "g_mix", "g_ffn", "g_final", "m_w_in", "m_b_gate", "m_g_head",
          "m_w_out", "r_w_in", "r_conv_w", "r_conv_b", "r_w_gate", "r_b_gate", "r_lam", "r_w_out", "w_router",
          "b_router", "e_w1", "e_w3", "e_w2"]


def kernel(**inputs):
    import concourse.bacc as bacc
    from concourse.bass_utils import run_bass_kernel_spmd

    nc = bacc.Bacc("TRN2", target_bir_lowering=False, num_devices=1)
    arrays = {name: np.ascontiguousarray(inputs[name]) for name in INPUTS}
    arrays["pos"] = position_table(SEQ, D)
    args = {name: nc.dram_tensor("in_" + name, v.shape, F32, kind="ExternalInput").ap() for name, v in arrays.items()}
    out = nc.dram_tensor("out", (1, SEQ, D), F32, kind="ExternalOutput")
    build(nc, args, out.ap())
    r = run_bass_kernel_spmd(nc, [{"in_" + name: v for name, v in arrays.items()}], core_ids=[0])
    return r.results[0]["out"]
```
